# Optimizing a Trainium2 kernel written in Bass

```python
import math
import jax, jax.numpy as jnp
from jax import lax
import numpy as np

D_MODEL = 1024
BATCH = 1
SEQ = 1024
DEPTH = 1
DEC_BATCH = 8
DEC_SEQ = 8
PAST_LEN = 4096
PAGE_SIZE = 128

N_MEM = 256
H_R = 4
DK_R = 64
DV_R = 128
RET_CHUNK = 128
ROPE_BASE = 10000.0
H_F = 8
D_F = 64
Q_BLOCK = 128
FORGET_BIAS_INIT = 2.0
H_M = 4
D_M = 128
D_FF = 2816
N_BRANCH = 3
LN_EPS = 1e-5
GN_EPS = 1e-5
ALPHA = (2.0 * DEPTH) ** 0.25
BETA = (8.0 * DEPTH) ** -0.25

RQ = H_R * DK_R
RV = H_R * DV_R
FQ = H_F * D_F
MQ = H_M * D_M
SPLIT_SIZES = (RQ, RQ, RV, RV, FQ, FQ, FQ, H_F, MQ, N_BRANCH * D_MODEL)
SPLIT_SCALE = (1.0, 1.0, BETA, 1.0, 1.0, 1.0, BETA, 1.0, 1.0, 1.0)
SPLIT_IDX = tuple(int(i) for i in np.cumsum(SPLIT_SIZES)[:-1])

kernel_name = 'hybrid_retention_fox_memory_macaron_step'

F32 = jnp.float32

def layer_norm(x, g, b):
    xf = x.astype(F32)
    mu = jnp.mean(xf, axis=-1, keepdims=True)
    var = jnp.mean(jnp.square(xf - mu), axis=-1, keepdims=True)
    y = (xf - mu) * lax.rsqrt(var + LN_EPS) * g.astype(F32) + b.astype(F32)
    return y.astype(x.dtype)

def swiglu(x, wg, wu, wd):
    return (jax.nn.silu(x @ wg) * (x @ wu)) @ wd

def rotary(x, pos):
    half = x.shape[-1] // 2
    inv = ROPE_BASE ** (-jnp.arange(half, dtype=F32) / half)
    ang = pos[:, None] * inv[None, :]
    cos = jnp.cos(ang)[None, :, None, :]
    sin = jnp.sin(ang)[None, :, None, :]
    x1 = x[..., :half].astype(F32)
    x2 = x[..., half:].astype(F32)
    return jnp.concatenate([x1 * cos - x2 * sin, x2 * cos + x1 * sin], axis=-1)

def retention(q, k, v, s0):
    B, L, H, dk = q.shape
    dv = v.shape[-1]
    C = math.gcd(L, RET_CHUNK)
    n = L // C
    log_g = jnp.log1p(-jnp.exp2(-5.0 - jnp.arange(H, dtype=F32)))
    i = jnp.arange(C, dtype=F32)
    diff = i[:, None] - i[None, :]
    dmask = jnp.where(diff[None] >= 0, jnp.exp(jnp.maximum(diff, 0.0)[None] * log_g[:, None, None]), 0.0)
    q_dec = jnp.exp((i + 1.0)[:, None] * log_g[None, :])
    k_dec = jnp.exp((C - 1.0 - i)[:, None] * log_g[None, :])
    chunk_dec = jnp.exp(C * log_g)

    def to_chunks(a, d):
        return a.astype(F32).reshape(B, n, C, H, d).transpose(1, 0, 2, 3, 4)

    qc, kc, vc = to_chunks(q, dk), to_chunks(k, dk), to_chunks(v, dv)

    def step(S, inp):
        qb, kb, vb = inp
        a = jnp.einsum('bihd,bjhd->bhij', qb, kb) * dmask[None]
        o = (jnp.einsum('bhij,bjhe->bihe', a, vb)
             + jnp.einsum('bihd,bhde->bihe', qb * q_dec[None, :, :, None], S))
        S = S * chunk_dec[None, :, None, None] + jnp.einsum('bjhd,bjhe->bhde', kb * k_dec[None, :, :, None], vb)
        return S, o

    S, o = lax.scan(step, s0.astype(F32), (qc, kc, vc))
    o = o.transpose(1, 0, 2, 3, 4).reshape(B, L, H, dv)
    return o, S

def head_norm(o, g):
    mu = jnp.mean(o, axis=-1, keepdims=True)
    var = jnp.mean(jnp.square(o - mu), axis=-1, keepdims=True)
    y = (o - mu) * lax.rsqrt(var + GN_EPS)
    B, L, H, dv = o.shape
    return y.reshape(B, L, H * dv) * g.astype(F32)

def fox_attention(q, cq, q_offset, k, v, ck):
    B, Lq, H, D = q.shape
    Lk = k.shape[1]
    QB = math.gcd(Lq, Q_BLOCK)
    nb = Lq // QB
    kpos = jnp.arange(Lk)
    ckT = ck.astype(F32).transpose(0, 2, 1)[:, :, None, :]
    qb = q.reshape(B, nb, QB, H, D).transpose(1, 0, 2, 3, 4)
    cqb = cq.reshape(B, nb, QB, H).transpose(1, 0, 2, 3)
    starts = q_offset + jnp.arange(nb) * QB
    scale = D ** -0.5

    def block(args):
        qi, ci, st = args
        s = jnp.einsum('bqhd,bkhd->bhqk', qi, k, preferred_element_type=F32) * scale
        s = s + ci.astype(F32).transpose(0, 2, 1)[..., None] - ckT
        qpos = st + jnp.arange(QB)
        s = jnp.where(kpos[None, :] <= qpos[:, None], s, -jnp.inf)
        p = jax.nn.softmax(s, axis=-1)
        return jnp.einsum('bhqk,bkhd->bqhd', p.astype(v.dtype), v)

    o = lax.map(block, (qb, cqb, starts))
    return o.transpose(1, 0, 2, 3, 4).reshape(B, Lq, H, D)

def decoder_layer(x, pos, ret_s0, past_k, past_v, past_logf, mem_k, mem_v,
                  ln_g, ln_b, w_ffn_gate, w_ffn_up, w_ffn_down, w_in, b_forget, b_gate,
                  ret_gn_g, w_ret_o, w_fox_o, w_mem_o, w_out):
    B, L, _ = x.shape
    h = layer_norm(ALPHA * x + 0.5 * swiglu(x, w_ffn_gate[0], w_ffn_up[0], w_ffn_down[0]), ln_g[0], ln_b[0])
    proj = h @ w_in
    rq, rk, rv, rg, fq, fk, fv, fl, mq, gl = jnp.split(proj, SPLIT_IDX, axis=-1)

    rq = rotary(rq.reshape(B, L, H_R, DK_R), pos)
    rk = rotary(rk.reshape(B, L, H_R, DK_R), pos) * (DK_R ** -0.5)
    ro, ret_state = retention(rq, rk, rv.reshape(B, L, H_R, DV_R), ret_s0)
    ret_out = (jax.nn.silu(rg) * head_norm(ro, ret_gn_g).astype(rg.dtype)) @ w_ret_o

    fq = fq.reshape(B, L, H_F, D_F)
    fk = fk.reshape(B, L, H_F, D_F)
    fv = fv.reshape(B, L, H_F, D_F)
    logf = jax.nn.log_sigmoid(fl.astype(F32) + b_forget.astype(F32))
    if past_k is None:
        k_all, v_all, lf_all, offset = fk, fv, logf, 0
    else:
        k_all = jnp.concatenate([past_k, fk], axis=1)
        v_all = jnp.concatenate([past_v, fv], axis=1)
        lf_all = jnp.concatenate([past_logf.astype(F32), logf], axis=1)
        offset = past_k.shape[1]
    c_all = lax.cumsum(lf_all, axis=1)
    fo = fox_attention(fq, c_all[:, offset:], offset, k_all, v_all, c_all)
    fox_out = fo.reshape(B, L, FQ).astype(h.dtype) @ w_fox_o

    mqh = mq.reshape(B, L, H_M, D_M)
    s = jnp.einsum('blhd,bmhd->bhlm', mqh, mem_k, preferred_element_type=F32) * (D_M ** -0.5)
    p = jax.nn.softmax(s, axis=-1)
    mo = jnp.einsum('bhlm,bmhd->blhd', p.astype(mem_v.dtype), mem_v)
    mem_out = mo.reshape(B, L, MQ).astype(h.dtype) @ w_mem_o

    g = jax.nn.sigmoid(gl.reshape(B, L, N_BRANCH, D_MODEL) + b_gate)
    mix = (g[:, :, 0] * ret_out + g[:, :, 1] * fox_out + g[:, :, 2] * mem_out) @ w_out
    h = layer_norm(ALPHA * h + mix, ln_g[1], ln_b[1])

    y = layer_norm(ALPHA * h + 0.5 * swiglu(h, w_ffn_gate[1], w_ffn_up[1], w_ffn_down[1]), ln_g[2], ln_b[2])
    return y, fk, fv, logf, ret_state

def setup_inputs(seed: int = 0) -> dict:
    key = jax.random.key(seed)
    ks = jax.random.split(key, 26)

    def nrm(k, shape, scale):
        return jax.random.normal(k, shape, F32) * scale

    n_pages = PAST_LEN // PAGE_SIZE
    n_used = DEC_BATCH * n_pages
    n_pool = n_used + max(1, n_used // 4)
    s_in = D_MODEL ** -0.5

    x_prompt = nrm(ks[0], (BATCH, SEQ, D_MODEL), 1.0)
    x_sample = nrm(ks[1], (DEC_BATCH, DEC_SEQ, D_MODEL), 1.0)
    mem_prompt = nrm(ks[2], (BATCH, N_MEM, D_MODEL), 1.0)
    cache_fox_k = nrm(ks[3], (n_pool, PAGE_SIZE, H_F, D_F), 1.0)
    cache_fox_v = nrm(ks[4], (n_pool, PAGE_SIZE, H_F, D_F), 1.0)
    cache_fox_logf = jax.nn.log_sigmoid(FORGET_BIAS_INIT + nrm(ks[5], (n_pool, PAGE_SIZE, H_F), 1.0))
    state_ret = nrm(ks[6], (DEC_BATCH, H_R, DK_R, DV_R), 1.0)
    cache_mem_k = nrm(ks[7], (DEC_BATCH, N_MEM, H_M, D_M), 1.0)
    cache_mem_v = nrm(ks[8], (DEC_BATCH, N_MEM, H_M, D_M), 1.0)
    page_table = jax.random.permutation(ks[9], n_pool)[:n_used].reshape(DEC_BATCH, n_pages).astype(jnp.int32)

    ln_g = 1.0 + nrm(ks[10], (3, D_MODEL), 0.01)
    ln_b = nrm(ks[11], (3, D_MODEL), 0.01)
    w_ffn_gate = nrm(ks[12], (2, D_MODEL, D_FF), s_in)
    w_ffn_up = nrm(ks[13], (2, D_MODEL, D_FF), s_in)
    w_ffn_down = nrm(ks[14], (2, D_FF, D_MODEL), (D_FF ** -0.5) * BETA)
    col_keys = jax.random.split(ks[15], len(SPLIT_SIZES))
    w_in = jnp.concatenate([nrm(kk, (D_MODEL, n), s_in * sc)
                            for kk, n, sc in zip(col_keys, SPLIT_SIZES, SPLIT_SCALE)], axis=1)
    b_forget = FORGET_BIAS_INIT + nrm(ks[16], (H_F,), 0.1)
    b_gate = nrm(ks[17], (N_BRANCH, D_MODEL), 0.01)
    ret_gn_g = 1.0 + nrm(ks[18], (RV,), 0.01)
    w_ret_o = nrm(ks[19], (RV, D_MODEL), (RV ** -0.5) * BETA)
    w_fox_o = nrm(ks[20], (FQ, D_MODEL), (FQ ** -0.5) * BETA)
    w_mem_k = nrm(ks[21], (D_MODEL, MQ), s_in)
    w_mem_v = nrm(ks[22], (D_MODEL, MQ), s_in * BETA)
    w_mem_o = nrm(ks[23], (MQ, D_MODEL), (MQ ** -0.5) * BETA)
    w_out = nrm(ks[24], (D_MODEL, D_MODEL), s_in * BETA)
    return {'x_prompt': x_prompt, 'x_sample': x_sample, 'mem_prompt': mem_prompt,
            'cache_fox_k': cache_fox_k, 'cache_fox_v': cache_fox_v, 'cache_fox_logf': cache_fox_logf,
            'state_ret': state_ret, 'cache_mem_k': cache_mem_k, 'cache_mem_v': cache_mem_v,
            'page_table': page_table,
            'ln_g': ln_g, 'ln_b': ln_b, 'w_ffn_gate': w_ffn_gate, 'w_ffn_up': w_ffn_up,
            'w_ffn_down': w_ffn_down, 'w_in': w_in, 'b_forget': b_forget, 'b_gate': b_gate,
            'ret_gn_g': ret_gn_g, 'w_ret_o': w_ret_o, 'w_fox_o': w_fox_o, 'w_mem_k': w_mem_k,
            'w_mem_v': w_mem_v, 'w_mem_o': w_mem_o, 'w_out': w_out}

def reference(x_prompt, x_sample, mem_prompt, cache_fox_k, cache_fox_v, cache_fox_logf, state_ret,
              cache_mem_k, cache_mem_v, page_table, ln_g, ln_b, w_ffn_gate, w_ffn_up, w_ffn_down,
              w_in, b_forget, b_gate, ret_gn_g, w_ret_o, w_fox_o, w_mem_k, w_mem_v, w_mem_o, w_out):
    bp, lp, _ = x_prompt.shape
    mem_k_p = (mem_prompt @ w_mem_k).reshape(bp, N_MEM, H_M, D_M)
    mem_v_p = (mem_prompt @ w_mem_v).reshape(bp, N_MEM, H_M, D_M)
    ret0 = jnp.zeros((bp, H_R, DK_R, DV_R), F32)
    pos_p = jnp.arange(lp, dtype=F32)
    y_p, fk_p, fv_p, lf_p, ret_p = decoder_layer(
        x_prompt, pos_p, ret0, None, None, None, mem_k_p, mem_v_p,
        ln_g, ln_b, w_ffn_gate, w_ffn_up, w_ffn_down, w_in, b_forget, b_gate,
        ret_gn_g, w_ret_o, w_fox_o, w_mem_o, w_out)

    db, n_pages = page_table.shape
    past_len = n_pages * PAGE_SIZE
    past_k = cache_fox_k[page_table].reshape(db, past_len, H_F, D_F)
    past_v = cache_fox_v[page_table].reshape(db, past_len, H_F, D_F)
    past_lf = cache_fox_logf[page_table].reshape(db, past_len, H_F)
    pos_s = past_len + jnp.arange(x_sample.shape[1], dtype=F32)
    y_s, fk_s, fv_s, lf_s, ret_s = decoder_layer(
        x_sample, pos_s, state_ret, past_k, past_v, past_lf, cache_mem_k, cache_mem_v,
        ln_g, ln_b, w_ffn_gate, w_ffn_up, w_ffn_down, w_in, b_forget, b_gate,
        ret_gn_g, w_ret_o, w_fox_o, w_mem_o, w_out)

    return (y_p, y_s, fk_p, fv_p, lf_p, ret_p, mem_k_p, mem_v_p, fk_s, fv_s, lf_s, ret_s)


_drawn_inputs = setup_inputs


def setup_inputs(seed=0):
    import zlib

    import numpy as np

    out = dict(_drawn_inputs(seed))
    spreads = {}
    factors = {'cache_fox_logf': 200.0,
     'cache_mem_k': 4.471,
     'cache_mem_v': 3.491,
     'ln_g': 3.173,
     'ln_b': 3.151,
     'b_gate': 28.99,
     'ret_gn_g': 200.0,
     'w_mem_o': 3.508,
     'cache_fox_k': 13.697,
     'cache_fox_v': 12.323}
    for name, (base, spread) in spreads.items():
        noise = np.random.default_rng([zlib.crc32(name.encode()), seed]).standard_normal(out[name].shape)
        drawn = base * np.exp(spread * noise) if base else spread * noise
        out[name] = __import__('jax').numpy.asarray(drawn.astype(out[name].dtype))
    for name, factor in factors.items():
        out[name] = (out[name] * factor).astype(out[name].dtype)
    return out
```

```python
from contextlib import ExitStack

import concourse.bass as bass
from concourse import mybir

F32 = mybir.dt.float32
F32R = mybir.dt.float32r
I32 = mybir.dt.int32
ALU = mybir.AluOpType
ACT = mybir.ActivationFunctionType
AX = mybir.AxisListType
ds = bass.ds

P = 128
D = 1024
KD = D // P
TP = 1024
NSEQ, LSEQ = 8, 8
TS = NSEQ * LSEQ
T = TP + TS
NB, TB = 3, 364
TW = NB * TB
NCH = TP // P
D_FF = 2816
FT = D_FF // P
FC = 4
H_R, DK, H_F, DF, H_M, DM = 4, 64, 8, 64, 4, 128
N_MEM, PAGE, NPG = 256, 128, 32
PAST = PAGE * NPG
C_FQ, C_FL, C_MQ, C_GATE = 1536, 3072, 3080, 3592
ALPHA = 2.0 ** 0.25
EPS = 1e-5
NEG = -1e30
PAIRS = H_F // 2
RING = 16


def gammas():
    import numpy as np
    h = np.arange(H_R, dtype=np.float32)
    return np.log1p(-np.exp2(np.float32(-5.0) - h)).astype(np.float32)


def decays(c):
    import numpy as np
    return [float(np.exp(np.float32(c) * g, dtype=np.float32)) for g in gammas()]


def shape_tables():
    import numpy as np
    f = np.float32
    lg = gammas()
    ident = np.eye(P, dtype=f)
    rot = np.zeros((P, P), f)
    for m in range(P):
        if m % DK < DK // 2:
            rot[m + DK // 2, m] = -1.0
        else:
            rot[m - DK // 2, m] = 1.0
    half = DK // 2
    inv = (10000.0 ** (-np.arange(half) / half)).astype(f)
    pos = np.concatenate([np.arange(TP, dtype=f), np.tile(PAST + np.arange(LSEQ, dtype=f), NSEQ)])
    ang = (pos[None, :] * inv[:, None]).astype(f)
    cos = np.tile(np.cos(ang), (4, 1)).astype(f)
    sin = np.tile(np.sin(ang), (4, 1)).astype(f)

    def dec(steps):
        return np.exp(steps[..., None].astype(f) * lg).astype(f)

    i = np.arange(P)
    j = np.arange(TS)
    scale = f(DK ** -0.5)
    qd = dec(i + 1).T.reshape(2, 2, 1, P).transpose(1, 2, 0, 3)
    q_dec = np.broadcast_to(qd, (2, DK, 2, P)).reshape(P, 2, P)
    qs = dec(j % LSEQ + 1).T.reshape(2, 2, 1, TS).transpose(1, 2, 0, 3)
    q_dec_s = np.broadcast_to(qs, (2, DK, 2, TS)).reshape(P, 2, TS)
    k_dec = np.repeat(dec(P - 1 - i) * scale, DK, axis=1)
    k_dec_s = np.repeat(dec(LSEQ - 1 - j % LSEQ) * scale, DK, axis=1)
    d = i[None, :] - i[:, None]
    dmask = (np.where(d[..., None] >= 0, dec(np.maximum(d, 0)), 0) * scale).transpose(0, 2, 1)
    e = j[None, :] - j[:, None]
    same = (j[None, :] // LSEQ == j[:, None] // LSEQ) & (e >= 0)
    dmask_s = (np.where(same[..., None], dec(np.maximum(e, 0)), 0) * scale).transpose(0, 2, 1)
    causal = np.where(i[:, None] >= i[None, :], 0.0, NEG)
    seq = (j[:, None] // LSEQ == np.arange(NSEQ)[None, :])
    cols = np.broadcast_to(seq.T[None], (P, NSEQ, TS))
    new = np.where(seq[:, :, None] & (j[:, None, None] % LSEQ <= np.arange(LSEQ)), 0.0, NEG)
    pair_row = np.zeros((2, 2, P), f)
    pair_row[0, 0] = 1.0
    pair_row[1, 1] = 1.0
    tables = {
        "ident": ident, "rot": rot, "cos": cos, "sin": sin,
        "q_dec": q_dec, "q_dec_s": q_dec_s, "k_dec": k_dec, "k_dec_s": k_dec_s,
        "dmask": dmask, "dmask_s": dmask_s, "causal": causal, "seq_rows": seq, "seq_cols": cols,
        "new_mask": new, "pair_row": pair_row,
        "after": (i[:, None] > i[None, :]),
        "upto": (same & (e >= 0)),
    }
    return {n: np.ascontiguousarray(a, dtype=f) for n, a in tables.items()}


class Chain:

    def __init__(self, sem, base=0):
        self.sem, self.base, self.n = sem, base, 0

    def mark(self, instruction):
        instruction.then_inc(self.sem, 1)
        self.n += 1

    def wait(self, engine):
        engine.wait_ge(self.sem, self.base + self.n)


class Weights:

    def __init__(self, nc, ctx):
        self.nc = nc
        self.loaded = [ctx.enter_context(nc.semaphore(f"w_loaded{s}")) for s in range(2)]
        self.high = [ctx.enter_context(nc.semaphore(f"w_high{s}")) for s in range(2)]
        self.low = [ctx.enter_context(nc.semaphore(f"w_low{s}")) for s in range(2)]
        self.done = [ctx.enter_context(nc.semaphore(f"w_done{s}")) for s in range(2)]
        self.passed = ctx.enter_context(nc.semaphore("w_passed"))
        self.n = [0, 0]

    def open(self, ctx, tag):
        nc = self.nc
        self.raw = [ctx.enter_context(nc.sbuf_tensor(f"w_raw{s}_{tag}", [P, KD, P], F32)) for s in range(2)]
        self.hi = [ctx.enter_context(nc.sbuf_tensor(f"w_hi{s}_{tag}", [P, KD, P], F32R)) for s in range(2)]
        self.lo = [ctx.enter_context(nc.sbuf_tensor(f"w_lo{s}_{tag}", [P, KD, P], F32R)) for s in range(2)]

    def load(self, sp, s, n, src, kt):
        sp.wait_ge(self.low[s], n + 1)
        sp.dma_start(self.raw[s][:, 0:kt, :], src.rearrange("(k p) c -> p k c", p=P))\
          .then_inc(self.loaded[s], 16)

    def split(self, pool, s, n, kt):
        raw, hi, lo = (x[s][:, 0:kt, :] for x in (self.raw, self.hi, self.lo))
        pool.wait_ge(self.loaded[s], n * 16 + 16)
        pool.wait_ge(self.done[s], n + 1)
        pool.sem_inc(self.passed, 1)
        self.nc.gpsimd.tensor_copy(hi, raw).then_inc(self.high[s], 1)
        pool.wait_ge(self.high[s], n + 1)
        self.nc.gpsimd.tensor_tensor(lo, raw, hi.bitcast(F32), ALU.subtract).then_inc(self.low[s], 1)

    def products(self, pe, s, n, kt, out, x_hi, x_lo, width=TB, blocks=NB, ready=None):
        pe.wait_ge(self.low[s], n + 2)
        for k in range(kt):
            if ready is not None:
                pe.wait_ge(ready[0], ready[1] + k)
            for w, x, first, last in ((self.hi, x_hi, True, False), (self.hi, x_lo, False, False),
                                      (self.lo, x_hi, False, True)):
                for b in range(blocks):
                    mm = self.nc.tensor.matmul(out[:, b, 0:width], w[s][:, k, :],
                                               x[:, k, b * width:(b + 1) * width],
                                               start=(k == 0 and first), stop=(k == kt - 1 and last))
        mm.then_inc(self.done[s], 1)


class Build:

    def __init__(self, nc, ctx, io):
        self.nc, self.ctx, self.io = nc, ctx, io
        self.sems = []

    def sem(self, name):
        self.sems.append(self.nc.alloc_semaphore(name))
        return self.sems[-1]

    def end_phase(self):
        for sem in self.sems:
            self.nc.gpsimd.sem_clear(sem)
        self.nc.all_engine_barrier()
        for sem in self.sems:
            self.nc.release_semaphore(sem)
        self.sems = []

    def sb(self, ctx, name, shape, dt=F32):
        return ctx.enter_context(self.nc.sbuf_tensor(name, shape, dt))

    def ps(self, ctx, name, shape):
        size = 1
        for n in shape[1:]:
            size *= n
        whole = ctx.enter_context(self.nc.psum_tensor(name, [shape[0], -(-size // 512) * 512], F32))
        flat = whole[:, 0:size]
        return flat if len(shape) == 2 else flat.rearrange("p (a b) -> p a b", b=shape[2]) if len(shape) == 3 \
            else flat.rearrange("p (a b c) -> p a b c", b=shape[2], c=shape[3])


def blocks_of(tile):
    return tile.rearrange("p (b t) -> p b t", t=TB)


def phase_load(g):
    nc, io = g.nc, g.io
    with ExitStack() as ctx:
        xin = [g.sb(ctx, f"x_in{s}", [P, D]) for s in range(2)]
        xt = [g.ps(ctx, f"x_t{s}", [P, KD, P]) for s in range(2)]
        consts, ones = g.sem("consts_loaded"), g.sem("ones_set")
        loaded = [g.sem(f"x_loaded{s}") for s in range(2)]
        turned = [g.sem(f"x_turned{s}") for s in range(2)]
        hi = [g.sem(f"x_hi{s}") for s in range(2)]
        lo = [g.sem(f"x_lo{s}") for s in range(2)]
        acc = [g.sem(f"x_acc{s}") for s in range(2)]
        n_const = 8
        xs = io["x_sample"].rearrange("b t d -> (b t) d")
        with nc.Block() as block:
            @block.sync
            def _(sp):
                for s in range(2):
                    for sem in (g.w.low[s], g.w.done[s], turned[s], lo[s], acc[s]):
                        sp.sem_inc(sem, 1)
                sp.dma_start(g.ident[:], io["ident"]).then_inc(consts, 16)
                sp.dma_start(g.ln_g[:], io["ln_g"].rearrange("l (k p) -> p l k", p=P),
                             allow_slow_non_contiguous=True).then_inc(consts, 16)
                sp.dma_start(g.ln_b[:], io["ln_b"].rearrange("l (k p) -> p l k", p=P),
                             allow_slow_non_contiguous=True).then_inc(consts, 16)
                sp.dma_start(g.b_gate[:], io["b_gate"].rearrange("i (k p) -> p i k", p=P),
                             allow_slow_non_contiguous=True).then_inc(consts, 16)
                sp.dma_start(g.gn_g[:], io["ret_gn_g"].rearrange("(h p) -> p h", p=P),
                             allow_slow_non_contiguous=True).then_inc(consts, 16)
                sp.dma_start(g.b_forget[:], io["b_forget"].rearrange("(h o) -> h o", o=1)).then_inc(consts, 16)
                sp.dma_start(g.pages[:], io["page_table"].rearrange("b n -> (b n)").unsqueeze(0)).then_inc(consts, 16)
                sp.dma_start(g.causal[:], io["causal"]).then_inc(consts, 16)
                with sp.Fori(0, NCH // 2) as i:
                    for s in range(2):
                        src = io["x_prompt"][0, ds((i * 2 + s) * P, P), :]
                        sp.wait_ge(turned[s], i + 1)
                        sp.dma_start(xin[s][:], src).then_inc(loaded[s], 16)
                sp.wait_ge(turned[0], NCH // 2 + 1)
                sp.dma_start(xin[0][0:TS, :], xs).then_inc(loaded[0], 16)
                sp.wait_ge(consts, 16 * n_const)

            def turn(pe, s, n, rows):
                pe.wait_ge(loaded[s], n * 16 + 16)
                pe.wait_ge(lo[s], n + 1)
                pe.wait_ge(acc[s], n + 1)
                for k in range(KD):
                    mm = nc.tensor.transpose(xt[s][:, k, 0:rows], xin[s][0:rows, k * P:(k + 1) * P],
                                             g.ident[0:rows, 0:rows])
                mm.then_inc(turned[s], 1)

            @block.tensor
            def _(pe):
                pe.wait_ge(consts, 16 * n_const)
                with pe.Fori(0, NCH // 2) as i:
                    for s in range(2):
                        turn(pe, s, i, P)
                turn(pe, 0, NCH // 2, TS)

            @block.scalar
            def _(act):
                def copies(s, n, hi_dst, acc_dst, rows):
                    act.wait_ge(turned[s], n + 2)
                    nc.scalar.copy(hi_dst, xt[s][:, :, 0:rows]).then_inc(hi[s], 1)
                    nc.scalar.mul(acc_dst, xt[s][:, :, 0:rows], ALPHA).then_inc(acc[s], 1)
                with act.Fori(0, NCH // 2) as i:
                    for s in range(2):
                        at = ds((i * 2 + s) * P, P)
                        copies(s, i, g.xh[:, :, at], g.res[:, :, at], P)
                copies(0, NCH // 2, g.xh[:, :, TP:T], g.res[:, :, TP:T], TS)

            @block.vector
            def _(dve):
                nc.vector.memset(g.xh[:, :, T:TW].bitcast(F32), 0.0)
                nc.vector.memset(g.xl[:, :, T:TW].bitcast(F32), 0.0)
                nc.vector.memset(g.res[:, :, T:TW], 0.0)
                nc.vector.memset(g.ones[:], 1.0)

                def lows(s, n, lo_dst, hi_src, rows):
                    dve.wait_ge(hi[s], n + 1)
                    dve.wait_ge(acc[s], n + 2)
                    nc.vector.tensor_tensor(lo_dst, xt[s][:, :, 0:rows], hi_src.bitcast(F32), ALU.subtract)\
                        .then_inc(lo[s], 1)
                with dve.Fori(0, NCH // 2) as i:
                    for s in range(2):
                        at = ds((i * 2 + s) * P, P)
                        lows(s, i, g.xl[:, :, at], g.xh[:, :, at], P)
                lows(0, NCH // 2, g.xl[:, :, TP:T], g.xh[:, :, TP:T], TS)


def phase_memory(g):
    nc, io, w = g.nc, g.io, g.w
    MT = N_MEM // P
    with ExitStack() as ctx:
        w.open(ctx, "mem")
        m_in = g.sb(ctx, "m_in", [P, MT, D])
        mh = g.sb(ctx, "mh", [P, KD, N_MEM], F32R)
        ml = g.sb(ctx, "ml", [P, KD, N_MEM], F32R)
        kv = [g.sb(ctx, f"m_kv{s}", [P, N_MEM]) for s in range(2)]
        kn = g.sb(ctx, "m_kn", [P, MT, H_M * DM])
        acc = [g.ps(ctx, f"m_acc{s}", [P, 1, 512]) for s in range(2)]
        mt = g.ps(ctx, "m_t", [P, KD, P])
        tn = g.ps(ctx, "m_tn", [P, 2, MT, P])
        loaded, turned, hi, lo = g.sem("m_loaded"), g.sem("m_turned"), g.sem("m_hi"), g.sem("m_lo")
        kv_out = [g.sem(f"m_kv_out{s}") for s in range(2)]
        nat, nat_out, stored = g.sem("m_nat"), g.sem("m_nat_out"), g.sem("m_stored")
        kt_out = g.sem("m_kt_out")
        base = list(w.n)
        with nc.Block() as block:
            @block.sync
            def _(sp):
                for s in range(2):
                    sp.sem_inc(kv_out[s], 1)
                sp.sem_inc(nat_out, 1)
                sp.dma_start(m_in[:], io["mem_prompt"][0].rearrange("(m p) d -> p m d", p=P)).then_inc(loaded, 16)
                with sp.Fori(0, H_M) as h:
                    for s, name in enumerate(("w_mem_k", "w_mem_v")):
                        w.load(sp, s, h + base[s], io[name][:, ds(h * DM, DM)], KD)
                sp.wait_ge(nat_out, H_M + 1)
                for name, src in (("mem_k_prompt", kn), ("mem_v_prompt", g.mem_v)):
                    sp.dma_start(io[name][0].rearrange("(m p) h d -> p m (h d)", p=P), src[:]).then_inc(stored, 16)
                sp.wait_ge(stored, 32)

            @block.gpsimd
            def _(pool):
                with pool.Fori(0, H_M) as h:
                    for s in range(2):
                        w.split(pool, s, h + base[s], KD)

            @block.tensor
            def _(pe):
                pe.wait_ge(loaded, 16)
                for m in range(MT):
                    if m > 0:
                        pe.wait_ge(lo, m)
                    for k in range(KD):
                        mm = nc.tensor.transpose(mt[:, k, :], m_in[:, m, k * P:(k + 1) * P], g.ident[:])
                    mm.then_inc(turned, 1)
                pe.wait_ge(lo, MT)
                with pe.Fori(0, H_M) as h:
                    for s in range(2):
                        pe.wait_ge(kv_out[s], h + 1)
                        w.products(pe, s, h + base[s], KD, acc[s], mh, ml, width=N_MEM, blocks=1)
                    pe.wait_ge(nat_out, h + 1)
                    for s in range(2):
                        pe.wait_ge(kv_out[s], h + 2)
                        for m in range(MT):
                            mm = nc.tensor.transpose(tn[:, s, m, :], kv[s][:, m * P:(m + 1) * P], g.ident[:])
                    mm.then_inc(nat, 1)

            @block.scalar
            def _(act):
                for m in range(MT):
                    act.wait_ge(turned, m + 1)
                    nc.scalar.copy(mh[:, :, m * P:(m + 1) * P], mt[:]).then_inc(hi, 1)
                with act.Fori(0, H_M) as h:
                    act.wait_ge(w.done[0], h + (base[0] + 2))
                    nc.scalar.copy(kv[0][:], acc[0][:, 0, 0:N_MEM]).then_inc(kv_out[0], 1)
                    dst = g.mem_kt[:, h, :]
                    act.wait_ge(kv_out[0], h + 2)
                    nc.scalar.copy(dst, kv[0][:]).then_inc(kt_out, 1)
                    act.wait_ge(kt_out, h + 1)
                    act.wait_ge(nat, h + 1)

            @block.vector
            def _(dve):
                for m in range(MT):
                    dve.wait_ge(hi, m + 1)
                    nc.vector.tensor_tensor(ml[:, :, m * P:(m + 1) * P], mt[:],
                                            mh[:, :, m * P:(m + 1) * P].bitcast(F32), ALU.subtract).then_inc(lo, 1)
                with dve.Fori(0, H_M) as h:
                    dve.wait_ge(w.done[1], h + (base[1] + 2))
                    nc.vector.tensor_copy(kv[1][:], acc[1][:, 0, 0:N_MEM]).then_inc(kv_out[1], 1)
                    k_dst, v_dst = kn[:, :, ds(h * DM, DM)], g.mem_v[:, :, ds(h * DM, DM)]
                    dve.wait_ge(nat, h + 1)
                    nc.vector.tensor_copy(k_dst, tn[:, 0])
                    nc.vector.tensor_copy(v_dst, tn[:, 1]).then_inc(nat_out, 1)
        w.n = [x + H_M for x in base]


def phase_ffn(g, layer):
    nc, io, w = g.nc, g.io, g.w
    wg, wu, wd = (io[n][layer] for n in ("w_ffn_gate", "w_ffn_up", "w_ffn_down"))
    full = FT // FC
    rest = FT - full * FC
    per = FC + KD // 2
    with ExitStack() as ctx:
        w.open(ctx, f"ffn{layer}")
        hh = g.sb(ctx, f"h_hi{layer}", [P, FC, TW], F32R)
        hl = g.sb(ctx, f"h_lo{layer}", [P, FC, TW], F32R)
        silu = g.sb(ctx, f"silu{layer}", [P, TW])
        hid = g.sb(ctx, f"hid{layer}", [P, TW])
        acc = [g.ps(ctx, f"f_acc{s}_{layer}", [P, NB, 512]) for s in range(2)]
        free = [g.sem(f"f_free{s}_{layer}") for s in range(2)]
        hh_ok, hl_ok = g.sem(f"f_hh{layer}"), g.sem(f"f_hl{layer}")
        b0, b1 = w.n
        with nc.Block() as block:
            @block.sync
            def _(sp):
                for s in range(2):
                    sp.sem_inc(free[s], 1)

                def ups(c, n, ft):
                    with sp.Fori(0, ft) as f:
                        at = ds((c * FC + f) * P, P)
                        w.load(sp, 0, n + f + b0, wg[:, at], KD)
                        w.load(sp, 1, n + f + b1, wu[:, at], KD)

                def downs(c, n, ft):
                    with sp.Fori(0, KD // 2) as j:
                        for s in range(2):
                            src = wd[ds(c * (FC * P), ft * P), ds((j * 2 + s) * P, P)]
                            w.load(sp, s, n + j + (b0, b1)[s], src, ft)

                with sp.Fori(0, full) as c:
                    ups(c, c * per, FC)
                    downs(c, c * per + FC, FC)
                ups(full, full * per, rest)
                downs(full, full * per + rest, rest)

            @block.tensor
            def _(pe):
                def ups(n, ft):
                    with pe.Fori(0, ft) as f:
                        for s in range(2):
                            pe.wait_ge(free[s], n + f + 1)
                            w.products(pe, s, n + f + (b0, b1)[s], KD, acc[s], g.xh, g.xl)

                def downs(c, n, ft):
                    with pe.Fori(0, KD // 2) as j:
                        for s in range(2):
                            pe.wait_ge(free[s], n + j + 1)
                            w.products(pe, s, n + j + (b0, b1)[s], ft, acc[s], hh, hl,
                                       ready=(hl_ok, c * FC + 1))

                with pe.Fori(0, full) as c:
                    ups(c * per, FC)
                    downs(c, c * per + FC, FC)
                ups(full * per, rest)
                downs(full, full * per + rest, rest)

            @block.gpsimd
            def _(pool):
                def tiles(n, count, kt):
                    with pool.Fori(0, count) as j:
                        for s in range(2):
                            w.split(pool, s, n + j + (b0, b1)[s], kt)

                with pool.Fori(0, full) as c:
                    tiles(c * per, FC, KD)
                    tiles(c * per + FC, KD // 2, FC)
                tiles(full * per, rest, KD)
                tiles(full * per + rest, KD // 2, rest)

            @block.scalar
            def _(act):
                act.preload_act_table(ACT.Silu)

                def ups(c, n, ft):
                    with act.Fori(0, ft) as f:
                        dst = hh[:, f, :]
                        act.wait_ge(w.done[0], n + f + (b0 + 2))
                        nc.scalar.activation(blocks_of(silu[:]), acc[0][:, :, 0:TB], ACT.Silu)\
                            .then_inc(free[0], 1)
                        act.wait_ge(free[1], n + f + 2)
                        nc.scalar.copy(dst, hid[:]).then_inc(hh_ok, 1)

                with act.Fori(0, full) as c:
                    ups(c, c * per, FC)
                ups(full, full * per, rest)

            @block.vector
            def _(dve):
                def ups(c, n, ft):
                    with dve.Fori(0, ft) as f:
                        hi_src, lo_dst = hh[:, f, :], hl[:, f, :]
                        dve.wait_ge(free[0], n + f + 2)
                        dve.wait_ge(w.done[1], n + f + (b1 + 2))
                        nc.vector.tensor_tensor(blocks_of(hid[:]), blocks_of(silu[:]), acc[1][:, :, 0:TB],
                                                ALU.mult).then_inc(free[1], 1)
                        dve.wait_ge(free[1], n + f + 2)
                        dve.wait_ge(hh_ok, c * FC + f + 1)
                        nc.vector.tensor_tensor(lo_dst, hid[:], hi_src.bitcast(F32), ALU.subtract)\
                            .then_inc(hl_ok, 1)
                        dve.wait_ge(hl_ok, c * FC + f + 1)

                def downs(n, ft):
                    with dve.Fori(0, KD // 2) as j:
                        for s in range(2):
                            row = g.res[:, j * 2 + s, :]
                            dve.wait_ge(w.done[s], n + j + ((b0, b1)[s] + 2))
                            nc.vector.scalar_tensor_tensor(blocks_of(row), acc[s][:, :, 0:TB], 0.5, blocks_of(row),
                                                           ALU.mult, ALU.add).then_inc(free[s], 1)

                with dve.Fori(0, full) as c:
                    ups(c, c * per, FC)
                    downs(c * per + FC, FC)
                ups(full, full * per, rest)
                downs(full * per + rest, rest)
        used = full * per + rest + KD // 2
        w.n = [b0 + used, b1 + used]


def phase_norm(g, which, last):
    nc = g.nc
    with ExitStack() as ctx:
        mean_w = g.sb(ctx, f"mean_w{which}", [P, P])
        sq = g.sb(ctx, f"sq{which}", [P, KD, TB])
        rstd = [g.sb(ctx, f"rstd{b}_{which}", [P, TB]) for b in range(NB)]
        std = [g.sb(ctx, f"std{b}_{which}", [P, TB]) for b in range(NB)]
        hn = [g.sb(ctx, f"hn{s}_{which}", [P, KD, TB]) for s in range(2)]
        eps = g.sb(ctx, f"eps{which}", [P, 1])
        mean = [g.ps(ctx, f"mean{b}_{which}", [P, 512]) for b in range(NB)]
        var = [g.ps(ctx, f"var{b}_{which}", [P, 512]) for b in range(NB)]
        ready, mean_ok, var_ok = g.sem(f"n_ready{which}"), g.sem(f"n_mean{which}"), g.sem(f"n_var{which}")
        centred, squared, std_ok = g.sem(f"n_centred{which}"), g.sem(f"n_squared{which}"), g.sem(f"n_std{which}")
        rstd_ok, scaled, affine = g.sem(f"n_rstd{which}"), g.sem(f"n_scaled{which}"), g.sem(f"n_affine{which}")
        high, low = g.sem(f"n_high{which}"), g.sem(f"n_low{which}")

        def cols(b):
            return slice(b * TB, (b + 1) * TB)

        def over_k(tile):
            return tile.unsqueeze(1).broadcast_to([P, KD, TB])
        with nc.Block() as block:
            @block.gpsimd
            def _(pool):
                nc.gpsimd.memset(mean_w[:], 1.0 / D).then_inc(ready, 1)
                nc.gpsimd.memset(eps[:], EPS).then_inc(ready, 1)

            @block.tensor
            def _(pe):
                pe.wait_ge(ready, 2)
                for b in range(NB):
                    for k in range(KD):
                        mm = nc.tensor.matmul(mean[b][:, 0:TB], mean_w[:], g.res[:, k, cols(b)],
                                              start=(k == 0), stop=(k == KD - 1))
                    mm.then_inc(mean_ok, 1)
                for b in range(NB):
                    pe.wait_ge(squared, b + 1)
                    for k in range(KD):
                        mm = nc.tensor.matmul(var[b][:, 0:TB], mean_w[:], sq[:, k, :],
                                              start=(k == 0), stop=(k == KD - 1))
                    mm.then_inc(var_ok, 1)

            @block.vector
            def _(dve):
                for b in range(NB):
                    dve.wait_ge(mean_ok, b + 1)
                    nc.vector.tensor_tensor(g.res[:, :, cols(b)], g.res[:, :, cols(b)],
                                            over_k(mean[b][:, 0:TB]), ALU.subtract).then_inc(centred, 1)
                for b in range(NB):
                    dve.wait_ge(std_ok, b + 1)
                    nc.vector.reciprocal(rstd[b][:], std[b][:]).then_inc(rstd_ok, 1)
                    dve.wait_ge(rstd_ok, b + 1)
                    nc.vector.tensor_tensor(g.res[:, :, cols(b)], g.res[:, :, cols(b)], over_k(rstd[b][:]),
                                            ALU.mult).then_inc(scaled, 1)
                    if not last and b > 0:
                        dve.wait_ge(high, b)
                        nc.vector.tensor_tensor(g.xl[:, :, cols(b - 1)], hn[(b - 1) % 2][:],
                                                g.xh[:, :, cols(b - 1)].bitcast(F32), ALU.subtract).then_inc(low, 1)
                if not last:
                    dve.wait_ge(high, NB)
                    nc.vector.tensor_tensor(g.xl[:, :, cols(NB - 1)], hn[(NB - 1) % 2][:],
                                            g.xh[:, :, cols(NB - 1)].bitcast(F32), ALU.subtract).then_inc(low, 1)

            @block.scalar
            def _(act):
                act.wait_ge(ready, 2)
                for b in range(NB):
                    act.wait_ge(centred, b + 1)
                    if b > 0:
                        act.wait_ge(var_ok, b)
                    nc.scalar.activation(sq[:], g.res[:, :, cols(b)], ACT.Square).then_inc(squared, 1)
                for b in range(NB):
                    act.wait_ge(var_ok, b + 1)
                    nc.scalar.activation(std[b][:], var[b][:, 0:TB], ACT.Sqrt, bias=eps[:]).then_inc(std_ok, 1)
                for b in range(NB):
                    act.wait_ge(scaled, b + 1)
                    if not last and b >= 2:
                        act.wait_ge(low, b - 1)
                    for k in range(KD):
                        dst = g.res[:, k, cols(b)] if last else hn[b % 2][:, k, :]
                        nc.scalar.activation(dst, g.res[:, k, cols(b)], ACT.Identity,
                                             bias=g.ln_b[:, which, k:k + 1], scale=g.ln_g[:, which, k:k + 1])\
                            .then_inc(affine, 1)
                    if not last:
                        act.wait_ge(affine, KD * (b + 1))
                        nc.scalar.copy(g.xh[:, :, cols(b)], hn[b % 2][:]).then_inc(high, 1)
                        nc.scalar.mul(g.res[:, :, cols(b)], hn[b % 2][:], ALPHA)


def phase_retention_in(g):
    nc, io, w = g.nc, g.io, g.w
    pairs, plain = 6, 4
    with ExitStack() as ctx:
        w.open(ctx, "ret")
        acc = [g.ps(ctx, f"r_acc{s}", [P, NB, 512]) for s in range(2)]
        free = [g.sem(f"r_free{s}") for s in range(2)]
        b0, b1 = w.n
        with nc.Block() as block:
            @block.sync
            def _(sp):
                for s in range(2):
                    sp.sem_inc(free[s], 1)
                with sp.Fori(0, pairs) as n:
                    for s in range(2):
                        w.load(sp, s, n + (b0, b1)[s], io["w_in"][:, ds((n * 2 + s) * P, P)], KD)

            @block.gpsimd
            def _(pool):
                with pool.Fori(0, pairs) as n:
                    for s in range(2):
                        w.split(pool, s, n + (b0, b1)[s], KD)

            @block.tensor
            def _(pe):
                with pe.Fori(0, pairs) as n:
                    for s in range(2):
                        pe.wait_ge(free[s], n + 1)
                        w.products(pe, s, n + (b0, b1)[s], KD, acc[s], g.xh, g.xl)

            @block.scalar
            def _(act):
                act.preload_act_table(ACT.Silu)
                with act.Fori(0, plain) as n:
                    dst = blocks_of(g.br[:, n * 2 + 4, :])
                    act.wait_ge(w.done[0], n + (b0 + 2))
                    nc.scalar.copy(dst, acc[0][:, :, 0:TB]).then_inc(free[0], 1)
                with act.Fori(plain, pairs) as n:
                    for s in range(2):
                        dst = blocks_of(g.br[:, n * 2 + (s - 2 * plain), :])
                        act.wait_ge(w.done[s], n + ((b0, b1)[s] + 2))
                        nc.scalar.activation(dst, acc[s][:, :, 0:TB], ACT.Silu).then_inc(free[s], 1)

            @block.vector
            def _(dve):
                with dve.Fori(0, plain) as n:
                    dst = blocks_of(g.br[:, n * 2 + 5, :])
                    dve.wait_ge(w.done[1], n + (b1 + 2))
                    nc.vector.tensor_copy(dst, acc[1][:, :, 0:TB]).then_inc(free[1], 1)
        w.n = [b0 + pairs, b1 + pairs]


HALVES = [slice(0, DK), slice(DK, P)]


def phase_retention(g):
    nc, io = g.nc, g.io
    dec_c, dec_s = decays(P), decays(LSEQ)
    with ExitStack() as ctx:
        def sb(name, shape):
            return g.sb(ctx, "rt_" + name, shape)
        cos, sin, rot = sb("cos", [P, T]), sb("sin", [P, T]), sb("rot", [P, P])
        q_dec, k_dec, dmask = sb("q_dec", [P, 2, P]), sb("k_dec", [P, H_R * DK]), sb("dmask", [P, H_R, P])
        q_dec_s, k_dec_s = sb("q_dec_s", [P, 2, TS]), sb("k_dec_s", [TS, H_R * DK])
        dmask_s, seq_rows, seq_cols = sb("dmask_s", [TS, H_R, TS]), sb("seq_rows", [TS, NSEQ]), sb("seq_cols", [P, NSEQ, TS])
        stage = sb("stage", [P, 8, P])
        turned, qk, qd = sb("turned", [P, 4, P]), sb("qk", [P, 4, P]), sb("qd", [P, 2, 2, P])
        qz = sb("qz", [P, 2, 2, P])
        kd, vn, at = sb("kd", [P, H_R * DK]), sb("vn", [P, H_R, P]), sb("at", [P, H_R, P])
        state = sb("state", [P, 2, DM])
        s0, s1 = sb("s0", [P, 2, DM]), sb("s1", [P, 2, DM])
        kdm, qdm = sb("kdm", [TS, H_R * DK]), sb("qdm", [P, 2, 2, TS])
        swap = g.ps(ctx, "rt_swap", [P, 4, P])
        vt = g.ps(ctx, "rt_vt", [P, H_R, P])
        kt = g.ps(ctx, "rt_kt", [P, 2, P])
        scores = g.ps(ctx, "rt_scores", [P, H_R, P])
        o = g.ps(ctx, "rt_o", [P, H_R, P])
        o_s = g.ps(ctx, "rt_o_s", [P, H_R, P])
        upd = g.ps(ctx, "rt_upd", [P, H_R, P])
        names = {"cos": cos, "sin": sin, "rot": rot, "q_dec": q_dec, "k_dec": k_dec, "dmask": dmask,
                 "q_dec_s": q_dec_s, "k_dec_s": k_dec_s, "dmask_s": dmask_s, "seq_rows": seq_rows, "seq_cols": seq_cols}
        consts, zeroed = g.sem("rt_consts"), g.sem("rt_zeroed")
        staged, pe_swap, roped = g.sem("rt_staged"), g.sem("rt_pe_swap"), g.sem("rt_roped")
        v_nat, pe_scores, masked = g.sem("rt_v_nat"), g.sem("rt_pe_scores"), g.sem("rt_masked")
        pe_out, o_read, state_ok = g.sem("rt_pe_out"), g.sem("rt_o_read"), g.sem("rt_state")
        steps = g.sem("rt_steps")
        loaded, s_masked, s_pe = g.sem("rt_s_loaded"), g.sem("rt_s_masked"), g.sem("rt_s_pe")
        s_new, s_stored, stored = g.sem("rt_s_new"), g.sem("rt_s_stored"), g.sem("rt_stored")
        STEPS = 2

        def rope(dve, chain, t_cos, t_sin, q_decay, n, src):
            nc.vector.tensor_tensor(turned[:, :, 0:n], src, t_cos.unsqueeze(1).broadcast_to([P, 4, n]), ALU.mult)
            chain.mark(nc.vector.tensor_tensor(qk[:, :, 0:n], swap[:, :, 0:n],
                                               t_sin.unsqueeze(1).broadcast_to([P, 4, n]), ALU.mult))
            chain.wait(dve)
            nc.vector.tensor_tensor(qk[:, 2:4, 0:n], qk[:, 2:4, 0:n], turned[:, 2:4, 0:n], ALU.add)
            for s, rows in enumerate(HALVES):
                ins = nc.vector.tensor_tensor(qz[rows, s, :, 0:n], qk[rows, 0:2, 0:n], turned[rows, 0:2, 0:n], ALU.add)
            chain.mark(ins)
            chain.wait(dve)
            for s, rows in enumerate(HALVES):
                ins = nc.vector.tensor_tensor(qd[rows, s, :, 0:n], qz[rows, s, :, 0:n], q_decay[rows], ALU.mult)
            ins.then_inc(roped, 1)

        def chunk_scores(n):
            for p in range(2):
                nc.tensor.transpose(kt[0:n, p, :], qk[:, 2 + p, 0:n], g.ident[:])
            for h in range(H_R):
                mm = nc.tensor.matmul(scores[0:n, h, 0:n], qk[:, 2 + h // 2, 0:n], qz[:, h % 2, h // 2, 0:n],
                                      start=True, stop=True)
            mm.then_inc(pe_scores, 1)

        with nc.Block() as block:
            @block.sync
            def _(sp):
                for sem in (roped, v_nat, o_read, s_new, s_stored):
                    sp.sem_inc(sem, 16 if sem is s_stored else 1)
                for name, dst in names.items():
                    sp.dma_start(dst[:], io[name]).then_inc(consts, 16)
                with sp.Fori(0, NSEQ) as b:
                    src = io["state_ret"][b].rearrange("(pr two) d e -> two d pr e", two=2)
                    new = io["ret_state_sample"][b].rearrange("(pr two) d e -> two d pr e", two=2)
                    halves = [(src[i], new[i]) for i in range(2)]
                    sp.wait_ge(s_new, b + 1)
                    for i in range(2):
                        sp.dma_start(s0[HALVES[i]], src[i]).then_inc(loaded, 16)
                    sp.wait_ge(s_new, b + 2)
                    for i in range(2):
                        sp.dma_start(new[i], s1[HALVES[i]]).then_inc(s_stored, 16)
                sp.wait_ge(state_ok, NCH + 1)
                dst = io["ret_state_prompt"][0].rearrange("(pr two) d e -> two d pr e", two=2)
                for i in range(2):
                    sp.dma_start(dst[i], state[HALVES[i]]).then_inc(stored, 16)
                sp.wait_ge(stored, 32)
                sp.wait_ge(s_stored, 16 + 32 * NSEQ)

            @block.gpsimd
            def _(pool):
                nc.gpsimd.memset(qz[:], 0.0).then_inc(zeroed, 1)
                nc.gpsimd.memset(qd[:], 0.0).then_inc(zeroed, 1)
                with pool.Fori(0, NCH) as c:
                    src = g.br[:, 4:12, ds(c * P, P)]
                    pool.wait_ge(roped, c + 1)
                    pool.wait_ge(v_nat, c + 1)
                    pool.sem_inc(g.w.passed, 1)
                    nc.gpsimd.tensor_copy(stage[:], src).then_inc(staged, 1)

            @block.tensor
            def _(pe):
                pe.wait_ge(consts, 16 * len(names))
                with pe.Fori(0, NCH) as c:
                    pe.wait_ge(staged, c + 1)
                    nc.tensor.matmul(swap[:], rot[:], stage[:, 0:4, :], start=True, stop=True)
                    for h in range(H_R):
                        mm = nc.tensor.transpose(vt[:, h, :], stage[:, 4 + h, :], g.ident[:])
                    mm.then_inc(pe_swap, 1)
                    pe.wait_ge(roped, c + 2)
                    chunk_scores(P)
                    pe.wait_ge(masked, c + 1)
                    pe.wait_ge(v_nat, c + 2)
                    pe.wait_ge(state_ok, c + 1)
                    pe.wait_ge(o_read, c + 1)
                    for h in range(H_R):
                        nc.tensor.matmul(o[:, h, :], vn[:, h, :], at[:, h, :], start=True, stop=False)
                        nc.tensor.matmul(o[:, h, :], state[:, h // 2, :], qd[:, h % 2, h // 2, :],
                                         start=False, stop=True)
                    for h in range(H_R):
                        mm = nc.tensor.matmul(upd[:, h, :], kd[:, (h // 2) * P:(h // 2 + 1) * P], vn[:, h, :],
                                              start=True, stop=True)
                    mm.then_inc(pe_out, 1)
                nc.tensor.matmul(swap[:, :, 0:TS], rot[:], g.br[:, 4:8, TP:T], start=True, stop=True)
                for h in range(H_R):
                    mm = nc.tensor.transpose(vt[0:TS, h, :], g.br[:, 8 + h, TP:T], g.ident[:])
                mm.then_inc(pe_swap, 1)
                pe.wait_ge(roped, NCH + 2)
                chunk_scores(TS)
                pe.wait_ge(masked, NCH + 1)
                pe.wait_ge(v_nat, NCH + 2)
                for h in range(H_R):
                    nc.tensor.matmul(o_s[:, h, 0:TS], vn[0:TS, h, :], at[0:TS, h, 0:TS], start=(h == 0), stop=False,
                                     skip_group_check=True)
                with pe.Fori(0, NSEQ) as b:
                    pe.wait_ge(loaded, b * 32 + 32)
                    pe.wait_ge(s_masked, b + 1)
                    for h in range(H_R):
                        nc.tensor.matmul(o_s[:, h, 0:TS], s0[:, h // 2, :], qdm[:, h % 2, h // 2, :], start=False,
                                         stop=False, skip_group_check=True)
                    pe.wait_ge(s_new, b + 1)
                    for h in range(H_R):
                        mm = nc.tensor.matmul(upd[:, h, :], kdm[:, (h // 2) * P:(h // 2 + 1) * P], vn[0:TS, h, :],
                                              start=True, stop=True)
                    mm.then_inc(s_pe, 1)

            @block.scalar
            def _(act):
                with act.Fori(0, NCH) as c:
                    dst = g.br[:, 8:12, ds(c * P, P)]
                    act.wait_ge(pe_swap, c + 1)
                    nc.scalar.copy(vn[:], vt[:]).then_inc(v_nat, 1)
                    act.wait_ge(pe_out, c + 1)
                    nc.scalar.copy(dst, o[:]).then_inc(o_read, 1)
                act.wait_ge(pe_swap, NCH + 1)
                nc.scalar.copy(vn[0:TS], vt[0:TS]).then_inc(v_nat, 1)
                act.wait_ge(s_pe, NSEQ)
                nc.scalar.copy(g.br[:, 8:12, TP:T], o_s[:, :, 0:TS]).then_inc(o_read, 1)

            def masks(dve, mask, k_decay, n):
                nc.vector.tensor_tensor(at[0:n, :, 0:n], scores[0:n, :, 0:n], mask, ALU.mult)
                nc.vector.tensor_tensor(kd[0:n, :], kt[0:n].rearrange("p a b -> p (a b)"), k_decay, ALU.mult)\
                    .then_inc(masked, 1)

            def new_state(dst, old, dec, done):
                for h in range(H_R):
                    rows = HALVES[h % 2]
                    ins = nc.vector.scalar_tensor_tensor(dst[rows, h // 2, :], old[rows, h // 2, :], dec[h],
                                                         upd[rows, h, :], ALU.mult, ALU.add)
                ins.then_inc(done, 1)

            @block.vector
            def _(dve):
                dve.wait_ge(consts, 16 * len(names))
                nc.vector.memset(state[:], 0.0).then_inc(state_ok, 1)
                dve.wait_ge(zeroed, 2)
                with dve.Fori(0, NCH) as c:
                    t_cos, t_sin = cos[:, ds(c * P, P)], sin[:, ds(c * P, P)]
                    chain = Chain(steps, c * STEPS)
                    dve.wait_ge(staged, c + 1)
                    dve.wait_ge(pe_swap, c + 1)
                    rope(dve, chain, t_cos, t_sin, q_dec[:], P, stage[:, 0:4, :])
                    assert chain.n == STEPS
                    dve.wait_ge(pe_scores, c + 1)
                    masks(dve, dmask[:], k_dec[:], P)
                    dve.wait_ge(pe_out, c + 1)
                    dve.wait_ge(state_ok, c + 1)
                    new_state(state, state, dec_c, state_ok)
                chain = Chain(steps, NCH * STEPS)
                dve.wait_ge(pe_swap, NCH + 1)
                rope(dve, chain, cos[:, TP:T], sin[:, TP:T], q_dec_s[:], TS, g.br[:, 4:8, TP:T])
                dve.wait_ge(pe_scores, NCH + 1)
                masks(dve, dmask_s[:], k_dec_s[:], TS)
                dve.wait_ge(masked, NCH + 1)
                with dve.Fori(0, NSEQ) as b:
                    cols = seq_cols[:, ds(b, 1), :].broadcast_to([P, 4, TS])
                    row = seq_rows[:, ds(b, 1)]
                    nc.vector.tensor_tensor(qdm[:].rearrange("p s a t -> p (s a) t"),
                                            qd[:].rearrange("p s a t -> p (s a) t")[:, :, 0:TS], cols, ALU.mult)
                    nc.vector.tensor_scalar(kdm[:], kd[0:TS, :], row, None, ALU.mult).then_inc(s_masked, 1)
                    dve.wait_ge(s_pe, b + 1)
                    dve.wait_ge(s_stored, b * 32 + 16)
                    new_state(s1, s0, dec_s, s_new)


def phase_head_norm(g):
    nc = g.nc
    with ExitStack() as ctx:
        mean_w, eps = g.sb(ctx, "hn_mean_w", [P, P]), g.sb(ctx, "hn_eps", [P, 1])
        sq = [g.sb(ctx, f"hn_sq{s}", [P, TW]) for s in range(2)]
        std = [g.sb(ctx, f"hn_std{s}", [P, TW]) for s in range(2)]
        mean = g.ps(ctx, "hn_mean", [P, NB, 512])
        var = g.ps(ctx, "hn_var", [P, NB, 512])
        ready, mean_ok, centred, squared = g.sem("hn_ready"), g.sem("hn_mean_ok"), g.sem("hn_centred"), g.sem("hn_squared")
        var_ok, std_ok, steps = g.sem("hn_var_ok"), g.sem("hn_std_ok"), g.sem("hn_steps")
        with nc.Block() as block:
            @block.gpsimd
            def _(pool):
                nc.gpsimd.memset(mean_w[:], 1.0 / P).then_inc(ready, 1)
                nc.gpsimd.memset(eps[:], EPS).then_inc(ready, 1)

            @block.tensor
            def _(pe):
                pe.wait_ge(ready, 2)
                for h in range(H_R + 1):
                    if h < H_R:
                        if h > 0:
                            pe.wait_ge(centred, h)
                        for b in range(NB):
                            mm = nc.tensor.matmul(mean[:, b, 0:TB], mean_w[:], g.br[:, 8 + h, b * TB:(b + 1) * TB],
                                                  start=True, stop=True)
                        mm.then_inc(mean_ok, 1)
                    if h > 0:
                        pe.wait_ge(squared, h)
                        if h > 1:
                            pe.wait_ge(std_ok, h - 1)
                        for b in range(NB):
                            mm = nc.tensor.matmul(var[:, b, 0:TB], mean_w[:], sq[(h - 1) % 2][:, b * TB:(b + 1) * TB],
                                                  start=True, stop=True)
                        mm.then_inc(var_ok, 1)

            @block.scalar
            def _(act):
                act.wait_ge(ready, 2)
                for h in range(H_R):
                    act.wait_ge(centred, h + 1)
                    if h >= 2:
                        act.wait_ge(var_ok, h - 1)
                    nc.scalar.activation(sq[h % 2][:], g.br[:, 8 + h, :], ACT.Square).then_inc(squared, 1)
                    act.wait_ge(var_ok, h + 1)
                    if h >= 2:
                        act.wait_ge(steps, 3 * (h - 1))
                    nc.scalar.activation(blocks_of(std[h % 2][:]), var[:, :, 0:TB], ACT.Sqrt, bias=eps[:])\
                        .then_inc(std_ok, 1)

            @block.vector
            def _(dve):
                chain = Chain(steps)
                for h in range(H_R + 1):
                    if h < H_R:
                        row = blocks_of(g.br[:, 8 + h, :])
                        dve.wait_ge(mean_ok, h + 1)
                        nc.vector.tensor_tensor(row, row, mean[:, :, 0:TB], ALU.subtract).then_inc(centred, 1)
                    if h > 0:
                        s, x, y = std[(h - 1) % 2], g.br[:, 7 + h, :], g.br[:, h - 1, :]
                        dve.wait_ge(std_ok, h)
                        chain.mark(nc.vector.reciprocal(s[:], s[:]))
                        chain.wait(dve)
                        chain.mark(nc.vector.tensor_tensor(x, x, s[:], ALU.mult))
                        chain.wait(dve)
                        chain.mark(nc.vector.scalar_tensor_tensor(y, x, g.gn_g[:, h - 1:h], y, ALU.mult, ALU.mult))


def phase_attention_in(g):
    nc, io, w = g.nc, g.io, g.w
    fox, mq = 6, 2
    pairs = fox + mq
    with ExitStack() as ctx:
        w.open(ctx, "att")
        ga = g.sb(ctx, "ga", [H_F, TW])
        gb = g.negc
        lf = g.sb(ctx, "lf", [H_F, TW])
        acc = [g.ps(ctx, f"a_acc{s}", [P, NB, 512]) for s in range(2)]
        lfn_ps = g.ps(ctx, "lfn_ps", [P, NCH + 1, H_F])
        free = [g.sem(f"a_free{s}") for s in range(2)]
        steps, a_steps = g.sem("a_dve_steps"), g.sem("a_act_steps")
        turned, nat, stored, scanned = (g.sem(n) for n in ("lf_turned", "lf_nat", "lf_stored", "lf_scanned"))
        b0, b1 = w.n
        with nc.Block() as block:
            @block.sync
            def _(sp):
                for s in range(2):
                    sp.sem_inc(free[s], 1)
                w.load(sp, 0, b0, io["w_in"][:, C_FL:C_FL + P], KD)
                w.load(sp, 1, b1, io["w_in"][:, C_FQ:C_FQ + P], KD)
                with sp.Fori(1, 2 * fox // 2) as n:
                    w.load(sp, 0, n + b0, io["w_in"][:, ds(n * (2 * P) + (C_FQ - P), P)], KD)
                    w.load(sp, 1, n + b1, io["w_in"][:, ds(n * (2 * P) + C_FQ, P)], KD)
                w.load(sp, 0, fox + b0, io["w_in"][:, C_FQ + (2 * fox - 1) * P:C_FQ + 2 * fox * P], KD)
                w.load(sp, 1, fox + b1, io["w_in"][:, C_MQ:C_MQ + P], KD)
                with sp.Fori(1, mq) as n:
                    w.load(sp, 0, n + (fox + b0), io["w_in"][:, ds(n * (2 * P) + (C_MQ - P), P)], KD)
                    w.load(sp, 1, n + (fox + b1), io["w_in"][:, ds(n * (2 * P) + C_MQ, P)], KD)
                w.load(sp, 0, fox + mq + b0, io["w_in"][:, C_MQ + 3 * P:C_MQ + 4 * P], KD)
                sp.wait_ge(nat, 1)
                sp.dma_start(io["fox_logf_prompt"][0].rearrange("(c p) h -> p c h", p=P), g.lfn[:, 0:NCH, :],
                             allow_slow_non_contiguous=True).then_inc(stored, 16)
                sp.dma_start(io["fox_logf_sample"].rearrange("b t h -> (b t) h"), g.lfn[0:TS, NCH, :])\
                    .then_inc(stored, 16)
                sp.wait_ge(stored, 32)

            @block.gpsimd
            def _(pool):
                with pool.Fori(0, pairs) as n:
                    for s in range(2):
                        w.split(pool, s, n + (b0, b1)[s], KD)
                w.split(pool, 0, pairs + b0, KD)

            @block.tensor
            def _(pe):
                with pe.Fori(0, pairs) as n:
                    for s in range(2):
                        pe.wait_ge(free[s], n + 1)
                        w.products(pe, s, n + (b0, b1)[s], KD, acc[s], g.xh, g.xl)
                pe.wait_ge(free[0], pairs + 1)
                w.products(pe, 0, pairs + b0, KD, acc[0], g.xh, g.xl)
                pe.wait_ge(scanned, 1)
                for c in range(NCH + 1):
                    n = P if c < NCH else TS
                    mm = nc.tensor.transpose(lfn_ps[0:n, c, :], lf[:, c * P:c * P + n], g.ident[0:H_F, 0:H_F])
                mm.then_inc(turned, 1)

            @block.scalar
            def _(act):
                act.wait_ge(free[0], 2)
                chain = Chain(a_steps)
                chain.mark(nc.scalar.activation(gb[:], ga[:], ACT.Abs))
                chain.wait(act)
                chain.mark(nc.scalar.activation(gb[:], gb[:], ACT.Exp, scale=-1.0))
                chain.wait(act)
                chain.mark(nc.scalar.activation(gb[:], gb[:], ACT.Ln, bias=1.0))

                def read(n, dst, scale):
                    act.wait_ge(w.done[0], n + (b0 + 2))
                    nc.scalar.mul(dst, acc[0][:, :, 0:TB], scale).then_inc(free[0], 1)
                for n in range(1, 3):
                    read(n, blocks_of(g.br[:, 8 + 2 * n - 1, :]), DF ** -0.5)
                with act.Fori(3, 7) as n:
                    read(n, blocks_of(g.fkv[:, n * 2 - 5, :]), 1.0)
                for n in range(7, 9):
                    read(n, blocks_of(g.br[:, 4 + 2 * (n - fox) - 1, :]), 1.0)

            @block.vector
            def _(dve):
                chain = Chain(steps)
                dve.wait_ge(w.done[0], b0 + 2)
                nc.vector.tensor_scalar(blocks_of(ga[:]), acc[0][0:H_F, :, 0:TB], g.b_forget[:], None, ALU.add)\
                    .then_inc(free[0], 1)

                def read(n, dst, scale):
                    dve.wait_ge(w.done[1], n + (b1 + 2))
                    nc.vector.tensor_scalar(dst, acc[1][:, :, 0:TB], scale, None, ALU.mult).then_inc(free[1], 1)
                for n in range(2):
                    read(n, blocks_of(g.br[:, 8 + 2 * n, :]), DF ** -0.5)
                dve.wait_ge(a_steps, 3)
                chain.mark(nc.vector.scalar_tensor_tensor(lf[:], ga[:], 0.0, gb[:], ALU.min, ALU.subtract))
                chain.wait(dve)
                chain.mark(nc.vector.memset(ga[:], 1.0))
                chain.wait(dve)
                nc.vector.tensor_tensor_scan(gb[:, 0:TP], ga[:, 0:TP], lf[:, 0:TP], 0.0, ALU.mult, ALU.subtract)\
                    .then_inc(scanned, 1)
                with dve.Fori(2, 6) as n:
                    read(n, blocks_of(g.fkv[:, n * 2 - 4, :]), 1.0)
                for n in range(6, 8):
                    read(n, blocks_of(g.br[:, 4 + 2 * (n - fox), :]), 1.0)
                dve.wait_ge(turned, 1)
                nc.vector.tensor_copy(g.lfn[:, 0:NCH, :], lfn_ps[:, 0:NCH, :])
                nc.vector.tensor_copy(g.lfn[0:TS, NCH, :], lfn_ps[0:TS, NCH, :]).then_inc(nat, 1)
        w.n = [b0 + pairs + 1, b1 + pairs]


def phase_kv_natural(g):
    nc, io = g.nc, g.io
    with ExitStack() as ctx:
        stage = g.sb(ctx, "kv_stage", [P, 8, P])
        kn, vn = g.sb(ctx, "kv_kn", [P, 4, P]), g.sb(ctx, "kv_vn", [P, 4, P])
        kt, vt = g.ps(ctx, "kv_kt", [P, 4, P]), g.ps(ctx, "kv_vt", [P, 4, P])
        staged, turned, k_ok, v_ok = g.sem("kv_staged"), g.sem("kv_turned"), g.sem("kv_k_ok"), g.sem("kv_v_ok")
        k_out, v_out, placed = g.sem("kv_k_out"), g.sem("kv_v_out"), g.sem("kv_placed")
        with nc.Block() as block:
            @block.gpsimd
            def _(pool):
                nc.gpsimd.tensor_copy(g.k_s[:], g.fkv[:, 0:4, TP:T])
                with pool.Fori(0, NCH) as c:
                    src = g.fkv[:, :, ds(c * P, P)]
                    dst = g.fkv[:, 4:8, ds(c * P, P)]
                    pool.wait_ge(turned, c + 1)
                    pool.sem_inc(g.w.passed, 1)
                    nc.gpsimd.tensor_copy(stage[:], src).then_inc(staged, 1)
                    pool.wait_ge(v_ok, c + 2)
                    pool.sem_inc(g.w.passed, 1)
                    nc.gpsimd.tensor_copy(dst, vn[:]).then_inc(placed, 1)

            @block.tensor
            def _(pe):
                def turn(n, k_of, v_of):
                    for j in range(4):
                        nc.tensor.transpose(kt[0:n, j, :], k_of(j), g.ident[:])
                    for j in range(4):
                        mm = nc.tensor.transpose(vt[0:n, j, :], v_of(j), g.ident[:])
                    mm.then_inc(turned, 1)
                with pe.Fori(0, NCH) as c:
                    pe.wait_ge(staged, c + 1)
                    pe.wait_ge(k_ok, c + 1)
                    pe.wait_ge(v_ok, c + 1)
                    turn(P, lambda j: stage[:, j, :], lambda j: stage[:, 4 + j, :])
                pe.wait_ge(k_ok, NCH + 1)
                pe.wait_ge(v_ok, NCH + 1)
                turn(TS, lambda j: g.fkv[:, j, TP:T], lambda j: g.fkv[:, 4 + j, TP:T])

            @block.scalar
            def _(act):
                with act.Fori(0, NCH) as c:
                    act.wait_ge(turned, c + 2)
                    act.wait_ge(k_out, c * 16 + 16)
                    nc.scalar.copy(kn[:], kt[:]).then_inc(k_ok, 1)
                act.wait_ge(turned, NCH + 2)
                act.wait_ge(k_out, NCH * 16 + 16)
                nc.scalar.copy(kn[0:TS], kt[0:TS]).then_inc(k_ok, 1)

            @block.vector
            def _(dve):
                with dve.Fori(0, NCH) as c:
                    dve.wait_ge(turned, c + 2)
                    dve.wait_ge(v_out, c * 16 + 16)
                    dve.wait_ge(placed, c + 1)
                    nc.vector.tensor_copy(vn[:], vt[:]).then_inc(v_ok, 1)
                dve.wait_ge(turned, NCH + 2)
                nc.vector.tensor_copy(g.v_s[:], vt[0:TS].rearrange("p a b -> p (a b)")).then_inc(v_ok, 1)

            @block.sync
            def _(sp):
                for sem in (turned, k_ok, v_ok, placed):
                    sp.sem_inc(sem, 1)
                sp.sem_inc(k_out, 16)
                sp.sem_inc(v_out, 16)
                with sp.Fori(0, NCH) as c:
                    k_dst = io["fox_k_prompt"][0, ds(c * P, P)].rearrange("t h d -> t (h d)")
                    v_dst = io["fox_v_prompt"][0, ds(c * P, P)].rearrange("t h d -> t (h d)")
                    sp.wait_ge(k_ok, c + 2)
                    sp.dma_start(k_dst, kn[:].rearrange("p a b -> p (a b)")).then_inc(k_out, 16)
                    sp.wait_ge(v_ok, c + 2)
                    sp.dma_start(v_dst, vn[:].rearrange("p a b -> p (a b)")).then_inc(v_out, 16)
                sp.wait_ge(k_ok, NCH + 2)
                sp.dma_start(io["fox_k_sample"].rearrange("b t h d -> (b t) (h d)"),
                             kn[0:TS].rearrange("p a b -> p (a b)")).then_inc(k_out, 16)
                sp.wait_ge(v_ok, NCH + 2)
                sp.dma_start(io["fox_v_sample"].rearrange("b t h d -> (b t) (h d)"), g.v_s[:]).then_inc(v_out, 16)
                sp.wait_ge(k_out, 16 * (NCH + 2))
                sp.wait_ge(v_out, 16 * (NCH + 2))


def phase_cross(g):
    nc, io = g.nc, g.io
    MT = N_MEM // P
    scale = DM ** -0.5
    STEPS = 3
    with ExitStack() as ctx:
        q = g.sb(ctx, "c_q", [P, H_M, P])
        prob, pt = g.sb(ctx, "c_prob", [P, H_M, N_MEM]), g.sb(ctx, "c_pt", [P, H_M * MT, P])
        nmax, ssum, rsum = g.sb(ctx, "c_nmax", [P, H_M]), g.sb(ctx, "c_ssum", [P, H_M]), g.sb(ctx, "c_rsum", [P, H_M])
        kin, vin = g.sb(ctx, "c_kin", [P, MT, H_M * DM]), g.sb(ctx, "c_vin", [P, MT, H_M * DM])
        kts = g.sb(ctx, "c_kts", [P, H_M, N_MEM])
        sc = g.ps(ctx, "c_sc", [P, H_M, N_MEM])
        ptp = g.ps(ctx, "c_ptp", [P, H_M * MT, P])
        o = g.ps(ctx, "c_o", [P, H_M, P])
        ktp = g.ps(ctx, "c_ktp", [P, H_M, N_MEM])
        staged, scored, maxed, exped = g.sem("c_staged"), g.sem("c_scored"), g.sem("c_maxed"), g.sem("c_exped")
        normed, turned, pt_ok, out_ok = g.sem("c_normed"), g.sem("c_turned"), g.sem("c_pt_ok"), g.sem("c_out_ok")
        o_read, steps = g.sem("c_o_read"), g.sem("c_steps")
        loaded, k_turned, k_ok = g.sem("c_loaded"), g.sem("c_k_turned"), g.sem("c_k_ok")

        def block_pe(pe, i, n, kt, v):
            pe.wait_ge(staged, i + 1)
            for h in range(H_M):
                mm = nc.tensor.matmul(sc[0:n, h, :], q[:, h, 0:n], kt[:, h, :], start=True, stop=True)
            mm.then_inc(scored, 1)
            pe.wait_ge(normed, i + 1)
            pe.sem_inc(g.w.passed, 1)
            for h in range(H_M):
                for m in range(MT):
                    mm = nc.tensor.transpose(ptp[:, h * MT + m, 0:n], prob[0:n, h, m * P:(m + 1) * P],
                                             g.ident[0:n, 0:n])
            mm.then_inc(turned, 1)
            pe.wait_ge(pt_ok, i + 1)
            pe.wait_ge(o_read, i + 1)
            for h in range(H_M):
                for m in range(MT):
                    mm = nc.tensor.matmul(o[:, h, 0:n], v[:, m, h * DM:(h + 1) * DM], pt[:, h * MT + m, 0:n],
                                          start=(m == 0), stop=(m == MT - 1))
            mm.then_inc(out_ok, 1)

        def block_dve(dve, i, n):
            dve.wait_ge(scored, i + 1)
            chain = Chain(steps, i * STEPS)
            chain.mark(nc.vector.tensor_reduce(nmax[0:n], sc[0:n], AX.X, ALU.max))
            chain.wait(dve)
            nc.vector.tensor_scalar(nmax[0:n], nmax[0:n], -scale, None, ALU.mult).then_inc(maxed, 1)
            dve.wait_ge(exped, i + 1)
            chain.mark(nc.vector.reciprocal(rsum[0:n], ssum[0:n]))
            chain.wait(dve)
            nc.vector.tensor_tensor(prob[0:n], prob[0:n], rsum[0:n].unsqueeze(2).broadcast_to([n, H_M, N_MEM]),
                                    ALU.mult).then_inc(normed, 1)
            dve.wait_ge(turned, i + 1)
            chain.mark(nc.vector.tensor_copy(pt[:, :, 0:n], ptp[:, :, 0:n]))
            assert chain.n == STEPS
            chain.wait(dve)
            dve.sem_inc(pt_ok, 1)

        def block_act(act, i, n, dst):
            act.wait_ge(maxed, i + 1)
            for h in range(H_M):
                ins = nc.scalar.activation(prob[0:n, h, :], sc[0:n, h, :], ACT.Exp, bias=nmax[0:n, h:h + 1],
                                           scale=scale, accum_out=ssum[0:n, h:h + 1])
            ins.then_inc(exped, 1)
            act.wait_ge(out_ok, i + 1)
            nc.scalar.copy(dst, o[:, :, 0:n]).then_inc(o_read, 1)

        with nc.Block() as block:
            @block.sync
            def _(sp):
                sp.sem_inc(o_read, 1)
                sp.sem_inc(k_ok, 1)
                with sp.Fori(0, NSEQ) as b:
                    ks = io["cache_mem_k"][b].rearrange("(m p) h d -> p m (h d)", p=P)
                    vs = io["cache_mem_v"][b].rearrange("(m p) h d -> p m (h d)", p=P)
                    sp.wait_ge(k_ok, b + 1)
                    sp.dma_start(kin[:], ks).then_inc(loaded, 16)
                    sp.wait_ge(o_read, b + (NCH + 1))
                    sp.dma_start(vin[:], vs).then_inc(loaded, 16)

            @block.gpsimd
            def _(pool):
                with pool.Fori(0, NCH) as i:
                    src = g.br[:, 4:8, ds(i * P, P)]
                    pool.wait_ge(o_read, i + 1)
                    pool.sem_inc(g.w.passed, 1)
                    nc.gpsimd.tensor_copy(q[:], src).then_inc(staged, 1)
                with pool.Fori(0, NSEQ) as b:
                    src = g.br[:, 4:8, ds(b * LSEQ + TP, LSEQ)]
                    pool.wait_ge(o_read, b + (NCH + 1))
                    pool.sem_inc(g.w.passed, 1)
                    nc.gpsimd.tensor_copy(q[:, :, 0:LSEQ], src).then_inc(staged, 1)

            @block.tensor
            def _(pe):
                with pe.Fori(0, NCH) as i:
                    block_pe(pe, i, P, g.mem_kt, g.mem_v)
                with pe.Fori(0, NSEQ) as b:
                    pe.wait_ge(loaded, b * 32 + 32)
                    for h in range(H_M):
                        for m in range(MT):
                            mm = nc.tensor.transpose(ktp[:, h, m * P:(m + 1) * P], kin[:, m, h * DM:(h + 1) * DM],
                                                     g.ident[:])
                    mm.then_inc(k_turned, 1)
                    pe.wait_ge(k_ok, b + 2)
                    block_pe(pe, b + NCH, LSEQ, kts, vin)

            @block.scalar
            def _(act):
                act.preload_act_table(ACT.Exp)
                with act.Fori(0, NCH) as i:
                    block_act(act, i, P, g.br[:, 4:8, ds(i * P, P)])
                with act.Fori(0, NSEQ) as b:
                    dst = g.br[:, 4:8, ds(b * LSEQ + TP, LSEQ)]
                    act.wait_ge(k_turned, b + 1)
                    nc.scalar.copy(kts[:], ktp[:]).then_inc(k_ok, 1)
                    block_act(act, b + NCH, LSEQ, dst)

            @block.vector
            def _(dve):
                with dve.Fori(0, NCH) as i:
                    block_dve(dve, i, P)
                with dve.Fori(0, NSEQ) as b:
                    block_dve(dve, b + NCH, LSEQ)


def phase_fox_prompt(g):
    nc = g.nc
    with ExitStack() as ctx:
        qz = g.sb(ctx, "p_qz", [P, 2, P])
        prob = [g.sb(ctx, f"p_prob{s}", [P, TP]) for s in range(2)]
        pt = [g.sb(ctx, f"p_pt{s}", [P, NCH, P]) for s in range(2)]
        nmax, ssum, rsum = (g.sb(ctx, "p_" + n, [P, 2]) for n in ("nmax", "ssum", "rsum"))
        on = g.sb(ctx, "p_on", [P, 2, DF])
        row = g.sb(ctx, "p_row", [2, 2, P])
        negc = g.sb(ctx, "p_negc", [2, PAIRS, TP])
        sc = [g.ps(ctx, f"p_sc{s}", [P, TP]) for s in range(2)]
        ptp = g.ps(ctx, "p_ptp", [P, NCH, P])
        o = g.ps(ctx, "p_o", [P, 2, DF])
        ot = g.ps(ctx, "p_ot", [P, P])
        const, zero, staged = g.sem("p_const"), g.sem("p_zero"), g.sem("p_staged")
        scored = [g.sem(f"p_scored{s}") for s in range(2)]
        maxed = [g.sem(f"p_maxed{s}") for s in range(2)]
        exped = [g.sem(f"p_exped{s}") for s in range(2)]
        turned, pt_ok, pv_ok = g.sem("p_turned"), g.sem("p_pt_ok"), g.sem("p_pv_ok")
        recip, on_ok, ot_ok, placed = g.sem("p_recip"), g.sem("p_on_ok"), g.sem("p_ot_ok"), g.sem("p_placed")
        with nc.Block() as block:
            @block.sync
            def _(sp):
                sp.dma_start(row[:], g.io["pair_row"]).then_inc(const, 16)
                for s in range(2):
                    sp.dma_start(negc[s:s + 1, :, :], g.negc[s:H_F:2, 0:TP]).then_inc(const, 16)
                    sp.sem_inc(exped[s], 1)
                for sem in (scored[1], pt_ok, placed, on_ok, ot_ok):
                    sp.sem_inc(sem, 1)
                sp.sem_inc(turned, 2)
                sp.sem_inc(recip, 2)
                sp.wait_ge(const, 48)

            @block.gpsimd
            def _(pool):
                nc.gpsimd.memset(qz[:], 0.0).then_inc(zero, 1)
                pool.wait_ge(zero, 1)
                for i in range(NCH):
                    with pool.Fori(0, PAIRS) as p:
                        src = [g.br[HALVES[s], p + 8, i * P:(i + 1) * P] for s in range(2)]
                        t = i * PAIRS
                        pool.wait_ge(scored[1], p + (t + 1))
                        pool.sem_inc(g.w.passed, 1)
                        for s in range(2):
                            ins = nc.gpsimd.tensor_copy(qz[HALVES[s], s, :], src[s])
                        ins.then_inc(staged, 1)

            @block.tensor
            def _(pe):
                pe.wait_ge(const, 48)
                for i in range(NCH):
                    keys = (i + 1) * P
                    with pe.Fori(0, PAIRS) as p:
                        t = i * PAIRS
                        pe.wait_ge(staged, p + (t + 1))
                        for s in range(2):
                            pe.wait_ge(exped[s], p + (t + 1))
                            for k0 in range(0, keys, 512):
                                k1 = min(k0 + 512, keys)
                                nc.tensor.matmul(sc[s][:, k0:k1], qz[:, s, :], g.fkv[:, p, k0:k1],
                                                 start=True, stop=False)
                                mm = nc.tensor.matmul(sc[s][:, k0:k1], row[:, s, :], negc[:, p, k0:k1],
                                                      start=False, stop=(k1 < keys))
                            mm = nc.tensor.matmul(sc[s][:, i * P:keys], g.ident[:], g.causal[:],
                                                  start=False, stop=True)
                            mm.then_inc(scored[s], 1)
                        for s in range(2):
                            n = (p + t) * 2 + s
                            pe.wait_ge(exped[s], p + (t + 2))
                            pe.wait_ge(pt_ok, n + 1)
                            for k in range(i + 1):
                                mm = nc.tensor.transpose(ptp[:, k, :], prob[s][:, k * P:(k + 1) * P], g.ident[:])
                            mm.then_inc(turned, 1)
                            pe.wait_ge(pt_ok, n + 2)
                            if s == 0:
                                pe.wait_ge(on_ok, p + (t + 1))
                            for k in range(i + 1):
                                v = g.fkv[:, p + 4, k * P + s * DF:k * P + (s + 1) * DF]
                                mm = nc.tensor.matmul(o[:, s, :], pt[s][:, k, :], v, start=(k == 0), stop=(k == i))
                            mm.then_inc(pv_ok, 1)
                        pe.wait_ge(on_ok, p + (t + 2))
                        pe.wait_ge(placed, p + (t + 1))
                        nc.tensor.transpose(ot[:], on[:].rearrange("p a b -> p (a b)"), g.ident[:]).then_inc(ot_ok, 1)

            @block.scalar
            def _(act):
                act.preload_act_table(ACT.Exp)
                for i in range(NCH):
                    keys = (i + 1) * P
                    with act.Fori(0, PAIRS) as p:
                        t = i * PAIRS
                        dst = g.br[:, p + 8, i * P:keys]
                        for s in range(2):
                            act.wait_ge(maxed[s], p + (t + 1))
                            act.wait_ge(turned, (p + t) * 2 + (s + 1))
                            act.wait_ge(recip, (p + t) * 2 + (s + 1))
                            nc.scalar.activation(prob[s][:, 0:keys], sc[s][:, 0:keys], ACT.Exp, bias=nmax[:, s:s + 1],
                                                 accum_out=ssum[:, s:s + 1]).then_inc(exped[s], 1)
                        act.wait_ge(ot_ok, p + (t + 2))
                        nc.scalar.copy(dst, ot[:]).then_inc(placed, 1)

            @block.vector
            def _(dve):
                for i in range(NCH):
                    keys = (i + 1) * P
                    with dve.Fori(0, PAIRS) as p:
                        t = i * PAIRS
                        for s in range(2):
                            dve.wait_ge(scored[s], p + (t + (2 if s else 1)))
                            dve.wait_ge(exped[s], p + (t + 1))
                            nc.vector.tensor_reduce(nmax[:, s:s + 1], sc[s][:, 0:keys], AX.X, ALU.max, negate=True)\
                                .then_inc(maxed[s], 1)
                        for s in range(2):
                            n = (p + t) * 2 + s
                            dve.wait_ge(exped[s], p + (t + 2))
                            nc.vector.reciprocal(rsum[:, s:s + 1], ssum[:, s:s + 1]).then_inc(recip, 1)
                            dve.wait_ge(turned, n + 3)
                            nc.vector.tensor_copy(pt[s][:, 0:i + 1, :], ptp[:, 0:i + 1, :]).then_inc(pt_ok, 1)
                        dve.wait_ge(recip, (p + t) * 2 + 4)
                        dve.wait_ge(ot_ok, p + (t + 1))
                        dve.wait_ge(pv_ok, (p + t) * 2 + 2)
                        nc.vector.tensor_tensor(on[:], o[:], rsum[:].unsqueeze(2).broadcast_to([P, 2, DF]), ALU.mult)\
                            .then_inc(on_ok, 1)


def phase_fox_sample(g):
    nc, io = g.nc, g.io
    HQ = H_F * LSEQ
    SLOTS = NPG + 1
    with ExitStack() as ctx:
        suf = g.sb(ctx, "d_suf", [P, NSEQ * NPG, H_F])
        qb = g.sb(ctx, "d_qb", [P, NSEQ, PAIRS, 2 * LSEQ])
        bias_n = g.sb(ctx, "d_bias_n", [TS, NSEQ, H_F, LSEQ])
        with ExitStack() as pre:
            lft = g.lft
            tot = [g.sb(pre, f"d_tot{s}", [P, NSEQ, NPG, H_F]) for s in range(2)]
            after, upto = g.sb(pre, "d_after", [P, P]), g.sb(pre, "d_upto", [TS, TS])
            new_mask, cn = g.sb(pre, "d_new_mask", [TS, NSEQ, LSEQ]), g.sb(pre, "d_cn", [TS, H_F])
            a = g.ps(pre, "d_a", [P, 4, 512])
            b_ = g.ps(pre, "d_b", [P, 4, 512])
            const, totals = g.sem("d_const"), g.sem("d_totals")
            within, steps, tot_read, cn_ok, qb_steps = g.sem("d_within"), g.sem("d_steps"), g.sem("d_tot_read"), g.sem("d_cn_ok"), g.sem("d_qb")
            with nc.Block() as block:
                @block.sync
                def _(sp):
                    for name, dst in (("after", after), ("upto", upto), ("new_mask", new_mask)):
                        sp.dma_start(dst[:], io[name]).then_inc(const, 16)
                    sp.wait_ge(const, 48)

                @block.tensor
                def _(pe):
                    pe.wait_ge(const, 48)
                    cols = lft[:].rearrange("p g h -> p (g h)")
                    for j in range(4):
                        mm = nc.tensor.matmul(b_[:, j, :], g.ones[:], cols[:, j * 512:(j + 1) * 512], start=True, stop=True)
                    mm.then_inc(totals, 1)
                    for j in range(4):
                        mm = nc.tensor.matmul(a[:, j, :], after[:], cols[:, j * 512:(j + 1) * 512], start=True, stop=True)
                    mm.then_inc(within, 1)
                    pe.wait_ge(tot_read, 1)
                    nc.tensor.matmul(b_[0:TS, 0, 0:H_F], upto[:], g.lfn[0:TS, NCH, :], start=True, stop=True)\
                        .then_inc(cn_ok, 1)

                @block.gpsimd
                def _(pool):
                    nc.gpsimd.memset(qb[:], 0.0).then_inc(qb_steps, 1)
                    pool.wait_ge(qb_steps, 1)
                    q = g.br[:, 8:12, TP:T].rearrange("p a (b q) -> p b a q", q=LSEQ)
                    for b in range(NSEQ):
                        for s in range(2):
                            nc.gpsimd.tensor_copy(qb[HALVES[s], b, :, s * LSEQ:(s + 1) * LSEQ], q[HALVES[s], b])

                @block.vector
                def _(dve):
                    chain = Chain(steps)
                    dve.wait_ge(totals, 1)
                    flat = tot[0][:].rearrange("p b g h -> p (b g h)")
                    nc.vector.tensor_copy(flat.rearrange("p (j c) -> p j c", j=4), b_[:]).then_inc(tot_read, 1)
                    dve.wait_ge(tot_read, 1)
                    now, step = 0, 1
                    while step < NPG:
                        x, y = tot[now], tot[1 - now]
                        nc.vector.tensor_tensor(y[:, :, 0:NPG - step, :].rearrange("p b g h -> p b (g h)"),
                                                x[:, :, 0:NPG - step, :].rearrange("p b g h -> p b (g h)"),
                                                x[:, :, step:NPG, :].rearrange("p b g h -> p b (g h)"), ALU.add)
                        chain.mark(nc.vector.tensor_copy(y[:, :, NPG - step:NPG, :], x[:, :, NPG - step:NPG, :]))
                        chain.wait(dve)
                        now, step = 1 - now, step * 2
                    dve.wait_ge(within, 1)
                    chain.mark(nc.vector.tensor_copy(suf[:].rearrange("p g h -> p (g h)").rearrange("p (j c) -> p j c", j=4), a[:]))
                    chain.wait(dve)
                    s4 = suf[:].rearrange("p (b g) h -> p b (g h)", b=NSEQ)
                    chain.mark(nc.vector.tensor_tensor(
                        s4[:, :, 0:(NPG - 1) * H_F], s4[:, :, 0:(NPG - 1) * H_F],
                        tot[now][:, :, 1:NPG, :].rearrange("p b g h -> p b (g h)"), ALU.add))
                    dve.wait_ge(cn_ok, 1)
                    chain.mark(nc.vector.tensor_copy(cn[:], b_[0:TS, 0, 0:H_F]))
                    chain.wait(dve)
                    for b in range(NSEQ):
                        nc.vector.tensor_tensor(bias_n[:, b], new_mask[:, b, :].unsqueeze(1).broadcast_to([TS, H_F, LSEQ]),
                                                cn[:].unsqueeze(2).broadcast_to([TS, H_F, LSEQ]), ALU.subtract)

        st = g.sb(ctx, "d_st", [P, SLOTS, HQ])
        ring = [g.sb(ctx, f"d_page{s}", [P, H_F * DF]) for s in range(RING)]
        kt = [g.sb(ctx, f"d_kt{s}", [P, PAIRS, P]) for s in range(2)]
        m1, rs1, rd = g.sb(ctx, "d_m1", [P, HQ]), g.sb(ctx, "d_rs1", [P, HQ]), g.sb(ctx, "d_rd", [P, HQ])
        mx, dg = g.sb(ctx, "d_mx", [HQ, 1]), g.sb(ctx, "d_dg", [HQ, HQ])
        ktp = [g.ps(ctx, f"d_ktp{s}", [P, PAIRS, P]) for s in range(2)]
        stp = [g.ps(ctx, f"d_stp{s}", [P, 8, HQ]) for s in range(2)]
        stn = g.ps(ctx, "d_stn", [P, 512])
        mp = g.ps(ctx, "d_mp", [P, 512])
        ov = g.ps(ctx, "d_ov", [P, PAIRS, 2 * LSEQ])
        loaded = [g.sem(f"d_loaded{s}") for s in range(RING)]
        used = g.sem("d_used")
        k_turned, kt_ok = g.sem("d_k_turned"), g.sem("d_kt_ok")
        st8 = g.sem("d_st8")
        new_sc, new_st, m_ok, mt_ok, dg_ok, mb_ok = (g.sem("d_" + n) for n in ("new_sc", "new_st", "m_ok", "mt_ok", "dg_ok", "mb_ok"))
        sub_ok, exp_ok, rs_ok, den_ok, ov_ok, out_ok = (g.sem("d_" + n) for n in ("sub_ok", "exp_ok", "rs_ok", "den_ok", "ov_ok", "out_ok"))
        steps2, blank = g.sem("d_steps2"), g.sem("d_blank")
        GR = NPG // RING
        with nc.Block() as block:
            @block.sync
            def _(sp):
                sp.sem_inc(used, RING)
                sp.sem_inc(kt_ok, 2)
                sp.sem_inc(st8, 2)
                sp.sem_inc(out_ok, 1)
                with sp.Fori(0, NSEQ) as b:
                    for v, cache in enumerate((io["cache_fox_k"], io["cache_fox_v"])):
                        with sp.Fori(0, GR) as r:
                            for s in range(RING):
                                page = sp.value_load(g.pages[0:1, ds(b * NPG + r * RING + s, 1)], min_val=0,
                                                     max_val=cache.shape[0] - 1)
                                src = cache[page].rearrange("t h d -> t (h d)")
                                sp.wait_ge(used, b * (2 * NPG) + r * RING + (v * NPG + s + 1))
                                sp.dma_start(ring[s][:], src).then_inc(loaded[s], 16)

            @block.tensor
            def _(pe):
                with pe.Fori(0, NSEQ) as b:
                    with pe.Fori(0, GR) as r:
                        def turn(s):
                            n = b * NPG + r * RING + s
                            pe.wait_ge(loaded[s], (b * (2 * GR) + r) * 16 + 16)
                            pe.wait_ge(kt_ok, n + 1)
                            for p in range(PAIRS):
                                mm = nc.tensor.transpose(ktp[s % 2][:, p, :], ring[s][:, p * P:(p + 1) * P], g.ident[:])
                            mm.then_inc(k_turned, 1)
                        turn(0)
                        for s in range(RING):
                            if s + 1 < RING:
                                turn(s + 1)
                            n = b * NPG + r * RING + s
                            if s % 8 == 0:
                                pe.wait_ge(st8, b * (NPG // 8) + r * (RING // 8) + (s // 8 + 1))
                            pe.wait_ge(kt_ok, n + 3)
                            for p in range(PAIRS):
                                mm = nc.tensor.matmul(stp[s // 8 % 2][:, s % 8, p * 16:(p + 1) * 16],
                                                      kt[s % 2][:, p, :], qb[:, b, p, :], start=True, stop=True)
                            mm.then_inc(used, 1)
                    for p in range(PAIRS):
                        mm = nc.tensor.matmul(stn[0:TS, p * 16:(p + 1) * 16], g.k_s[:, p, :], qb[:, b, p, :],
                                              start=True, stop=True)
                    mm.then_inc(new_sc, 1)
                    pe.wait_ge(m_ok, b + 1)
                    pe.sem_inc(g.w.passed, 1)
                    nc.tensor.transpose(mp[0:HQ, 0:P], m1[:], g.ident[:]).then_inc(mt_ok, 1)
                    pe.wait_ge(dg_ok, b + 1)
                    nc.tensor.matmul(mp[:, 128:128 + HQ], g.ones[0:HQ, :], dg[:], start=True, stop=True)\
                        .then_inc(mb_ok, 1)
                    pe.wait_ge(exp_ok, b + 1)
                    pe.wait_ge(out_ok, b + 1)
                    for p in range(PAIRS):
                        nc.tensor.matmul(ov[:, p, :], g.v_s[:, p * P:(p + 1) * P], st[0:TS, NPG, p * 16:(p + 1) * 16],
                                         start=(p == 0), stop=False, skip_group_check=True)
                    with pe.Fori(0, GR) as r:
                        for s in range(RING):
                            pe.wait_ge(loaded[s], (b * (2 * GR) + r) * 16 + (GR * 16 + 16))
                            for p in range(PAIRS):
                                mm = nc.tensor.matmul(ov[:, p, :], ring[s][:, p * P:(p + 1) * P],
                                                      st[:, r * RING + s, p * 16:(p + 1) * 16],
                                                      start=False, stop=False, skip_group_check=True)
                            mm.then_inc(used, 1)
                    pe.wait_ge(rs_ok, b + 1)
                    nc.tensor.matmul(mp[:, 256:256 + HQ], g.ones[:], rs1[:], start=True, stop=True).then_inc(den_ok, 1)

            @block.scalar
            def _(act):
                act.preload_act_table(ACT.Exp)
                with act.Fori(0, NSEQ) as b:
                    with act.Fori(0, GR) as r:
                        for s in range(RING):
                            n = b * NPG + r * RING + s
                            act.wait_ge(k_turned, n + 1)
                            act.wait_ge(used, b * (2 * NPG) + r * RING + (s + RING - 1))
                            nc.scalar.copy(kt[s % 2][:], ktp[s % 2][:]).then_inc(kt_ok, 1)
                    act.wait_ge(sub_ok, b + 1)
                    nc.scalar.activation(st[:], st[:], ACT.Exp).then_inc(exp_ok, 1)

            @block.vector
            def _(dve):
                STEPS = 2
                with dve.Fori(0, NSEQ) as b:
                    chain = Chain(steps2, b * STEPS)
                    nc.vector.memset(st[TS:P, NPG, :], NEG)
                    with dve.Fori(0, GR) as r:
                        for x in range(RING // 8):
                            at = r * RING + x * 8
                            dst = st[:, ds(at, 8), :].rearrange("p g (h q) -> p (g h) q", q=LSEQ)
                            bias = suf[:, ds(b * NPG + at, 8), :].rearrange("p g h -> p (g h)").unsqueeze(2)\
                                .broadcast_to([P, 8 * H_F, LSEQ])
                            src = stp[x][:].rearrange("p g (h q) -> p (g h) q", q=LSEQ)
                            dve.wait_ge(used, b * (2 * NPG) + r * RING + (x * 8 + 8 + RING))
                            nc.vector.tensor_tensor(dst, src, bias, ALU.add).then_inc(st8, 1)
                    bn = bias_n[:, b].rearrange("p h q -> p (h q)")
                    dve.wait_ge(new_sc, b + 1)
                    nc.vector.tensor_tensor(st[0:TS, NPG, :], stn[0:TS, 0:HQ], bn, ALU.add).then_inc(new_st, 1)
                    dve.wait_ge(new_st, b + 1)
                    nc.vector.tensor_reduce(m1[:], st[:].rearrange("p g x -> p x g"), AX.X, ALU.max).then_inc(m_ok, 1)
                    dve.wait_ge(mt_ok, b + 1)
                    chain.mark(nc.vector.tensor_reduce(mx[:], mp[0:HQ, 0:P], AX.X, ALU.max))
                    chain.wait(dve)
                    nc.vector.tensor_scalar(dg[:], g.ident[0:HQ, 0:HQ], mx[:], None, ALU.mult).then_inc(dg_ok, 1)
                    dve.wait_ge(mb_ok, b + 1)
                    nc.vector.tensor_tensor(st[:], st[:], mp[:, 128:128 + HQ].unsqueeze(1).broadcast_to([P, SLOTS, HQ]),
                                            ALU.subtract).then_inc(sub_ok, 1)
                    dve.wait_ge(exp_ok, b + 1)
                    nc.vector.tensor_reduce(rs1[:], st[:].rearrange("p g x -> p x g"), AX.X, ALU.add).then_inc(rs_ok, 1)
                    dve.wait_ge(den_ok, b + 1)
                    chain.mark(nc.vector.reciprocal(rd[:], mp[:, 256:256 + HQ]))
                    assert chain.n == STEPS
                    chain.wait(dve)
                    for s in range(2):
                        rows = HALVES[s]
                        dst = g.br[rows, 8:12, ds(b * LSEQ + TP, LSEQ)]
                        ins = nc.vector.tensor_tensor(
                            dst, ov[rows, :, s * LSEQ:(s + 1) * LSEQ],
                            rd[rows].rearrange("p (a s q) -> p a s q", s=2, q=LSEQ)[:, :, s, :], ALU.mult)
                    ins.then_inc(out_ok, 1)


def phase_mix(g, mix):
    nc, io, w = g.nc, g.io, g.w
    KB = 4
    outs = ("w_ret_o", "w_fox_o", "w_mem_o")
    tiles = (0, 8, 4)
    with ExitStack() as ctx:
        w.open(ctx, "mix")
        raw = [g.sb(ctx, f"mo_raw{i}", [P, KB, P]) for i in range(3)]
        gate = [g.sb(ctx, f"mo_gate{i}", [P, TW]) for i in range(2)]
        part = g.sb(ctx, "mo_part", [P, TW])
        acc = [g.ps(ctx, f"mo_acc{s}", [P, NB, 512]) for s in range(2)]
        raw_ok = [g.sem(f"mo_raw_ok{i}") for i in range(3)]
        branch, gated, mixed, steps = g.sem("mo_branch"), g.sem("mo_gated"), g.sem("mo_mixed"), g.sem("mo_steps")
        b0, b1 = w.n
        with nc.Block() as block:
            @block.sync
            def _(sp):
                sp.sem_inc(gated, 1)
                sp.sem_inc(mixed, 1)
                sp.sem_inc(branch, 3)
                with sp.Fori(0, KD // 2) as jj:
                    for u in range(6):
                        x, i = divmod(u, 3)
                        s = u % 2
                        w_src = io["w_in"][:, ds(jj * (2 * P) + (C_GATE + i * D + x * P), P)]
                        o_src = io[outs[i]][:, ds(jj * (2 * P) + x * P, P)].rearrange("(k p) c -> p k c", p=P)
                        w.load(sp, s, jj * 3 + (u // 2 + (b0, b1)[s]), w_src, KD)
                        sp.wait_ge(branch, jj * 6 + (u + 1))
                        sp.sem_inc(g.w.passed, 1)
                        sp.dma_start(raw[i][:], o_src).then_inc(raw_ok[i], 16)

            @block.gpsimd
            def _(pool):
                with pool.Fori(0, KD // 2) as jj:
                    for u in range(6):
                        s = u % 2
                        w.split(pool, s, jj * 3 + (u // 2 + (b0, b1)[s]), KD)

            @block.tensor
            def _(pe):
                with pe.Fori(0, KD // 2) as jj:
                    for u in range(6):
                        x, i = divmod(u, 3)
                        s = u % 2
                        pe.wait_ge(gated, jj * 6 + (u + 1))
                        w.products(pe, s, jj * 3 + (u // 2 + (b0, b1)[s]), KD, acc[0], g.xh, g.xl)
                        pe.wait_ge(raw_ok[i], jj * 32 + (x * 16 + 16))
                        pe.wait_ge(mixed, jj * 6 + (u + 1))
                        for k in range(KB):
                            for b in range(NB):
                                mm = nc.tensor.matmul(acc[1][:, b, 0:TB], raw[i][:, k, :],
                                                      g.br[:, tiles[i] + k, b * TB:(b + 1) * TB],
                                                      start=(k == 0), stop=(k == KB - 1))
                        mm.then_inc(branch, 1)

            @block.scalar
            def _(act):
                act.preload_act_table(ACT.Sigmoid)
                with act.Fori(0, KD // 2) as jj:
                    for u in range(6):
                        x, i = divmod(u, 3)
                        s = u % 2
                        bias = g.b_gate[:, i, ds(jj * 2 + x, 1)]
                        act.wait_ge(w.done[s], jj * 3 + (u // 2 + 2 + (b0, b1)[s]))
                        if u >= 2:
                            act.wait_ge(mixed, jj * 6 + u)
                        else:
                            act.wait_ge(mixed, jj * 6 + 1)
                        nc.scalar.activation(blocks_of(gate[s][:]), acc[0][:, :, 0:TB], ACT.Sigmoid, bias=bias)\
                            .then_inc(gated, 1)

            @block.vector
            def _(dve):
                with dve.Fori(0, KD // 2) as jj:
                    for u in range(6):
                        x, i = divmod(u, 3)
                        s = u % 2
                        row = mix[:, jj * 2 + x, :]
                        out = row if i == 0 else part[:]
                        dve.wait_ge(gated, jj * 6 + (u + 2))
                        dve.wait_ge(branch, jj * 6 + (u + 4))
                        nc.vector.tensor_tensor(blocks_of(out), blocks_of(gate[s][:]), acc[1][:, :, 0:TB], ALU.mult)\
                            .then_inc(mixed, 1)
                        dve.wait_ge(mixed, jj * 6 + (u + 2))
                        if i:
                            nc.vector.tensor_tensor(row, row, part[:], ALU.add).then_inc(steps, 1)
                            dve.wait_ge(steps, jj * 4 + (x * 2 + i))
        w.n = [b0 + 3 * KD // 2, b1 + 3 * KD // 2]


def phase_out(g, mix):
    nc, io = g.nc, g.io
    with ExitStack() as ctx:
        raw = [g.sb(ctx, f"o_raw{s}", [P, KD, P]) for s in range(2)]
        acc = [g.ps(ctx, f"o_acc{s}", [P, NB, 512]) for s in range(2)]
        loaded = [g.sem(f"o_loaded{s}") for s in range(2)]
        done = [g.sem(f"o_done{s}") for s in range(2)]
        free = [g.sem(f"o_free{s}") for s in range(2)]
        summed = g.sem("o_summed")
        with nc.Block() as block:
            @block.sync
            def _(sp):
                for s in range(2):
                    sp.sem_inc(done[s], 1)
                    sp.sem_inc(free[s], 1)
                with sp.Fori(0, KD // 2) as j:
                    for s in range(2):
                        src = io["w_out"][:, ds((j * 2 + s) * P, P)].rearrange("(k p) c -> p k c", p=P)
                        sp.wait_ge(done[s], j + 1)
                        sp.dma_start(raw[s][:], src).then_inc(loaded[s], 16)

            @block.gpsimd
            def _(pool):
                nc.gpsimd.tensor_tensor(g.res[:], g.xh[:].bitcast(F32), g.xl[:].bitcast(F32), ALU.add)\
                    .then_inc(summed, 1)

            @block.tensor
            def _(pe):
                with pe.Fori(0, KD // 2) as j:
                    for s in range(2):
                        pe.wait_ge(loaded[s], j * 16 + 16)
                        pe.wait_ge(free[s], j + 1)
                        for k in range(KD):
                            for b in range(NB):
                                mm = nc.tensor.matmul(acc[s][:, b, 0:TB], raw[s][:, k, :],
                                                      mix[:, k, b * TB:(b + 1) * TB], start=(k == 0), stop=(k == KD - 1))
                        mm.then_inc(done[s], 1)

            @block.vector
            def _(dve):
                dve.wait_ge(summed, 1)
                with dve.Fori(0, KD // 2) as j:
                    for s in range(2):
                        row = g.res[:, j * 2 + s, :]
                        dve.wait_ge(done[s], j + 2)
                        nc.vector.scalar_tensor_tensor(blocks_of(row), blocks_of(row), ALPHA, acc[s][:, :, 0:TB],
                                                       ALU.mult, ALU.add).then_inc(free[s], 1)


def phase_store(g):
    nc, io = g.nc, g.io
    with ExitStack() as ctx:
        stage = g.sb(ctx, "y_stage", [P, KD, P])
        y = g.sb(ctx, "y_out", [P, KD, P])
        yt = g.ps(ctx, "y_t", [P, KD, P])
        staged, turned, read, stored = g.sem("y_staged"), g.sem("y_turned"), g.sem("y_read"), g.sem("y_stored")
        with nc.Block() as block:
            @block.gpsimd
            def _(pool):
                with pool.Fori(0, NCH) as c:
                    src = g.res[:, :, ds(c * P, P)]
                    pool.wait_ge(turned, c + 1)
                    pool.sem_inc(g.w.passed, 1)
                    nc.gpsimd.tensor_copy(stage[:], src).then_inc(staged, 1)

            @block.tensor
            def _(pe):
                with pe.Fori(0, NCH) as c:
                    pe.wait_ge(staged, c + 1)
                    pe.wait_ge(read, c + 1)
                    for k in range(KD):
                        mm = nc.tensor.transpose(yt[:, k, :], stage[:, k, :], g.ident[:])
                    mm.then_inc(turned, 1)
                pe.wait_ge(read, NCH + 1)
                for k in range(KD):
                    mm = nc.tensor.transpose(yt[0:TS, k, :], g.res[:, k, TP:T], g.ident[:])
                mm.then_inc(turned, 1)

            @block.vector
            def _(dve):
                with dve.Fori(0, NCH) as c:
                    dve.wait_ge(turned, c + 2)
                    dve.wait_ge(stored, c * 16 + 16)
                    nc.vector.tensor_copy(y[:], yt[:]).then_inc(read, 1)
                dve.wait_ge(turned, NCH + 2)
                dve.wait_ge(stored, NCH * 16 + 16)
                nc.vector.tensor_copy(y[0:TS], yt[0:TS]).then_inc(read, 1)

            @block.sync
            def _(sp):
                sp.sem_inc(turned, 1)
                sp.sem_inc(read, 1)
                sp.sem_inc(stored, 16)
                with sp.Fori(0, NCH) as c:
                    dst = io["y_prompt"][0, ds(c * P, P), :]
                    sp.wait_ge(read, c + 2)
                    sp.dma_start(dst, y[:].rearrange("p a b -> p (a b)")).then_inc(stored, 16)
                sp.wait_ge(read, NCH + 2)
                sp.dma_start(io["y_sample"].rearrange("b t d -> (b t) d"), y[0:TS].rearrange("p a b -> p (a b)"))\
                    .then_inc(stored, 16)
                sp.wait_ge(stored, 16 * (NCH + 2))


def phase_logf_pages(g):
    nc, io = g.nc, g.io
    loaded = g.sem("lfp_loaded")
    cache = io["cache_fox_logf"]
    with nc.Block() as block:
        @block.sync
        def _(sp):
            with sp.Fori(0, NSEQ * NPG) as r:
                page = sp.value_load(g.pages[0:1, ds(r, 1)], min_val=0, max_val=cache.shape[0] - 1)
                sp.dma_start(g.lft[:, r, :], cache[page]).then_inc(loaded, 16)
            sp.wait_ge(loaded, 16 * NSEQ * NPG)


def build_step(nc, io, until=None):
    with ExitStack() as ctx:
        g = Build(nc, ctx, io)
        g.w = Weights(nc, ctx)
        g.xh, g.xl = (g.sb(ctx, n, [P, KD, TW], F32R) for n in ("x_hi", "x_lo"))
        g.ident, g.ones, g.causal = (g.sb(ctx, n, [P, P]) for n in ("ident_sb", "ones_sb", "causal_sb"))
        g.ln_g, g.ln_b = g.sb(ctx, "ln_g_sb", [P, 3, KD]), g.sb(ctx, "ln_b_sb", [P, 3, KD])
        g.b_gate, g.gn_g = g.sb(ctx, "b_gate_sb", [P, 3, KD]), g.sb(ctx, "gn_g_sb", [P, H_R])
        g.b_forget, g.pages = g.sb(ctx, "b_forget_sb", [H_F, 1]), g.sb(ctx, "pages_sb", [1, NSEQ * NPG], I32)
        g.mem_kt, g.mem_v = g.sb(ctx, "mem_kt", [P, H_M, N_MEM]), g.sb(ctx, "mem_v", [P, N_MEM // P, H_M * DM])
        with ExitStack() as first:
            g.res = g.sb(first, "res0", [P, KD, TW])
            phase_load(g)
            g.end_phase()
            phase_memory(g)
            g.end_phase()
            phase_ffn(g, 0)
            g.end_phase()
            phase_norm(g, 0, last=False)
            g.end_phase()
        if until == "norm0":
            return g
        with ExitStack() as middle:
            g.br = g.sb(middle, "br", [P, 12, TW])
            phase_retention_in(g)
            g.end_phase()
            phase_retention(g)
            g.end_phase()
            phase_head_norm(g)
            g.end_phase()
            with ExitStack() as fox:
                g.k_s, g.v_s = g.sb(fox, "k_s", [P, PAIRS, TS]), g.sb(fox, "v_s", [TS, H_F * DF])
                g.lfn = g.sb(fox, "lfn", [P, NCH + 1, H_F])
                with ExitStack() as sums:
                    g.fkv = g.sb(sums, "fkv", [P, 8, TW])
                    g.negc = g.sb(sums, "negc", [H_F, TW])
                    phase_attention_in(g)
                    g.end_phase()
                    phase_kv_natural(g)
                    g.end_phase()
                    phase_fox_prompt(g)
                    g.end_phase()
                phase_cross(g)
                g.end_phase()
                with ExitStack() as pages:
                    g.lft = g.sb(pages, "lft", [P, NSEQ * NPG, H_F])
                    phase_logf_pages(g)
                    g.end_phase()
                    phase_fox_sample(g)
                    g.end_phase()
            with ExitStack() as mixed:
                mix = g.sb(mixed, "mix", [P, KD, TW])
                phase_mix(g, mix)
                g.end_phase()
                g.res = g.br[:, 0:KD, :]
                phase_out(g, mix)
                g.end_phase()
            phase_norm(g, 1, last=False)
            g.end_phase()
            phase_ffn(g, 1)
            g.end_phase()
            phase_norm(g, 2, last=True)
            g.end_phase()
            phase_store(g)
            g.end_phase()
    return g


_INS = ["x_prompt", "x_sample", "mem_prompt", "cache_fox_k", "cache_fox_v", "cache_fox_logf", "state_ret",
        "cache_mem_k", "cache_mem_v", "page_table", "ln_g", "ln_b", "w_ffn_gate", "w_ffn_up", "w_ffn_down",
        "w_in", "b_forget", "b_gate", "ret_gn_g", "w_ret_o", "w_fox_o", "w_mem_k", "w_mem_v", "w_mem_o", "w_out"]
_OUTS = [("y_prompt", (1, TP, D)), ("y_sample", (NSEQ, LSEQ, D)),
         ("fox_k_prompt", (1, TP, H_F, DF)), ("fox_v_prompt", (1, TP, H_F, DF)), ("fox_logf_prompt", (1, TP, H_F)),
         ("ret_state_prompt", (1, H_R, DK, DM)), ("mem_k_prompt", (1, N_MEM, H_M, DM)),
         ("mem_v_prompt", (1, N_MEM, H_M, DM)), ("fox_k_sample", (NSEQ, LSEQ, H_F, DF)),
         ("fox_v_sample", (NSEQ, LSEQ, H_F, DF)), ("fox_logf_sample", (NSEQ, LSEQ, H_F)),
         ("ret_state_sample", (NSEQ, H_R, DK, DM))]


def kernel(**inputs):
    import numpy as np
    from concourse import bacc
    from concourse.bass_utils import run_bass_kernel_spmd

    nc = bacc.Bacc("TRN2", target_bir_lowering=False, num_devices=1)
    arrays = {n: np.ascontiguousarray(inputs[n]) for n in _INS}
    arrays.update(shape_tables())
    io = {n: nc.dram_tensor(n, a.shape, mybir.dt.from_np(a.dtype), kind="ExternalInput").ap()
          for n, a in arrays.items()}
    for n, shape in _OUTS:
        io[n] = nc.dram_tensor(n, shape, F32, kind="ExternalOutput").ap()
    build_step(nc, io)
    r = run_bass_kernel_spmd(nc, [arrays], core_ids=[0])
    return tuple(r.results[0][n] for n, _ in _OUTS)
```

```python
from contextlib import ExitStack

import concourse.bass as bass
from concourse import mybir

F32 = mybir.dt.float32
F32R = mybir.dt.float32r
I32 = mybir.dt.int32
ALU = mybir.AluOpType
ACT = mybir.ActivationFunctionType
AX = mybir.AxisListType
ds = bass.ds

P = 128
D = 1024
KD = D // P
TP = 1024
NSEQ, LSEQ = 8, 8
TS = NSEQ * LSEQ
T = TP + TS
NB, TB = 3, 364
TW = NB * TB
NCH = TP // P
D_FF = 2816
FT = D_FF // P
FC = 4
H_R, DK, H_F, DF, H_M, DM = 4, 64, 8, 64, 4, 128
N_MEM, PAGE, NPG = 256, 128, 32
PAST = PAGE * NPG
C_FQ, C_FL, C_MQ, C_GATE = 1536, 3072, 3080, 3592
ALPHA = 2.0 ** 0.25
EPS = 1e-5
NEG = -1e30
PAIRS = H_F // 2
RING = 16


def gammas():
    import numpy as np
    h = np.arange(H_R, dtype=np.float32)
    return np.log1p(-np.exp2(np.float32(-5.0) - h)).astype(np.float32)


def decays(c):
    import numpy as np
    return [float(np.exp(np.float32(c) * g, dtype=np.float32)) for g in gammas()]


def shape_tables():
    import numpy as np
    f = np.float32
    lg = gammas()
    ident = np.eye(P, dtype=f)
    rot = np.zeros((P, P), f)
    for m in range(P):
        if m % DK < DK // 2:
            rot[m + DK // 2, m] = -1.0
        else:
            rot[m - DK // 2, m] = 1.0
    half = DK // 2
    inv = (10000.0 ** (-np.arange(half) / half)).astype(f)
    pos = np.concatenate([np.arange(TP, dtype=f), np.tile(PAST + np.arange(LSEQ, dtype=f), NSEQ)])
    ang = (pos[None, :] * inv[:, None]).astype(f)
    cos = np.tile(np.cos(ang), (4, 1)).astype(f)
    sin = np.tile(np.sin(ang), (4, 1)).astype(f)

    def dec(steps):
        return np.exp(steps[..., None].astype(f) * lg).astype(f)

    i = np.arange(P)
    j = np.arange(TS)
    scale = f(DK ** -0.5)
    qd = dec(i + 1).T.reshape(2, 2, 1, P).transpose(1, 2, 0, 3)
    q_dec = np.broadcast_to(qd, (2, DK, 2, P)).reshape(P, 2, P)
    qs = dec(j % LSEQ + 1).T.reshape(2, 2, 1, TS).transpose(1, 2, 0, 3)
    q_dec_s = np.broadcast_to(qs, (2, DK, 2, TS)).reshape(P, 2, TS)
    k_dec = np.repeat(dec(P - 1 - i) * scale, DK, axis=1)
    k_dec_s = np.repeat(dec(LSEQ - 1 - j % LSEQ) * scale, DK, axis=1)
    d = i[None, :] - i[:, None]
    dmask = (np.where(d[..., None] >= 0, dec(np.maximum(d, 0)), 0) * scale).transpose(0, 2, 1)
    e = j[None, :] - j[:, None]
    same = (j[None, :] // LSEQ == j[:, None] // LSEQ) & (e >= 0)
    dmask_s = (np.where(same[..., None], dec(np.maximum(e, 0)), 0) * scale).transpose(0, 2, 1)
    causal = np.where(i[:, None] >= i[None, :], 0.0, NEG)
    seq = (j[:, None] // LSEQ == np.arange(NSEQ)[None, :])
    cols = np.broadcast_to(seq.T[None], (P, NSEQ, TS))
    new = np.where(seq[:, :, None] & (j[:, None, None] % LSEQ <= np.arange(LSEQ)), 0.0, NEG)
    pair_row = np.zeros((2, 2, P), f)
    pair_row[0, 0] = 1.0
    pair_row[1, 1] = 1.0
    tables = {
        "ident": ident, "rot": rot, "cos": cos, "sin": sin,
        "q_dec": q_dec, "q_dec_s": q_dec_s, "k_dec": k_dec, "k_dec_s": k_dec_s,
        "dmask": dmask, "dmask_s": dmask_s, "causal": causal, "seq_rows": seq, "seq_cols": cols,
        "new_mask": np.tile(new.transpose(2, 1, 0), (P // LSEQ, 1, 1)), "pair_row": pair_row,
        "after": (i[:, None] > i[None, :]),
        "upto": (same & (e >= 0)),
    }
    return {n: np.ascontiguousarray(a, dtype=f) for n, a in tables.items()}


class Chain:

    def __init__(self, sem, base=0):
        self.sem, self.base, self.n = sem, base, 0

    def mark(self, instruction):
        instruction.then_inc(self.sem, 1)
        self.n += 1

    def wait(self, engine):
        engine.wait_ge(self.sem, self.base + self.n)


class Weights:

    def __init__(self, nc, ctx):
        self.nc = nc
        self.loaded = [ctx.enter_context(nc.semaphore(f"w_loaded{s}")) for s in range(2)]
        self.high = [ctx.enter_context(nc.semaphore(f"w_high{s}")) for s in range(2)]
        self.low = [ctx.enter_context(nc.semaphore(f"w_low{s}")) for s in range(2)]
        self.done = [ctx.enter_context(nc.semaphore(f"w_done{s}")) for s in range(2)]
        self.passed = ctx.enter_context(nc.semaphore("w_passed"))
        self.n = [0, 0]

    def open(self, ctx, tag):
        nc = self.nc
        self.raw = [ctx.enter_context(nc.sbuf_tensor(f"w_raw{s}_{tag}", [P, KD, P], F32)) for s in range(2)]
        self.hi = [ctx.enter_context(nc.sbuf_tensor(f"w_hi{s}_{tag}", [P, KD, P], F32R)) for s in range(2)]
        self.lo = [ctx.enter_context(nc.sbuf_tensor(f"w_lo{s}_{tag}", [P, KD, P], F32R)) for s in range(2)]

    def load(self, sp, s, n, src, kt):
        sp.wait_ge(self.low[s], n + 1)
        sp.dma_start(self.raw[s][:, 0:kt, :], src.rearrange("(k p) c -> p k c", p=P))\
          .then_inc(self.loaded[s], 16)

    def split(self, pool, s, n, kt):
        raw, hi, lo = (x[s][:, 0:kt, :] for x in (self.raw, self.hi, self.lo))
        pool.wait_ge(self.loaded[s], n * 16 + 16)
        pool.wait_ge(self.done[s], n + 1)
        pool.sem_inc(self.passed, 1)
        self.nc.gpsimd.tensor_copy(hi, raw).then_inc(self.high[s], 1)
        pool.wait_ge(self.high[s], n + 1)
        self.nc.gpsimd.tensor_tensor(lo, raw, hi.bitcast(F32), ALU.subtract).then_inc(self.low[s], 1)

    def products(self, pe, s, n, kt, out, x_hi, x_lo, width=TB, blocks=NB, ready=None):
        pe.wait_ge(self.low[s], n + 2)
        for k in range(kt):
            if ready is not None:
                pe.wait_ge(ready[0], ready[1] + k)
            for w, x, first, last in ((self.hi, x_hi, True, False), (self.hi, x_lo, False, False),
                                      (self.lo, x_hi, False, True)):
                for b in range(blocks):
                    mm = self.nc.tensor.matmul(out[:, b, 0:width], w[s][:, k, :],
                                               x[:, k, b * width:(b + 1) * width],
                                               start=(k == 0 and first), stop=(k == kt - 1 and last))
        mm.then_inc(self.done[s], 1)


class Build:

    def __init__(self, nc, ctx, io):
        self.nc, self.ctx, self.io = nc, ctx, io
        self.sems = []

    def sem(self, name):
        self.sems.append(self.nc.alloc_semaphore(name))
        return self.sems[-1]

    def end_phase(self):
        for sem in self.sems:
            self.nc.gpsimd.sem_clear(sem)
        self.nc.all_engine_barrier()
        for sem in self.sems:
            self.nc.release_semaphore(sem)
        self.sems = []

    def sb(self, ctx, name, shape, dt=F32):
        return ctx.enter_context(self.nc.sbuf_tensor(name, shape, dt))

    def ps(self, ctx, name, shape):
        size = 1
        for n in shape[1:]:
            size *= n
        whole = ctx.enter_context(self.nc.psum_tensor(name, [shape[0], -(-size // 512) * 512], F32))
        flat = whole[:, 0:size]
        return flat if len(shape) == 2 else flat.rearrange("p (a b) -> p a b", b=shape[2]) if len(shape) == 3 \
            else flat.rearrange("p (a b c) -> p a b c", b=shape[2], c=shape[3])


def blocks_of(tile):
    return tile.rearrange("p (b t) -> p b t", t=TB)


def phase_load(g):
    nc, io = g.nc, g.io
    with ExitStack() as ctx:
        xin = [g.sb(ctx, f"x_in{s}", [P, D]) for s in range(2)]
        xt = [g.ps(ctx, f"x_t{s}", [P, KD, P]) for s in range(2)]
        consts, ones = g.sem("consts_loaded"), g.sem("ones_set")
        loaded = [g.sem(f"x_loaded{s}") for s in range(2)]
        turned = [g.sem(f"x_turned{s}") for s in range(2)]
        hi = [g.sem(f"x_hi{s}") for s in range(2)]
        lo = [g.sem(f"x_lo{s}") for s in range(2)]
        acc = [g.sem(f"x_acc{s}") for s in range(2)]
        n_const = 8
        xs = io["x_sample"].rearrange("b t d -> (b t) d")
        with nc.Block() as block:
            @block.sync
            def _(sp):
                for s in range(2):
                    for sem in (g.w.low[s], g.w.done[s], turned[s], lo[s], acc[s]):
                        sp.sem_inc(sem, 1)
                sp.dma_start(g.ident[:], io["ident"]).then_inc(consts, 16)
                sp.dma_start(g.ln_g[:], io["ln_g"].rearrange("l (k p) -> p l k", p=P),
                             allow_slow_non_contiguous=True).then_inc(consts, 16)
                sp.dma_start(g.ln_b[:], io["ln_b"].rearrange("l (k p) -> p l k", p=P),
                             allow_slow_non_contiguous=True).then_inc(consts, 16)
                sp.dma_start(g.b_gate[:], io["b_gate"].rearrange("i (k p) -> p i k", p=P),
                             allow_slow_non_contiguous=True).then_inc(consts, 16)
                sp.dma_start(g.gn_g[:], io["ret_gn_g"].rearrange("(h p) -> p h", p=P),
                             allow_slow_non_contiguous=True).then_inc(consts, 16)
                sp.dma_start(g.b_forget[:], io["b_forget"].rearrange("(h o) -> h o", o=1)).then_inc(consts, 16)
                sp.dma_start(g.pages[:], io["page_table"].rearrange("b n -> (b n)").unsqueeze(0)).then_inc(consts, 16)
                sp.dma_start(g.causal[:], io["causal"]).then_inc(consts, 16)
                with sp.Fori(0, NCH // 2) as i:
                    for s in range(2):
                        src = io["x_prompt"][0, ds((i * 2 + s) * P, P), :]
                        sp.wait_ge(turned[s], i + 1)
                        sp.dma_start(xin[s][:], src).then_inc(loaded[s], 16)
                sp.wait_ge(turned[0], NCH // 2 + 1)
                sp.dma_start(xin[0][0:TS, :], xs).then_inc(loaded[0], 16)
                sp.wait_ge(consts, 16 * n_const)

            def turn(pe, s, n, rows):
                pe.wait_ge(loaded[s], n * 16 + 16)
                pe.wait_ge(lo[s], n + 1)
                pe.wait_ge(acc[s], n + 1)
                for k in range(KD):
                    mm = nc.tensor.transpose(xt[s][:, k, 0:rows], xin[s][0:rows, k * P:(k + 1) * P],
                                             g.ident[0:rows, 0:rows])
                mm.then_inc(turned[s], 1)

            @block.tensor
            def _(pe):
                pe.wait_ge(consts, 16 * n_const)
                with pe.Fori(0, NCH // 2) as i:
                    for s in range(2):
                        turn(pe, s, i, P)
                turn(pe, 0, NCH // 2, TS)

            @block.scalar
            def _(act):
                def copies(s, n, hi_dst, acc_dst, rows):
                    act.wait_ge(turned[s], n + 2)
                    nc.scalar.copy(hi_dst, xt[s][:, :, 0:rows]).then_inc(hi[s], 1)
                    nc.scalar.mul(acc_dst, xt[s][:, :, 0:rows], ALPHA).then_inc(acc[s], 1)
                with act.Fori(0, NCH // 2) as i:
                    for s in range(2):
                        at = ds((i * 2 + s) * P, P)
                        copies(s, i, g.xh[:, :, at], g.res[:, :, at], P)
                copies(0, NCH // 2, g.xh[:, :, TP:T], g.res[:, :, TP:T], TS)

            @block.vector
            def _(dve):
                nc.vector.memset(g.xh[:, :, T:TW].bitcast(F32), 0.0)
                nc.vector.memset(g.xl[:, :, T:TW].bitcast(F32), 0.0)
                nc.vector.memset(g.res[:, :, T:TW], 0.0)
                nc.vector.memset(g.ones[:], 1.0)

                def lows(s, n, lo_dst, hi_src, rows):
                    dve.wait_ge(hi[s], n + 1)
                    dve.wait_ge(acc[s], n + 2)
                    nc.vector.tensor_tensor(lo_dst, xt[s][:, :, 0:rows], hi_src.bitcast(F32), ALU.subtract)\
                        .then_inc(lo[s], 1)
                with dve.Fori(0, NCH // 2) as i:
                    for s in range(2):
                        at = ds((i * 2 + s) * P, P)
                        lows(s, i, g.xl[:, :, at], g.xh[:, :, at], P)
                lows(0, NCH // 2, g.xl[:, :, TP:T], g.xh[:, :, TP:T], TS)


def phase_memory(g):
    nc, io, w = g.nc, g.io, g.w
    MT = N_MEM // P
    with ExitStack() as ctx:
        w.open(ctx, "mem")
        m_in = g.sb(ctx, "m_in", [P, MT, D])
        mh = g.sb(ctx, "mh", [P, KD, N_MEM], F32R)
        ml = g.sb(ctx, "ml", [P, KD, N_MEM], F32R)
        kv = [g.sb(ctx, f"m_kv{s}", [P, N_MEM]) for s in range(2)]
        kn = g.sb(ctx, "m_kn", [P, MT, H_M * DM])
        acc = [g.ps(ctx, f"m_acc{s}", [P, 1, 512]) for s in range(2)]
        mt = g.ps(ctx, "m_t", [P, KD, P])
        tn = g.ps(ctx, "m_tn", [P, 2, MT, P])
        loaded, turned, hi, lo = g.sem("m_loaded"), g.sem("m_turned"), g.sem("m_hi"), g.sem("m_lo")
        kv_out = [g.sem(f"m_kv_out{s}") for s in range(2)]
        nat, nat_out, stored = g.sem("m_nat"), g.sem("m_nat_out"), g.sem("m_stored")
        kt_out = g.sem("m_kt_out")
        base = list(w.n)
        with nc.Block() as block:
            @block.sync
            def _(sp):
                for s in range(2):
                    sp.sem_inc(kv_out[s], 1)
                sp.sem_inc(nat_out, 1)
                sp.dma_start(m_in[:], io["mem_prompt"][0].rearrange("(m p) d -> p m d", p=P)).then_inc(loaded, 16)
                with sp.Fori(0, H_M) as h:
                    for s, name in enumerate(("w_mem_k", "w_mem_v")):
                        w.load(sp, s, h + base[s], io[name][:, ds(h * DM, DM)], KD)
                sp.wait_ge(nat_out, H_M + 1)
                for name, src in (("mem_k_prompt", kn), ("mem_v_prompt", g.mem_v)):
                    sp.dma_start(io[name][0].rearrange("(m p) h d -> p m (h d)", p=P), src[:]).then_inc(stored, 16)
                sp.wait_ge(stored, 32)

            @block.gpsimd
            def _(pool):
                with pool.Fori(0, H_M) as h:
                    for s in range(2):
                        w.split(pool, s, h + base[s], KD)

            @block.tensor
            def _(pe):
                pe.wait_ge(loaded, 16)
                for m in range(MT):
                    if m > 0:
                        pe.wait_ge(lo, m)
                    for k in range(KD):
                        mm = nc.tensor.transpose(mt[:, k, :], m_in[:, m, k * P:(k + 1) * P], g.ident[:])
                    mm.then_inc(turned, 1)
                pe.wait_ge(lo, MT)
                with pe.Fori(0, H_M) as h:
                    for s in range(2):
                        pe.wait_ge(kv_out[s], h + 1)
                        w.products(pe, s, h + base[s], KD, acc[s], mh, ml, width=N_MEM, blocks=1)
                    pe.wait_ge(nat_out, h + 1)
                    for s in range(2):
                        pe.wait_ge(kv_out[s], h + 2)
                        for m in range(MT):
                            mm = nc.tensor.transpose(tn[:, s, m, :], kv[s][:, m * P:(m + 1) * P], g.ident[:])
                    mm.then_inc(nat, 1)

            @block.scalar
            def _(act):
                for m in range(MT):
                    act.wait_ge(turned, m + 1)
                    nc.scalar.copy(mh[:, :, m * P:(m + 1) * P], mt[:]).then_inc(hi, 1)
                with act.Fori(0, H_M) as h:
                    act.wait_ge(w.done[0], h + (base[0] + 2))
                    nc.scalar.copy(kv[0][:], acc[0][:, 0, 0:N_MEM]).then_inc(kv_out[0], 1)
                    dst = g.mem_kt[:, h, :]
                    act.wait_ge(kv_out[0], h + 2)
                    nc.scalar.copy(dst, kv[0][:]).then_inc(kt_out, 1)
                    act.wait_ge(kt_out, h + 1)
                    act.wait_ge(nat, h + 1)

            @block.vector
            def _(dve):
                for m in range(MT):
                    dve.wait_ge(hi, m + 1)
                    nc.vector.tensor_tensor(ml[:, :, m * P:(m + 1) * P], mt[:],
                                            mh[:, :, m * P:(m + 1) * P].bitcast(F32), ALU.subtract).then_inc(lo, 1)
                with dve.Fori(0, H_M) as h:
                    dve.wait_ge(w.done[1], h + (base[1] + 2))
                    nc.vector.tensor_copy(kv[1][:], acc[1][:, 0, 0:N_MEM]).then_inc(kv_out[1], 1)
                    k_dst, v_dst = kn[:, :, ds(h * DM, DM)], g.mem_v[:, :, ds(h * DM, DM)]
                    dve.wait_ge(nat, h + 1)
                    nc.vector.tensor_copy(k_dst, tn[:, 0])
                    nc.vector.tensor_copy(v_dst, tn[:, 1]).then_inc(nat_out, 1)
        w.n = [x + H_M for x in base]


def phase_ffn(g, layer):
    nc, io, w = g.nc, g.io, g.w
    wg, wu, wd = (io[n][layer] for n in ("w_ffn_gate", "w_ffn_up", "w_ffn_down"))
    full = FT // FC
    rest = FT - full * FC
    per = FC + KD // 2
    with ExitStack() as ctx:
        w.open(ctx, f"ffn{layer}")
        hh = g.sb(ctx, f"h_hi{layer}", [P, FC, TW], F32R)
        hl = g.sb(ctx, f"h_lo{layer}", [P, FC, TW], F32R)
        silu = g.sb(ctx, f"silu{layer}", [P, TW])
        hid = g.sb(ctx, f"hid{layer}", [P, TW])
        acc = [g.ps(ctx, f"f_acc{s}_{layer}", [P, NB, 512]) for s in range(2)]
        free = [g.sem(f"f_free{s}_{layer}") for s in range(2)]
        hh_ok, hl_ok = g.sem(f"f_hh{layer}"), g.sem(f"f_hl{layer}")
        b0, b1 = w.n
        with nc.Block() as block:
            @block.sync
            def _(sp):
                for s in range(2):
                    sp.sem_inc(free[s], 1)

                def ups(c, n, ft):
                    with sp.Fori(0, ft) as f:
                        at = ds((c * FC + f) * P, P)
                        w.load(sp, 0, n + f + b0, wg[:, at], KD)
                        w.load(sp, 1, n + f + b1, wu[:, at], KD)

                def downs(c, n, ft):
                    with sp.Fori(0, KD // 2) as j:
                        for s in range(2):
                            src = wd[ds(c * (FC * P), ft * P), ds((j * 2 + s) * P, P)]
                            w.load(sp, s, n + j + (b0, b1)[s], src, ft)

                with sp.Fori(0, full) as c:
                    ups(c, c * per, FC)
                    downs(c, c * per + FC, FC)
                ups(full, full * per, rest)
                downs(full, full * per + rest, rest)

            @block.tensor
            def _(pe):
                def ups(n, ft):
                    with pe.Fori(0, ft) as f:
                        for s in range(2):
                            pe.wait_ge(free[s], n + f + 1)
                            w.products(pe, s, n + f + (b0, b1)[s], KD, acc[s], g.xh, g.xl)

                def downs(c, n, ft):
                    with pe.Fori(0, KD // 2) as j:
                        for s in range(2):
                            pe.wait_ge(free[s], n + j + 1)
                            w.products(pe, s, n + j + (b0, b1)[s], ft, acc[s], hh, hl,
                                       ready=(hl_ok, c * FC + 1))

                with pe.Fori(0, full) as c:
                    ups(c * per, FC)
                    downs(c, c * per + FC, FC)
                ups(full * per, rest)
                downs(full, full * per + rest, rest)

            @block.gpsimd
            def _(pool):
                def tiles(n, count, kt):
                    with pool.Fori(0, count) as j:
                        for s in range(2):
                            w.split(pool, s, n + j + (b0, b1)[s], kt)

                with pool.Fori(0, full) as c:
                    tiles(c * per, FC, KD)
                    tiles(c * per + FC, KD // 2, FC)
                tiles(full * per, rest, KD)
                tiles(full * per + rest, KD // 2, rest)

            @block.scalar
            def _(act):
                act.preload_act_table(ACT.Silu)

                def ups(c, n, ft):
                    with act.Fori(0, ft) as f:
                        dst = hh[:, f, :]
                        act.wait_ge(w.done[0], n + f + (b0 + 2))
                        nc.scalar.activation(blocks_of(silu[:]), acc[0][:, :, 0:TB], ACT.Silu)\
                            .then_inc(free[0], 1)
                        act.wait_ge(free[1], n + f + 2)
                        nc.scalar.copy(dst, hid[:]).then_inc(hh_ok, 1)

                with act.Fori(0, full) as c:
                    ups(c, c * per, FC)
                ups(full, full * per, rest)

            @block.vector
            def _(dve):
                def ups(c, n, ft):
                    with dve.Fori(0, ft) as f:
                        hi_src, lo_dst = hh[:, f, :], hl[:, f, :]
                        dve.wait_ge(free[0], n + f + 2)
                        dve.wait_ge(w.done[1], n + f + (b1 + 2))
                        nc.vector.tensor_tensor(blocks_of(hid[:]), blocks_of(silu[:]), acc[1][:, :, 0:TB],
                                                ALU.mult).then_inc(free[1], 1)
                        dve.wait_ge(free[1], n + f + 2)
                        dve.wait_ge(hh_ok, c * FC + f + 1)
                        nc.vector.tensor_tensor(lo_dst, hid[:], hi_src.bitcast(F32), ALU.subtract)\
                            .then_inc(hl_ok, 1)
                        dve.wait_ge(hl_ok, c * FC + f + 1)

                def downs(n, ft):
                    with dve.Fori(0, KD // 2) as j:
                        for s in range(2):
                            row = g.res[:, j * 2 + s, :]
                            dve.wait_ge(w.done[s], n + j + ((b0, b1)[s] + 2))
                            nc.vector.scalar_tensor_tensor(blocks_of(row), acc[s][:, :, 0:TB], 0.5, blocks_of(row),
                                                           ALU.mult, ALU.add).then_inc(free[s], 1)

                with dve.Fori(0, full) as c:
                    ups(c, c * per, FC)
                    downs(c * per + FC, FC)
                ups(full, full * per, rest)
                downs(full * per + rest, rest)
        used = full * per + rest + KD // 2
        w.n = [b0 + used, b1 + used]


def phase_norm(g, which, last):
    nc = g.nc
    with ExitStack() as ctx:
        mean_w = g.sb(ctx, f"mean_w{which}", [P, P])
        sq = g.sb(ctx, f"sq{which}", [P, KD, TB])
        rstd = [g.sb(ctx, f"rstd{b}_{which}", [P, TB]) for b in range(NB)]
        std = [g.sb(ctx, f"std{b}_{which}", [P, TB]) for b in range(NB)]
        hn = [g.sb(ctx, f"hn{s}_{which}", [P, KD, TB]) for s in range(2)]
        eps = g.sb(ctx, f"eps{which}", [P, 1])
        mean = [g.ps(ctx, f"mean{b}_{which}", [P, 512]) for b in range(NB)]
        var = [g.ps(ctx, f"var{b}_{which}", [P, 512]) for b in range(NB)]
        ready, mean_ok, var_ok = g.sem(f"n_ready{which}"), g.sem(f"n_mean{which}"), g.sem(f"n_var{which}")
        centred, squared, std_ok = g.sem(f"n_centred{which}"), g.sem(f"n_squared{which}"), g.sem(f"n_std{which}")
        rstd_ok, scaled, affine = g.sem(f"n_rstd{which}"), g.sem(f"n_scaled{which}"), g.sem(f"n_affine{which}")
        high, low = g.sem(f"n_high{which}"), g.sem(f"n_low{which}")

        def cols(b):
            return slice(b * TB, (b + 1) * TB)

        def over_k(tile):
            return tile.unsqueeze(1).broadcast_to([P, KD, TB])
        with nc.Block() as block:
            @block.gpsimd
            def _(pool):
                nc.gpsimd.memset(mean_w[:], 1.0 / D).then_inc(ready, 1)
                nc.gpsimd.memset(eps[:], EPS).then_inc(ready, 1)

            @block.tensor
            def _(pe):
                pe.wait_ge(ready, 2)
                for b in range(NB):
                    for k in range(KD):
                        mm = nc.tensor.matmul(mean[b][:, 0:TB], mean_w[:], g.res[:, k, cols(b)],
                                              start=(k == 0), stop=(k == KD - 1))
                    mm.then_inc(mean_ok, 1)
                for b in range(NB):
                    pe.wait_ge(squared, b + 1)
                    for k in range(KD):
                        mm = nc.tensor.matmul(var[b][:, 0:TB], mean_w[:], sq[:, k, :],
                                              start=(k == 0), stop=(k == KD - 1))
                    mm.then_inc(var_ok, 1)

            @block.vector
            def _(dve):
                for b in range(NB):
                    dve.wait_ge(mean_ok, b + 1)
                    nc.vector.tensor_tensor(g.res[:, :, cols(b)], g.res[:, :, cols(b)],
                                            over_k(mean[b][:, 0:TB]), ALU.subtract).then_inc(centred, 1)
                for b in range(NB):
                    dve.wait_ge(std_ok, b + 1)
                    nc.vector.reciprocal(rstd[b][:], std[b][:]).then_inc(rstd_ok, 1)
                    dve.wait_ge(rstd_ok, b + 1)
                    nc.vector.tensor_tensor(g.res[:, :, cols(b)], g.res[:, :, cols(b)], over_k(rstd[b][:]),
                                            ALU.mult).then_inc(scaled, 1)
                    if not last and b > 0:
                        dve.wait_ge(high, b)
                        nc.vector.tensor_tensor(g.xl[:, :, cols(b - 1)], hn[(b - 1) % 2][:],
                                                g.xh[:, :, cols(b - 1)].bitcast(F32), ALU.subtract).then_inc(low, 1)
                if not last:
                    dve.wait_ge(high, NB)
                    nc.vector.tensor_tensor(g.xl[:, :, cols(NB - 1)], hn[(NB - 1) % 2][:],
                                            g.xh[:, :, cols(NB - 1)].bitcast(F32), ALU.subtract).then_inc(low, 1)

            @block.scalar
            def _(act):
                act.wait_ge(ready, 2)
                for b in range(NB):
                    act.wait_ge(centred, b + 1)
                    if b > 0:
                        act.wait_ge(var_ok, b)
                    nc.scalar.activation(sq[:], g.res[:, :, cols(b)], ACT.Square).then_inc(squared, 1)
                for b in range(NB):
                    act.wait_ge(var_ok, b + 1)
                    nc.scalar.activation(std[b][:], var[b][:, 0:TB], ACT.Sqrt, bias=eps[:]).then_inc(std_ok, 1)
                for b in range(NB):
                    act.wait_ge(scaled, b + 1)
                    if not last and b >= 2:
                        act.wait_ge(low, b - 1)
                    for k in range(KD):
                        dst = g.res[:, k, cols(b)] if last else hn[b % 2][:, k, :]
                        nc.scalar.activation(dst, g.res[:, k, cols(b)], ACT.Identity,
                                             bias=g.ln_b[:, which, k:k + 1], scale=g.ln_g[:, which, k:k + 1])\
                            .then_inc(affine, 1)
                    if not last:
                        act.wait_ge(affine, KD * (b + 1))
                        nc.scalar.copy(g.xh[:, :, cols(b)], hn[b % 2][:]).then_inc(high, 1)
                        nc.scalar.mul(g.res[:, :, cols(b)], hn[b % 2][:], ALPHA)


def phase_retention_in(g):
    nc, io, w = g.nc, g.io, g.w
    pairs, plain = 6, 4
    with ExitStack() as ctx:
        w.open(ctx, "ret")
        acc = [g.ps(ctx, f"r_acc{s}", [P, NB, 512]) for s in range(2)]
        free = [g.sem(f"r_free{s}") for s in range(2)]
        b0, b1 = w.n
        with nc.Block() as block:
            @block.sync
            def _(sp):
                for s in range(2):
                    sp.sem_inc(free[s], 1)
                with sp.Fori(0, pairs) as n:
                    for s in range(2):
                        w.load(sp, s, n + (b0, b1)[s], io["w_in"][:, ds((n * 2 + s) * P, P)], KD)

            @block.gpsimd
            def _(pool):
                with pool.Fori(0, pairs) as n:
                    for s in range(2):
                        w.split(pool, s, n + (b0, b1)[s], KD)

            @block.tensor
            def _(pe):
                with pe.Fori(0, pairs) as n:
                    for s in range(2):
                        pe.wait_ge(free[s], n + 1)
                        w.products(pe, s, n + (b0, b1)[s], KD, acc[s], g.xh, g.xl)

            @block.scalar
            def _(act):
                act.preload_act_table(ACT.Silu)
                with act.Fori(0, plain) as n:
                    dst = blocks_of(g.br[:, n * 2 + 4, :])
                    act.wait_ge(w.done[0], n + (b0 + 2))
                    nc.scalar.copy(dst, acc[0][:, :, 0:TB]).then_inc(free[0], 1)
                with act.Fori(plain, pairs) as n:
                    for s in range(2):
                        dst = blocks_of(g.br[:, n * 2 + (s - 2 * plain), :])
                        act.wait_ge(w.done[s], n + ((b0, b1)[s] + 2))
                        nc.scalar.activation(dst, acc[s][:, :, 0:TB], ACT.Silu).then_inc(free[s], 1)

            @block.vector
            def _(dve):
                with dve.Fori(0, plain) as n:
                    dst = blocks_of(g.br[:, n * 2 + 5, :])
                    dve.wait_ge(w.done[1], n + (b1 + 2))
                    nc.vector.tensor_copy(dst, acc[1][:, :, 0:TB]).then_inc(free[1], 1)
        w.n = [b0 + pairs, b1 + pairs]


HALVES = [slice(0, DK), slice(DK, P)]


def phase_retention(g):
    nc, io = g.nc, g.io
    dec_c, dec_s = decays(P), decays(LSEQ)
    with ExitStack() as ctx:
        def sb(name, shape):
            return g.sb(ctx, "rt_" + name, shape)
        cos, sin, rot = sb("cos", [P, T]), sb("sin", [P, T]), sb("rot", [P, P])
        q_dec, k_dec, dmask = sb("q_dec", [P, 2, P]), sb("k_dec", [P, H_R * DK]), sb("dmask", [P, H_R, P])
        q_dec_s, k_dec_s = sb("q_dec_s", [P, 2, TS]), sb("k_dec_s", [TS, H_R * DK])
        dmask_s, seq_rows, seq_cols = sb("dmask_s", [TS, H_R, TS]), sb("seq_rows", [TS, NSEQ]), sb("seq_cols", [P, NSEQ, TS])
        stage = sb("stage", [P, 8, P])
        turned, qk, qd = sb("turned", [P, 4, P]), sb("qk", [P, 4, P]), sb("qd", [P, 2, 2, P])
        qz = sb("qz", [P, 2, 2, P])
        kd, vn, at = sb("kd", [P, H_R * DK]), sb("vn", [P, H_R, P]), sb("at", [P, H_R, P])
        state = sb("state", [P, 2, DM])
        s0, s1 = sb("s0", [P, 2, DM]), sb("s1", [P, 2, DM])
        kdm, qdm = sb("kdm", [TS, H_R * DK]), sb("qdm", [P, 2, 2, TS])
        swap = g.ps(ctx, "rt_swap", [P, 4, P])
        vt = g.ps(ctx, "rt_vt", [P, H_R, P])
        kt = g.ps(ctx, "rt_kt", [P, 2, P])
        scores = g.ps(ctx, "rt_scores", [P, H_R, P])
        o = g.ps(ctx, "rt_o", [P, H_R, P])
        o_s = g.ps(ctx, "rt_o_s", [P, H_R, P])
        upd = g.ps(ctx, "rt_upd", [P, H_R, P])
        names = {"cos": cos, "sin": sin, "rot": rot, "q_dec": q_dec, "k_dec": k_dec, "dmask": dmask,
                 "q_dec_s": q_dec_s, "k_dec_s": k_dec_s, "dmask_s": dmask_s, "seq_rows": seq_rows, "seq_cols": seq_cols}
        consts, zeroed = g.sem("rt_consts"), g.sem("rt_zeroed")
        staged, pe_swap, roped = g.sem("rt_staged"), g.sem("rt_pe_swap"), g.sem("rt_roped")
        v_nat, pe_scores, masked = g.sem("rt_v_nat"), g.sem("rt_pe_scores"), g.sem("rt_masked")
        pe_out, o_read, state_ok = g.sem("rt_pe_out"), g.sem("rt_o_read"), g.sem("rt_state")
        steps = g.sem("rt_steps")
        loaded, s_masked, s_pe = g.sem("rt_s_loaded"), g.sem("rt_s_masked"), g.sem("rt_s_pe")
        s_new, s_stored, stored = g.sem("rt_s_new"), g.sem("rt_s_stored"), g.sem("rt_stored")
        STEPS = 2

        def rope(dve, chain, t_cos, t_sin, q_decay, n, src):
            nc.vector.tensor_tensor(turned[:, :, 0:n], src, t_cos.unsqueeze(1).broadcast_to([P, 4, n]), ALU.mult)
            chain.mark(nc.vector.tensor_tensor(qk[:, :, 0:n], swap[:, :, 0:n],
                                               t_sin.unsqueeze(1).broadcast_to([P, 4, n]), ALU.mult))
            chain.wait(dve)
            nc.vector.tensor_tensor(qk[:, 2:4, 0:n], qk[:, 2:4, 0:n], turned[:, 2:4, 0:n], ALU.add)
            for s, rows in enumerate(HALVES):
                ins = nc.vector.tensor_tensor(qz[rows, s, :, 0:n], qk[rows, 0:2, 0:n], turned[rows, 0:2, 0:n], ALU.add)
            chain.mark(ins)
            chain.wait(dve)
            for s, rows in enumerate(HALVES):
                ins = nc.vector.tensor_tensor(qd[rows, s, :, 0:n], qz[rows, s, :, 0:n], q_decay[rows], ALU.mult)
            ins.then_inc(roped, 1)

        def chunk_scores(n):
            for p in range(2):
                nc.tensor.transpose(kt[0:n, p, :], qk[:, 2 + p, 0:n], g.ident[:])
            for h in range(H_R):
                mm = nc.tensor.matmul(scores[0:n, h, 0:n], qk[:, 2 + h // 2, 0:n], qz[:, h % 2, h // 2, 0:n],
                                      start=True, stop=True)
            mm.then_inc(pe_scores, 1)

        with nc.Block() as block:
            @block.sync
            def _(sp):
                for sem in (roped, v_nat, o_read, s_new, s_stored):
                    sp.sem_inc(sem, 16 if sem is s_stored else 1)
                for name, dst in names.items():
                    sp.dma_start(dst[:], io[name]).then_inc(consts, 16)
                with sp.Fori(0, NSEQ) as b:
                    src = io["state_ret"][b].rearrange("(pr two) d e -> two d pr e", two=2)
                    new = io["ret_state_sample"][b].rearrange("(pr two) d e -> two d pr e", two=2)
                    halves = [(src[i], new[i]) for i in range(2)]
                    sp.wait_ge(s_new, b + 1)
                    for i in range(2):
                        sp.dma_start(s0[HALVES[i]], src[i]).then_inc(loaded, 16)
                    sp.wait_ge(s_new, b + 2)
                    for i in range(2):
                        sp.dma_start(new[i], s1[HALVES[i]]).then_inc(s_stored, 16)
                sp.wait_ge(state_ok, NCH + 1)
                dst = io["ret_state_prompt"][0].rearrange("(pr two) d e -> two d pr e", two=2)
                for i in range(2):
                    sp.dma_start(dst[i], state[HALVES[i]]).then_inc(stored, 16)
                sp.wait_ge(stored, 32)
                sp.wait_ge(s_stored, 16 + 32 * NSEQ)

            @block.gpsimd
            def _(pool):
                nc.gpsimd.memset(qz[:], 0.0).then_inc(zeroed, 1)
                nc.gpsimd.memset(qd[:], 0.0).then_inc(zeroed, 1)
                with pool.Fori(0, NCH) as c:
                    src = g.br[:, 4:12, ds(c * P, P)]
                    pool.wait_ge(roped, c + 1)
                    pool.wait_ge(v_nat, c + 1)
                    pool.sem_inc(g.w.passed, 1)
                    nc.gpsimd.tensor_copy(stage[:], src).then_inc(staged, 1)

            @block.tensor
            def _(pe):
                pe.wait_ge(consts, 16 * len(names))
                with pe.Fori(0, NCH) as c:
                    pe.wait_ge(staged, c + 1)
                    nc.tensor.matmul(swap[:], rot[:], stage[:, 0:4, :], start=True, stop=True)
                    for h in range(H_R):
                        mm = nc.tensor.transpose(vt[:, h, :], stage[:, 4 + h, :], g.ident[:])
                    mm.then_inc(pe_swap, 1)
                    pe.wait_ge(roped, c + 2)
                    chunk_scores(P)
                    pe.wait_ge(masked, c + 1)
                    pe.wait_ge(v_nat, c + 2)
                    pe.wait_ge(state_ok, c + 1)
                    pe.wait_ge(o_read, c + 1)
                    for h in range(H_R):
                        nc.tensor.matmul(o[:, h, :], vn[:, h, :], at[:, h, :], start=True, stop=False)
                        nc.tensor.matmul(o[:, h, :], state[:, h // 2, :], qd[:, h % 2, h // 2, :],
                                         start=False, stop=True)
                    for h in range(H_R):
                        mm = nc.tensor.matmul(upd[:, h, :], kd[:, (h // 2) * P:(h // 2 + 1) * P], vn[:, h, :],
                                              start=True, stop=True)
                    mm.then_inc(pe_out, 1)
                nc.tensor.matmul(swap[:, :, 0:TS], rot[:], g.br[:, 4:8, TP:T], start=True, stop=True)
                for h in range(H_R):
                    mm = nc.tensor.transpose(vt[0:TS, h, :], g.br[:, 8 + h, TP:T], g.ident[:])
                mm.then_inc(pe_swap, 1)
                pe.wait_ge(roped, NCH + 2)
                chunk_scores(TS)
                pe.wait_ge(masked, NCH + 1)
                pe.wait_ge(v_nat, NCH + 2)
                for h in range(H_R):
                    nc.tensor.matmul(o_s[:, h, 0:TS], vn[0:TS, h, :], at[0:TS, h, 0:TS], start=(h == 0), stop=False,
                                     skip_group_check=True)
                with pe.Fori(0, NSEQ) as b:
                    pe.wait_ge(loaded, b * 32 + 32)
                    pe.wait_ge(s_masked, b + 1)
                    for h in range(H_R):
                        nc.tensor.matmul(o_s[:, h, 0:TS], s0[:, h // 2, :], qdm[:, h % 2, h // 2, :], start=False,
                                         stop=False, skip_group_check=True)
                    pe.wait_ge(s_new, b + 1)
                    for h in range(H_R):
                        mm = nc.tensor.matmul(upd[:, h, :], kdm[:, (h // 2) * P:(h // 2 + 1) * P], vn[0:TS, h, :],
                                              start=True, stop=True)
                    mm.then_inc(s_pe, 1)

            @block.scalar
            def _(act):
                with act.Fori(0, NCH) as c:
                    dst = g.br[:, 8:12, ds(c * P, P)]
                    act.wait_ge(pe_swap, c + 1)
                    nc.scalar.copy(vn[:], vt[:]).then_inc(v_nat, 1)
                    act.wait_ge(pe_out, c + 1)
                    nc.scalar.copy(dst, o[:]).then_inc(o_read, 1)
                act.wait_ge(pe_swap, NCH + 1)
                nc.scalar.copy(vn[0:TS], vt[0:TS]).then_inc(v_nat, 1)
                act.wait_ge(s_pe, NSEQ)
                nc.scalar.copy(g.br[:, 8:12, TP:T], o_s[:, :, 0:TS]).then_inc(o_read, 1)

            def masks(dve, mask, k_decay, n):
                nc.vector.tensor_tensor(at[0:n, :, 0:n], scores[0:n, :, 0:n], mask, ALU.mult)
                nc.vector.tensor_tensor(kd[0:n, :], kt[0:n].rearrange("p a b -> p (a b)"), k_decay, ALU.mult)\
                    .then_inc(masked, 1)

            def new_state(dst, old, dec, done):
                for h in range(H_R):
                    rows = HALVES[h % 2]
                    ins = nc.vector.scalar_tensor_tensor(dst[rows, h // 2, :], old[rows, h // 2, :], dec[h],
                                                         upd[rows, h, :], ALU.mult, ALU.add)
                ins.then_inc(done, 1)

            @block.vector
            def _(dve):
                dve.wait_ge(consts, 16 * len(names))
                nc.vector.memset(state[:], 0.0).then_inc(state_ok, 1)
                dve.wait_ge(zeroed, 2)
                with dve.Fori(0, NCH) as c:
                    t_cos, t_sin = cos[:, ds(c * P, P)], sin[:, ds(c * P, P)]
                    chain = Chain(steps, c * STEPS)
                    dve.wait_ge(staged, c + 1)
                    dve.wait_ge(pe_swap, c + 1)
                    rope(dve, chain, t_cos, t_sin, q_dec[:], P, stage[:, 0:4, :])
                    assert chain.n == STEPS
                    dve.wait_ge(pe_scores, c + 1)
                    masks(dve, dmask[:], k_dec[:], P)
                    dve.wait_ge(pe_out, c + 1)
                    dve.wait_ge(state_ok, c + 1)
                    new_state(state, state, dec_c, state_ok)
                chain = Chain(steps, NCH * STEPS)
                dve.wait_ge(pe_swap, NCH + 1)
                rope(dve, chain, cos[:, TP:T], sin[:, TP:T], q_dec_s[:], TS, g.br[:, 4:8, TP:T])
                dve.wait_ge(pe_scores, NCH + 1)
                masks(dve, dmask_s[:], k_dec_s[:], TS)
                dve.wait_ge(masked, NCH + 1)
                with dve.Fori(0, NSEQ) as b:
                    cols = seq_cols[:, ds(b, 1), :].broadcast_to([P, 4, TS])
                    row = seq_rows[:, ds(b, 1)]
                    nc.vector.tensor_tensor(qdm[:].rearrange("p s a t -> p (s a) t"),
                                            qd[:].rearrange("p s a t -> p (s a) t")[:, :, 0:TS], cols, ALU.mult)
                    nc.vector.tensor_scalar(kdm[:], kd[0:TS, :], row, None, ALU.mult).then_inc(s_masked, 1)
                    dve.wait_ge(s_pe, b + 1)
                    dve.wait_ge(s_stored, b * 32 + 16)
                    new_state(s1, s0, dec_s, s_new)


def phase_head_norm(g):
    nc = g.nc
    with ExitStack() as ctx:
        mean_w, eps = g.sb(ctx, "hn_mean_w", [P, P]), g.sb(ctx, "hn_eps", [P, 1])
        sq = [g.sb(ctx, f"hn_sq{s}", [P, TW]) for s in range(2)]
        std = [g.sb(ctx, f"hn_std{s}", [P, TW]) for s in range(2)]
        mean = g.ps(ctx, "hn_mean", [P, NB, 512])
        var = g.ps(ctx, "hn_var", [P, NB, 512])
        ready, mean_ok, centred, squared = g.sem("hn_ready"), g.sem("hn_mean_ok"), g.sem("hn_centred"), g.sem("hn_squared")
        var_ok, std_ok, steps = g.sem("hn_var_ok"), g.sem("hn_std_ok"), g.sem("hn_steps")
        with nc.Block() as block:
            @block.gpsimd
            def _(pool):
                nc.gpsimd.memset(mean_w[:], 1.0 / P).then_inc(ready, 1)
                nc.gpsimd.memset(eps[:], EPS).then_inc(ready, 1)

            @block.tensor
            def _(pe):
                pe.wait_ge(ready, 2)
                for h in range(H_R + 1):
                    if h < H_R:
                        if h > 0:
                            pe.wait_ge(centred, h)
                        for b in range(NB):
                            mm = nc.tensor.matmul(mean[:, b, 0:TB], mean_w[:], g.br[:, 8 + h, b * TB:(b + 1) * TB],
                                                  start=True, stop=True)
                        mm.then_inc(mean_ok, 1)
                    if h > 0:
                        pe.wait_ge(squared, h)
                        if h > 1:
                            pe.wait_ge(std_ok, h - 1)
                        for b in range(NB):
                            mm = nc.tensor.matmul(var[:, b, 0:TB], mean_w[:], sq[(h - 1) % 2][:, b * TB:(b + 1) * TB],
                                                  start=True, stop=True)
                        mm.then_inc(var_ok, 1)

            @block.scalar
            def _(act):
                act.wait_ge(ready, 2)
                for h in range(H_R):
                    act.wait_ge(centred, h + 1)
                    if h >= 2:
                        act.wait_ge(var_ok, h - 1)
                    nc.scalar.activation(sq[h % 2][:], g.br[:, 8 + h, :], ACT.Square).then_inc(squared, 1)
                    act.wait_ge(var_ok, h + 1)
                    if h >= 2:
                        act.wait_ge(steps, 3 * (h - 1))
                    nc.scalar.activation(blocks_of(std[h % 2][:]), var[:, :, 0:TB], ACT.Sqrt, bias=eps[:])\
                        .then_inc(std_ok, 1)

            @block.vector
            def _(dve):
                chain = Chain(steps)
                for h in range(H_R + 1):
                    if h < H_R:
                        row = blocks_of(g.br[:, 8 + h, :])
                        dve.wait_ge(mean_ok, h + 1)
                        nc.vector.tensor_tensor(row, row, mean[:, :, 0:TB], ALU.subtract).then_inc(centred, 1)
                    if h > 0:
                        s, x, y = std[(h - 1) % 2], g.br[:, 7 + h, :], g.br[:, h - 1, :]
                        dve.wait_ge(std_ok, h)
                        chain.mark(nc.vector.reciprocal(s[:], s[:]))
                        chain.wait(dve)
                        chain.mark(nc.vector.tensor_tensor(x, x, s[:], ALU.mult))
                        chain.wait(dve)
                        chain.mark(nc.vector.scalar_tensor_tensor(y, x, g.gn_g[:, h - 1:h], y, ALU.mult, ALU.mult))


def phase_attention_in(g):
    nc, io, w = g.nc, g.io, g.w
    fox, mq = 6, 2
    pairs = fox + mq
    with ExitStack() as ctx:
        w.open(ctx, "att")
        ga = g.sb(ctx, "ga", [H_F, TW])
        gb = g.negc
        lf = g.sb(ctx, "lf", [H_F, TW])
        acc = [g.ps(ctx, f"a_acc{s}", [P, NB, 512]) for s in range(2)]
        lfn_ps = g.ps(ctx, "lfn_ps", [P, NCH + 1, H_F])
        free = [g.sem(f"a_free{s}") for s in range(2)]
        steps, a_steps = g.sem("a_dve_steps"), g.sem("a_act_steps")
        turned, nat, stored, scanned = (g.sem(n) for n in ("lf_turned", "lf_nat", "lf_stored", "lf_scanned"))
        b0, b1 = w.n
        with nc.Block() as block:
            @block.sync
            def _(sp):
                for s in range(2):
                    sp.sem_inc(free[s], 1)
                w.load(sp, 0, b0, io["w_in"][:, C_FL:C_FL + P], KD)
                w.load(sp, 1, b1, io["w_in"][:, C_FQ:C_FQ + P], KD)
                with sp.Fori(1, 2 * fox // 2) as n:
                    w.load(sp, 0, n + b0, io["w_in"][:, ds(n * (2 * P) + (C_FQ - P), P)], KD)
                    w.load(sp, 1, n + b1, io["w_in"][:, ds(n * (2 * P) + C_FQ, P)], KD)
                w.load(sp, 0, fox + b0, io["w_in"][:, C_FQ + (2 * fox - 1) * P:C_FQ + 2 * fox * P], KD)
                w.load(sp, 1, fox + b1, io["w_in"][:, C_MQ:C_MQ + P], KD)
                with sp.Fori(1, mq) as n:
                    w.load(sp, 0, n + (fox + b0), io["w_in"][:, ds(n * (2 * P) + (C_MQ - P), P)], KD)
                    w.load(sp, 1, n + (fox + b1), io["w_in"][:, ds(n * (2 * P) + C_MQ, P)], KD)
                w.load(sp, 0, fox + mq + b0, io["w_in"][:, C_MQ + 3 * P:C_MQ + 4 * P], KD)
                sp.wait_ge(nat, 1)
                sp.dma_start(io["fox_logf_prompt"][0].rearrange("(c p) h -> p c h", p=P), g.lfn[:, 0:NCH, :],
                             allow_slow_non_contiguous=True).then_inc(stored, 16)
                sp.dma_start(io["fox_logf_sample"].rearrange("b t h -> (b t) h"), g.lfn[0:TS, NCH, :])\
                    .then_inc(stored, 16)
                sp.wait_ge(stored, 32)

            @block.gpsimd
            def _(pool):
                with pool.Fori(0, pairs) as n:
                    for s in range(2):
                        w.split(pool, s, n + (b0, b1)[s], KD)
                w.split(pool, 0, pairs + b0, KD)

            @block.tensor
            def _(pe):
                with pe.Fori(0, pairs) as n:
                    for s in range(2):
                        pe.wait_ge(free[s], n + 1)
                        w.products(pe, s, n + (b0, b1)[s], KD, acc[s], g.xh, g.xl)
                pe.wait_ge(free[0], pairs + 1)
                w.products(pe, 0, pairs + b0, KD, acc[0], g.xh, g.xl)
                pe.wait_ge(scanned, 1)
                for c in range(NCH + 1):
                    n = P if c < NCH else TS
                    mm = nc.tensor.transpose(lfn_ps[0:n, c, :], lf[:, c * P:c * P + n], g.ident[0:H_F, 0:H_F])
                mm.then_inc(turned, 1)

            @block.scalar
            def _(act):
                act.wait_ge(free[0], 2)
                chain = Chain(a_steps)
                chain.mark(nc.scalar.activation(gb[:], ga[:], ACT.Abs))
                chain.wait(act)
                chain.mark(nc.scalar.activation(gb[:], gb[:], ACT.Exp, scale=-1.0))
                chain.wait(act)
                chain.mark(nc.scalar.activation(gb[:], gb[:], ACT.Ln, bias=1.0))

                def read(n, dst, scale):
                    act.wait_ge(w.done[0], n + (b0 + 2))
                    nc.scalar.mul(dst, acc[0][:, :, 0:TB], scale).then_inc(free[0], 1)
                for n in range(1, 3):
                    read(n, blocks_of(g.br[:, 8 + 2 * n - 1, :]), DF ** -0.5)
                with act.Fori(3, 7) as n:
                    read(n, blocks_of(g.fkv[:, n * 2 - 5, :]), 1.0)
                for n in range(7, 9):
                    read(n, blocks_of(g.br[:, 4 + 2 * (n - fox) - 1, :]), 1.0)

            @block.vector
            def _(dve):
                chain = Chain(steps)
                dve.wait_ge(w.done[0], b0 + 2)
                nc.vector.tensor_scalar(blocks_of(ga[:]), acc[0][0:H_F, :, 0:TB], g.b_forget[:], None, ALU.add)\
                    .then_inc(free[0], 1)

                def read(n, dst, scale):
                    dve.wait_ge(w.done[1], n + (b1 + 2))
                    nc.vector.tensor_scalar(dst, acc[1][:, :, 0:TB], scale, None, ALU.mult).then_inc(free[1], 1)
                for n in range(2):
                    read(n, blocks_of(g.br[:, 8 + 2 * n, :]), DF ** -0.5)
                dve.wait_ge(a_steps, 3)
                chain.mark(nc.vector.scalar_tensor_tensor(lf[:], ga[:], 0.0, gb[:], ALU.min, ALU.subtract))
                chain.wait(dve)
                chain.mark(nc.vector.memset(ga[:], 1.0))
                chain.wait(dve)
                nc.vector.tensor_tensor_scan(gb[:, 0:TP], ga[:, 0:TP], lf[:, 0:TP], 0.0, ALU.mult, ALU.subtract)\
                    .then_inc(scanned, 1)
                with dve.Fori(2, 6) as n:
                    read(n, blocks_of(g.fkv[:, n * 2 - 4, :]), 1.0)
                for n in range(6, 8):
                    read(n, blocks_of(g.br[:, 4 + 2 * (n - fox), :]), 1.0)
                dve.wait_ge(turned, 1)
                nc.vector.tensor_copy(g.lfn[:, 0:NCH, :], lfn_ps[:, 0:NCH, :])
                nc.vector.tensor_copy(g.lfn[0:TS, NCH, :], lfn_ps[0:TS, NCH, :]).then_inc(nat, 1)
        w.n = [b0 + pairs + 1, b1 + pairs]


def phase_kv_natural(g):
    nc, io = g.nc, g.io
    with ExitStack() as ctx:
        stage = g.sb(ctx, "kv_stage", [P, 8, P])
        kn, vn = g.sb(ctx, "kv_kn", [P, 4, P]), g.sb(ctx, "kv_vn", [P, 4, P])
        kt, vt = g.ps(ctx, "kv_kt", [P, 4, P]), g.ps(ctx, "kv_vt", [P, 4, P])
        staged, turned, k_ok, v_ok = g.sem("kv_staged"), g.sem("kv_turned"), g.sem("kv_k_ok"), g.sem("kv_v_ok")
        k_out, v_out, placed = g.sem("kv_k_out"), g.sem("kv_v_out"), g.sem("kv_placed")
        with nc.Block() as block:
            @block.gpsimd
            def _(pool):
                nc.gpsimd.tensor_copy(g.k_s[:], g.fkv[:, 0:4, TP:T])
                with pool.Fori(0, NCH) as c:
                    src = g.fkv[:, :, ds(c * P, P)]
                    dst = g.fkv[:, 4:8, ds(c * P, P)]
                    pool.wait_ge(turned, c + 1)
                    pool.sem_inc(g.w.passed, 1)
                    nc.gpsimd.tensor_copy(stage[:], src).then_inc(staged, 1)
                    pool.wait_ge(v_ok, c + 2)
                    pool.sem_inc(g.w.passed, 1)
                    nc.gpsimd.tensor_copy(dst, vn[:]).then_inc(placed, 1)

            @block.tensor
            def _(pe):
                def turn(n, k_of, v_of):
                    for j in range(4):
                        nc.tensor.transpose(kt[0:n, j, :], k_of(j), g.ident[:])
                    for j in range(4):
                        mm = nc.tensor.transpose(vt[0:n, j, :], v_of(j), g.ident[:])
                    mm.then_inc(turned, 1)
                with pe.Fori(0, NCH) as c:
                    pe.wait_ge(staged, c + 1)
                    pe.wait_ge(k_ok, c + 1)
                    pe.wait_ge(v_ok, c + 1)
                    turn(P, lambda j: stage[:, j, :], lambda j: stage[:, 4 + j, :])
                pe.wait_ge(k_ok, NCH + 1)
                pe.wait_ge(v_ok, NCH + 1)
                turn(TS, lambda j: g.fkv[:, j, TP:T], lambda j: g.fkv[:, 4 + j, TP:T])

            @block.scalar
            def _(act):
                with act.Fori(0, NCH) as c:
                    act.wait_ge(turned, c + 2)
                    act.wait_ge(k_out, c * 16 + 16)
                    nc.scalar.copy(kn[:], kt[:]).then_inc(k_ok, 1)
                act.wait_ge(turned, NCH + 2)
                act.wait_ge(k_out, NCH * 16 + 16)
                nc.scalar.copy(kn[0:TS], kt[0:TS]).then_inc(k_ok, 1)

            @block.vector
            def _(dve):
                with dve.Fori(0, NCH) as c:
                    dve.wait_ge(turned, c + 2)
                    dve.wait_ge(v_out, c * 16 + 16)
                    dve.wait_ge(placed, c + 1)
                    nc.vector.tensor_copy(vn[:], vt[:]).then_inc(v_ok, 1)
                dve.wait_ge(turned, NCH + 2)
                nc.vector.tensor_copy(g.v_s[0:TS], vt[0:TS].rearrange("p a b -> p (a b)")).then_inc(v_ok, 1)

            @block.sync
            def _(sp):
                for sem in (turned, k_ok, v_ok, placed):
                    sp.sem_inc(sem, 1)
                sp.sem_inc(k_out, 16)
                sp.sem_inc(v_out, 16)
                with sp.Fori(0, NCH) as c:
                    k_dst = io["fox_k_prompt"][0, ds(c * P, P)].rearrange("t h d -> t (h d)")
                    v_dst = io["fox_v_prompt"][0, ds(c * P, P)].rearrange("t h d -> t (h d)")
                    sp.wait_ge(k_ok, c + 2)
                    sp.dma_start(k_dst, kn[:].rearrange("p a b -> p (a b)")).then_inc(k_out, 16)
                    sp.wait_ge(v_ok, c + 2)
                    sp.dma_start(v_dst, vn[:].rearrange("p a b -> p (a b)")).then_inc(v_out, 16)
                sp.wait_ge(k_ok, NCH + 2)
                sp.dma_start(io["fox_k_sample"].rearrange("b t h d -> (b t) (h d)"),
                             kn[0:TS].rearrange("p a b -> p (a b)")).then_inc(k_out, 16)
                sp.wait_ge(v_ok, NCH + 2)
                sp.dma_start(io["fox_v_sample"].rearrange("b t h d -> (b t) (h d)"), g.v_s[0:TS]).then_inc(v_out, 16)
                sp.wait_ge(k_out, 16 * (NCH + 2))
                sp.wait_ge(v_out, 16 * (NCH + 2))


def phase_cross(g):
    nc, io = g.nc, g.io
    MT = N_MEM // P
    scale = DM ** -0.5
    STEPS = 3
    with ExitStack() as ctx:
        q = g.sb(ctx, "c_q", [P, H_M, P])
        prob, pt = g.sb(ctx, "c_prob", [P, H_M, N_MEM]), g.sb(ctx, "c_pt", [P, H_M * MT, P])
        nmax, ssum, rsum = g.sb(ctx, "c_nmax", [P, H_M]), g.sb(ctx, "c_ssum", [P, H_M]), g.sb(ctx, "c_rsum", [P, H_M])
        kin, vin = g.sb(ctx, "c_kin", [P, MT, H_M * DM]), g.sb(ctx, "c_vin", [P, MT, H_M * DM])
        kts = g.sb(ctx, "c_kts", [P, H_M, N_MEM])
        sc = g.ps(ctx, "c_sc", [P, H_M, N_MEM])
        ptp = g.ps(ctx, "c_ptp", [P, H_M * MT, P])
        o = g.ps(ctx, "c_o", [P, H_M, P])
        ktp = g.ps(ctx, "c_ktp", [P, H_M, N_MEM])
        staged, scored, maxed, exped = g.sem("c_staged"), g.sem("c_scored"), g.sem("c_maxed"), g.sem("c_exped")
        normed, turned, pt_ok, out_ok = g.sem("c_normed"), g.sem("c_turned"), g.sem("c_pt_ok"), g.sem("c_out_ok")
        o_read, steps = g.sem("c_o_read"), g.sem("c_steps")
        loaded, k_turned, k_ok = g.sem("c_loaded"), g.sem("c_k_turned"), g.sem("c_k_ok")

        def block_pe(pe, i, n, kt, v):
            pe.wait_ge(staged, i + 1)
            for h in range(H_M):
                mm = nc.tensor.matmul(sc[0:n, h, :], q[:, h, 0:n], kt[:, h, :], start=True, stop=True)
            mm.then_inc(scored, 1)
            pe.wait_ge(normed, i + 1)
            pe.sem_inc(g.w.passed, 1)
            for h in range(H_M):
                for m in range(MT):
                    mm = nc.tensor.transpose(ptp[:, h * MT + m, 0:n], prob[0:n, h, m * P:(m + 1) * P],
                                             g.ident[0:n, 0:n])
            mm.then_inc(turned, 1)
            pe.wait_ge(pt_ok, i + 1)
            pe.wait_ge(o_read, i + 1)
            for h in range(H_M):
                for m in range(MT):
                    mm = nc.tensor.matmul(o[:, h, 0:n], v[:, m, h * DM:(h + 1) * DM], pt[:, h * MT + m, 0:n],
                                          start=(m == 0), stop=(m == MT - 1))
            mm.then_inc(out_ok, 1)

        def block_dve(dve, i, n):
            dve.wait_ge(scored, i + 1)
            chain = Chain(steps, i * STEPS)
            chain.mark(nc.vector.tensor_reduce(nmax[0:n], sc[0:n], AX.X, ALU.max))
            chain.wait(dve)
            nc.vector.tensor_scalar(nmax[0:n], nmax[0:n], -scale, None, ALU.mult).then_inc(maxed, 1)
            dve.wait_ge(exped, i + 1)
            chain.mark(nc.vector.reciprocal(rsum[0:n], ssum[0:n]))
            chain.wait(dve)
            nc.vector.tensor_tensor(prob[0:n], prob[0:n], rsum[0:n].unsqueeze(2).broadcast_to([n, H_M, N_MEM]),
                                    ALU.mult).then_inc(normed, 1)
            dve.wait_ge(turned, i + 1)
            chain.mark(nc.vector.tensor_copy(pt[:, :, 0:n], ptp[:, :, 0:n]))
            assert chain.n == STEPS
            chain.wait(dve)
            dve.sem_inc(pt_ok, 1)

        def block_act(act, i, n, dst):
            act.wait_ge(maxed, i + 1)
            for h in range(H_M):
                ins = nc.scalar.activation(prob[0:n, h, :], sc[0:n, h, :], ACT.Exp, bias=nmax[0:n, h:h + 1],
                                           scale=scale, accum_out=ssum[0:n, h:h + 1])
            ins.then_inc(exped, 1)
            act.wait_ge(out_ok, i + 1)
            nc.scalar.copy(dst, o[:, :, 0:n]).then_inc(o_read, 1)

        with nc.Block() as block:
            @block.sync
            def _(sp):
                sp.sem_inc(o_read, 1)
                sp.sem_inc(k_ok, 1)
                with sp.Fori(0, NSEQ) as b:
                    ks = io["cache_mem_k"][b].rearrange("(m p) h d -> p m (h d)", p=P)
                    vs = io["cache_mem_v"][b].rearrange("(m p) h d -> p m (h d)", p=P)
                    sp.wait_ge(k_ok, b + 1)
                    sp.dma_start(kin[:], ks).then_inc(loaded, 16)
                    sp.wait_ge(o_read, b + (NCH + 1))
                    sp.dma_start(vin[:], vs).then_inc(loaded, 16)

            @block.gpsimd
            def _(pool):
                with pool.Fori(0, NCH) as i:
                    src = g.br[:, 4:8, ds(i * P, P)]
                    pool.wait_ge(o_read, i + 1)
                    pool.sem_inc(g.w.passed, 1)
                    nc.gpsimd.tensor_copy(q[:], src).then_inc(staged, 1)
                with pool.Fori(0, NSEQ) as b:
                    src = g.br[:, 4:8, ds(b * LSEQ + TP, LSEQ)]
                    pool.wait_ge(o_read, b + (NCH + 1))
                    pool.sem_inc(g.w.passed, 1)
                    nc.gpsimd.tensor_copy(q[:, :, 0:LSEQ], src).then_inc(staged, 1)

            @block.tensor
            def _(pe):
                with pe.Fori(0, NCH) as i:
                    block_pe(pe, i, P, g.mem_kt, g.mem_v)
                with pe.Fori(0, NSEQ) as b:
                    pe.wait_ge(loaded, b * 32 + 32)
                    for h in range(H_M):
                        for m in range(MT):
                            mm = nc.tensor.transpose(ktp[:, h, m * P:(m + 1) * P], kin[:, m, h * DM:(h + 1) * DM],
                                                     g.ident[:])
                    mm.then_inc(k_turned, 1)
                    pe.wait_ge(k_ok, b + 2)
                    block_pe(pe, b + NCH, LSEQ, kts, vin)

            @block.scalar
            def _(act):
                act.preload_act_table(ACT.Exp)
                with act.Fori(0, NCH) as i:
                    block_act(act, i, P, g.br[:, 4:8, ds(i * P, P)])
                with act.Fori(0, NSEQ) as b:
                    dst = g.br[:, 4:8, ds(b * LSEQ + TP, LSEQ)]
                    act.wait_ge(k_turned, b + 1)
                    nc.scalar.copy(kts[:], ktp[:]).then_inc(k_ok, 1)
                    block_act(act, b + NCH, LSEQ, dst)

            @block.vector
            def _(dve):
                with dve.Fori(0, NCH) as i:
                    block_dve(dve, i, P)
                with dve.Fori(0, NSEQ) as b:
                    block_dve(dve, b + NCH, LSEQ)


def phase_fox_prompt(g):
    nc = g.nc
    with ExitStack() as ctx:
        qz = g.sb(ctx, "p_qz", [P, 2, P])
        prob = [g.sb(ctx, f"p_prob{s}", [P, TP]) for s in range(2)]
        pt = [g.sb(ctx, f"p_pt{s}", [P, NCH, P]) for s in range(2)]
        nmax, ssum, rsum = (g.sb(ctx, "p_" + n, [P, 2]) for n in ("nmax", "ssum", "rsum"))
        on = g.sb(ctx, "p_on", [P, 2, DF])
        row = g.sb(ctx, "p_row", [2, 2, P])
        negc = g.sb(ctx, "p_negc", [2, PAIRS, TP])
        sc = [g.ps(ctx, f"p_sc{s}", [P, TP]) for s in range(2)]
        ptp = g.ps(ctx, "p_ptp", [P, NCH, P])
        o = g.ps(ctx, "p_o", [P, 2, DF])
        ot = g.ps(ctx, "p_ot", [P, P])
        const, zero, staged = g.sem("p_const"), g.sem("p_zero"), g.sem("p_staged")
        scored = [g.sem(f"p_scored{s}") for s in range(2)]
        maxed = [g.sem(f"p_maxed{s}") for s in range(2)]
        exped = [g.sem(f"p_exped{s}") for s in range(2)]
        turned, pt_ok, pv_ok = g.sem("p_turned"), g.sem("p_pt_ok"), g.sem("p_pv_ok")
        recip, on_ok, ot_ok, placed = g.sem("p_recip"), g.sem("p_on_ok"), g.sem("p_ot_ok"), g.sem("p_placed")
        with nc.Block() as block:
            @block.sync
            def _(sp):
                sp.dma_start(row[:], g.io["pair_row"]).then_inc(const, 16)
                for s in range(2):
                    sp.dma_start(negc[s:s + 1, :, :], g.negc[s:H_F:2, 0:TP]).then_inc(const, 16)
                    sp.sem_inc(exped[s], 1)
                for sem in (scored[1], pt_ok, placed, on_ok, ot_ok):
                    sp.sem_inc(sem, 1)
                sp.sem_inc(turned, 2)
                sp.sem_inc(recip, 2)
                sp.wait_ge(const, 48)

            @block.gpsimd
            def _(pool):
                nc.gpsimd.memset(qz[:], 0.0).then_inc(zero, 1)
                pool.wait_ge(zero, 1)
                for i in range(NCH):
                    with pool.Fori(0, PAIRS) as p:
                        src = [g.br[HALVES[s], p + 8, i * P:(i + 1) * P] for s in range(2)]
                        t = i * PAIRS
                        pool.wait_ge(scored[1], p + (t + 1))
                        pool.sem_inc(g.w.passed, 1)
                        for s in range(2):
                            ins = nc.gpsimd.tensor_copy(qz[HALVES[s], s, :], src[s])
                        ins.then_inc(staged, 1)

            @block.tensor
            def _(pe):
                pe.wait_ge(const, 48)
                for i in range(NCH):
                    keys = (i + 1) * P
                    with pe.Fori(0, PAIRS) as p:
                        t = i * PAIRS
                        pe.wait_ge(staged, p + (t + 1))
                        for s in range(2):
                            pe.wait_ge(exped[s], p + (t + 1))
                            for k0 in range(0, keys, 512):
                                k1 = min(k0 + 512, keys)
                                nc.tensor.matmul(sc[s][:, k0:k1], qz[:, s, :], g.fkv[:, p, k0:k1],
                                                 start=True, stop=False)
                                mm = nc.tensor.matmul(sc[s][:, k0:k1], row[:, s, :], negc[:, p, k0:k1],
                                                      start=False, stop=(k1 < keys))
                            mm = nc.tensor.matmul(sc[s][:, i * P:keys], g.ident[:], g.causal[:],
                                                  start=False, stop=True)
                            mm.then_inc(scored[s], 1)
                        for s in range(2):
                            n = (p + t) * 2 + s
                            pe.wait_ge(exped[s], p + (t + 2))
                            pe.wait_ge(pt_ok, n + 1)
                            for k in range(i + 1):
                                mm = nc.tensor.transpose(ptp[:, k, :], prob[s][:, k * P:(k + 1) * P], g.ident[:])
                            mm.then_inc(turned, 1)
                            pe.wait_ge(pt_ok, n + 2)
                            if s == 0:
                                pe.wait_ge(on_ok, p + (t + 1))
                            for k in range(i + 1):
                                v = g.fkv[:, p + 4, k * P + s * DF:k * P + (s + 1) * DF]
                                mm = nc.tensor.matmul(o[:, s, :], pt[s][:, k, :], v, start=(k == 0), stop=(k == i))
                            mm.then_inc(pv_ok, 1)
                        pe.wait_ge(on_ok, p + (t + 2))
                        pe.wait_ge(placed, p + (t + 1))
                        nc.tensor.transpose(ot[:], on[:].rearrange("p a b -> p (a b)"), g.ident[:]).then_inc(ot_ok, 1)

            @block.scalar
            def _(act):
                act.preload_act_table(ACT.Exp)
                for i in range(NCH):
                    keys = (i + 1) * P
                    with act.Fori(0, PAIRS) as p:
                        t = i * PAIRS
                        dst = g.br[:, p + 8, i * P:keys]
                        for s in range(2):
                            act.wait_ge(maxed[s], p + (t + 1))
                            act.wait_ge(turned, (p + t) * 2 + (s + 1))
                            act.wait_ge(recip, (p + t) * 2 + (s + 1))
                            nc.scalar.activation(prob[s][:, 0:keys], sc[s][:, 0:keys], ACT.Exp, bias=nmax[:, s:s + 1],
                                                 accum_out=ssum[:, s:s + 1]).then_inc(exped[s], 1)
                        act.wait_ge(ot_ok, p + (t + 2))
                        nc.scalar.copy(dst, ot[:]).then_inc(placed, 1)

            @block.vector
            def _(dve):
                for i in range(NCH):
                    keys = (i + 1) * P
                    with dve.Fori(0, PAIRS) as p:
                        t = i * PAIRS
                        for s in range(2):
                            dve.wait_ge(scored[s], p + (t + (2 if s else 1)))
                            dve.wait_ge(exped[s], p + (t + 1))
                            nc.vector.tensor_reduce(nmax[:, s:s + 1], sc[s][:, 0:keys], AX.X, ALU.max, negate=True)\
                                .then_inc(maxed[s], 1)
                        for s in range(2):
                            n = (p + t) * 2 + s
                            dve.wait_ge(exped[s], p + (t + 2))
                            nc.vector.reciprocal(rsum[:, s:s + 1], ssum[:, s:s + 1]).then_inc(recip, 1)
                            dve.wait_ge(turned, n + 3)
                            nc.vector.tensor_copy(pt[s][:, 0:i + 1, :], ptp[:, 0:i + 1, :]).then_inc(pt_ok, 1)
                        dve.wait_ge(recip, (p + t) * 2 + 4)
                        dve.wait_ge(ot_ok, p + (t + 1))
                        dve.wait_ge(pv_ok, (p + t) * 2 + 2)
                        nc.vector.tensor_tensor(on[:], o[:], rsum[:].unsqueeze(2).broadcast_to([P, 2, DF]), ALU.mult)\
                            .then_inc(on_ok, 1)


QUAD = 4
CHUNK = 8
ROWS = 32
NEW = PAST + TS


def phase_sample_bias(g, qz, bias_n, bias_past):
    nc, io = g.nc, g.io
    HG = NPG // 2
    with ExitStack() as ctx:
        idx = g.sb(ctx, "d_idx", [P, 2], I32)
        rows = [g.sb(ctx, f"d_rows{j}", [P, PAGE * H_F]) for j in range(2)]
        lft = g.sb(ctx, "d_lft", [P, NSEQ, NPG, H_F])
        tot = [g.sb(ctx, f"d_tot{s}", [P, NSEQ, NPG + 1, H_F]) for s in range(2)]
        after, upto = g.sb(ctx, "d_after", [P, P]), g.sb(ctx, "d_upto", [TS, TS])
        mask, lfx = g.sb(ctx, "d_mask", [P, NSEQ, TS]), g.sb(ctx, "d_lfx", [TS, PAIRS, 4, LSEQ])
        out = g.sb(ctx, "d_out", [P, 2 * NSEQ, P])
        t = [g.ps(ctx, f"d_t{j}", [P, H_F, P]) for j in range(2)]
        sums = g.ps(ctx, "d_sums", [P, NSEQ, P])
        cn = g.ps(ctx, "d_cn", [P, TS])
        const, paged, turned, copied = g.sem("d_const"), g.sem("d_paged"), g.sem("d_turned"), g.sem("d_copied")
        steps, summed, read, stored = g.sem("d_steps"), g.sem("d_summed"), g.sem("d_read"), g.sem("d_stored")
        expanded, cn_ok, qz_ok = g.sem("d_expanded"), g.sem("d_cn_ok"), g.sem("d_qz_ok")
        indexed = g.sem("d_indexed")
        with nc.Block() as block:
            @block.sync
            def _(sp):
                sp.dma_start(idx[:], io["page_table"].rearrange("b n -> (b n)").rearrange("(j p) -> p j", p=P),
                             allow_slow_non_contiguous=True).then_inc(indexed, 16)
                for name, dst in (("after", after), ("upto", upto), ("new_mask", mask)):
                    sp.dma_start(dst[:], io[name]).then_inc(const, 16)
                sp.wait_ge(const, 48)
                for x in range(2):
                    sp.wait_ge(read, x + 1)
                    c = slice(x * NSEQ, (x + 1) * NSEQ)
                    sp.dma_start(bias_past[c].rearrange("c g h t -> (g h) c t"), out[:, c, :]).then_inc(stored, 16)
                sp.wait_ge(stored, 32)

            @block.gpsimd
            def _(pool):
                pool.wait_ge(indexed, 16)
                gates = io["cache_fox_logf"].rearrange("n t h -> n (t h)")
                for j in range(2):
                    nc.gpsimd.indirect_dma_start(out=rows[j][:], out_offset=None, in_=gates,
                                                 in_offset=bass.IndirectOffsetOnAxis(ap=idx[:, j:j + 1], axis=0))\
                        .then_inc(paged, 16)
                nc.gpsimd.memset(qz[:], 0.0).then_inc(qz_ok, 1)
                pool.wait_ge(qz_ok, 1)
                pool.wait_ge(paged, 32)
                q = g.br[:, 8:12, TP:T].rearrange("p a (b q) -> p b a q", q=LSEQ)
                for b in range(NSEQ):
                    for s in range(2):
                        nc.gpsimd.tensor_copy(qz[HALVES[s], b, :, s * LSEQ:(s + 1) * LSEQ], q[HALVES[s], b])

            @block.tensor
            def _(pe):
                pe.wait_ge(paged, 32)
                for j in range(2):
                    by_head = rows[j][:].rearrange("p (t h) -> p h t", h=H_F)
                    for h in range(H_F):
                        mm = nc.tensor.transpose(t[j][:, h, :], by_head[:, h, :], g.ident[:])
                    mm.then_inc(turned, 1)
                pe.wait_ge(const, 48)
                pe.wait_ge(expanded, 2)
                nc.tensor.matmul(cn[:], lfx[:].rearrange("p a s q -> p (a s q)"), upto[:], start=True, stop=True)\
                    .then_inc(cn_ok, 1)
                pe.wait_ge(copied, 2)
                pe.wait_ge(steps, 6)
                for c in range(2 * NSEQ):
                    if c == NSEQ:
                        pe.wait_ge(read, 1)
                    b, x = divmod(c, 2)
                    own = lft[:, b, x * HG:(x + 1) * HG, :].rearrange("p g h -> p (g h)")
                    behind = tot[1][:, b, x * HG + 1:(x + 1) * HG + 1, :].rearrange("p g h -> p (g h)")
                    nc.tensor.matmul(sums[:, c % NSEQ, :], own, after[:], start=True, stop=False)
                    mm = nc.tensor.matmul(sums[:, c % NSEQ, :], behind, g.ones[:], start=False, stop=True)
                    if c % NSEQ == NSEQ - 1:
                        mm.then_inc(summed, 1)

            @block.scalar
            def _(act):
                for j in range(2):
                    act.wait_ge(turned, j + 1)
                    nc.scalar.copy(lft[:, j * 4:j * 4 + 4].rearrange("p b g h -> p h (b g)"), t[j][:])\
                        .then_inc(copied, 1)
                for x in range(2):
                    act.wait_ge(summed, x + 1)
                    nc.scalar.copy(out[:, x * NSEQ:(x + 1) * NSEQ, :], sums[:]).then_inc(read, 1)

            @block.vector
            def _(dve):
                chain = Chain(steps)
                nc.vector.memset(lfx[:], 0.0).then_inc(expanded, 1)
                nc.vector.memset(g.v_s[TS:P, :], 0.0)
                for s in range(2):
                    nc.vector.memset(tot[s][:, :, NPG, :], 0.0)
                dve.wait_ge(expanded, 1)
                nc.vector.tensor_copy(lfx[:, :, 0:2, :],
                                      g.lfn[0:TS, NCH, :].rearrange("p (a s) -> p a s", s=2).unsqueeze(3)
                                      .broadcast_to([TS, PAIRS, 2, LSEQ])).then_inc(expanded, 1)
                dve.wait_ge(copied, 2)
                chain.mark(nc.vector.tensor_copy(tot[0][:, :, 0:NPG, :].rearrange("p b g h -> p b (g h)"),
                                                 lft[:].rearrange("p b g h -> p b (g h)")))
                chain.wait(dve)
                now, step = 0, 1
                while step < NPG:
                    x, y = tot[now], tot[1 - now]
                    nc.vector.tensor_tensor(y[:, :, 0:NPG - step, :].rearrange("p b g h -> p b (g h)"),
                                            x[:, :, 0:NPG - step, :].rearrange("p b g h -> p b (g h)"),
                                            x[:, :, step:NPG, :].rearrange("p b g h -> p b (g h)"), ALU.add)
                    chain.mark(nc.vector.tensor_copy(y[:, :, NPG - step:NPG, :], x[:, :, NPG - step:NPG, :]))
                    chain.wait(dve)
                    now, step = 1 - now, step * 2
                assert now == 1 and chain.n == 6
                dve.wait_ge(const, 48)
                dve.wait_ge(cn_ok, 1)
                nc.vector.tensor_tensor(bias_n[:], mask[:], cn[:].unsqueeze(1).broadcast_to([P, NSEQ, TS]), ALU.subtract)


def phase_fox_sample(g, qz, bias_n, bias_past):
    nc, io = g.nc, g.io
    QUADS = NPG // QUAD
    CHUNKS = NPG // CHUNK
    Q_V = QUADS + 1
    USED = PAIRS * (NPG + 1)
    with ExitStack() as ctx:
        kt, pt = g.mem_kt, g.mem_v
        kt = [kt[:, 2 * s:2 * s + 2, :].rearrange("p a (b k) -> p (a b) k", k=P) for s in range(2)]
        pt = [pt[:, s, :].rearrange("p (a k) -> p a k", k=P) for s in range(2)]
        st = [g.sb(ctx, f"d_st{s}", [P, PAST + P]) for s in range(2)]
        k_in = [g.sb(ctx, f"d_k_in{s}", [P, H_F * DF]) for s in range(CHUNK)]
        v_in = [g.sb(ctx, f"d_v_in{s}", [P, H_F * DF]) for s in range(CHUNK)]
        q_now = [g.sb(ctx, f"d_q{s}", [P, PAIRS, ROWS]) for s in range(2)]
        tops, nmax = g.sb(ctx, "d_tops", [P, QUADS + 1]), g.sb(ctx, "d_nmax", [P, 1])
        parts, rsum = g.sb(ctx, "d_parts", [P, CHUNKS + 1]), g.sb(ctx, "d_rsum", [P, 1])
        on, o_t = g.sb(ctx, "d_on", [P, P]), g.sb(ctx, "d_o_t", [P, PAIRS, LSEQ])
        ktp = [g.ps(ctx, f"d_ktp{s}", [P, PAIRS, P]) for s in range(2)]
        stp = [g.ps(ctx, f"d_stp{s}", [P, QUAD * P]) for s in range(2)]
        ptp = [g.ps(ctx, f"d_ptp{s}", [P, QUAD, P]) for s in range(2)]
        ov = g.ps(ctx, "d_ov", [P, P])
        misc = g.ps(ctx, "d_misc", [P, 512])
        stn, ot = misc[:, 0:TS], misc[:, P:2 * P]
        k_in_ok = [g.sem(f"d_k_in_ok{s}") for s in range(CHUNK)]
        v_in_ok = [g.sem(f"d_v_in_ok{s}") for s in range(CHUNK)]
        k_turned = g.sem("d_k_turned")
        kt_ok = g.sem("d_kt_ok")
        scored = g.sem("d_scored")
        added = g.sem("d_added")
        topped = g.sem("d_topped")
        new_scored, new_st, max_ok = g.sem("d_new_scored"), g.sem("d_new_st"), g.sem("d_max_ok")
        exped = g.sem("d_exped")
        pturned = g.sem("d_pturned")
        pt_ok = g.sem("d_pt_ok")
        valued = g.sem("d_valued")
        q_ok = g.sem("d_q_ok")
        biased = [g.sem(f"d_biased{s}") for s in range(2)]
        on_ok, ot_ok, out_ok, steps = g.sem("d_on_ok"), g.sem("d_ot_ok"), g.sem("d_out_ok"), g.sem("d_steps2")
        zeroed = g.sem("d_zeroed")

        def sweep(engine, first, body):
            first()
            with engine.Fori(0, NSEQ // 2 - 1) as j:
                for e in range(2):
                    body(j * 2 + e, e, j, True)
            body(NSEQ - 2, 0, NSEQ // 2 - 1, True)
            body(NSEQ - 1, 1, NSEQ // 2 - 1, False)

        with nc.Block() as block:
            @block.sync
            def _(sp):
                sp.sem_inc(k_turned, CHUNK)
                sp.sem_inc(kt_ok, 2)
                sp.sem_inc(scored, 8)
                sp.sem_inc(added, 2)
                sp.sem_inc(pturned, 2 * Q_V)
                sp.sem_inc(pt_ok, 2)
                sp.sem_inc(valued, 40)
                sp.sem_inc(on_ok, 1)
                sp.sem_inc(out_ok, 1)
                cache = io["cache_fox_k"]
                with sp.Fori(0, NSEQ * CHUNKS) as c:
                    _, pages = nc.values_load_multi_w_load_instructions(
                        g.pages[0:1, ds(c * CHUNK, CHUNK)], engines=(mybir.EngineType.SP,), min_val=0,
                        max_val=cache.shape[0] - 1)
                    for s in range(CHUNK):
                        src = cache[pages[s]].rearrange("t h d -> t (h d)")
                        sp.wait_ge(k_turned, c * CHUNK + (s + 1))
                        sp.dma_start(k_in[s][:], src).then_inc(k_in_ok[s], 16)

            @block.gpsimd
            def _(pool):
                cache = io["cache_fox_v"]
                def start(b, e):
                    dst = st[e][:, 0:PAST].rearrange("p (g t) -> p g t", t=PAGE)
                    src_q = qz[:, b] if isinstance(b, int) else qz[:, ds(b, 1)].rearrange("p o a q -> p (o a) q")
                    pool.wait_ge(pturned, b * Q_V + Q_V)
                    pool.sem_inc(g.w.passed, 1)
                    nc.gpsimd.tensor_copy(q_now[e][:], src_q).then_inc(q_ok, 1)
                    for h in range(H_F):
                        row = ROWS * (h // 2) + LSEQ * (h % 2)
                        src = bias_past[ds(b * 2, 2), :, h].rearrange("x g t -> (x g) t").unsqueeze(0)\
                            .broadcast_to([LSEQ, NPG, PAGE])
                        pool.dma_start(dst[row:row + LSEQ], src).then_inc(biased[e], 16)

                def values(b):
                    for r in range(CHUNKS):
                        _, pages = nc.values_load_multi_w_load_instructions(
                            g.pages[0:1, ds(b * NPG + r * CHUNK, CHUNK)], engines=(mybir.EngineType.Pool,), min_val=0,
                            max_val=cache.shape[0] - 1)
                        for s in range(CHUNK):
                            src = cache[pages[s]].rearrange("t h d -> t (h d)")
                            at = 4 * s + 8 if r == 0 else 40 + PAIRS * ((r - 1) * CHUNK + s + 1)
                            pool.wait_ge(valued, b * USED + at)
                            pool.dma_start(v_in[s][:], src).then_inc(v_in_ok[s], 16)

                for s in range(2):
                    nc.gpsimd.memset(st[s][:], 0.0).then_inc(zeroed, 1)
                pool.wait_ge(zeroed, 2)
                start(0, 0)
                with pool.Fori(0, NSEQ // 2 - 1) as j:
                    for e in range(2):
                        start(j * 2 + e + 1, 1 - e)
                        values(j * 2 + e)
                start(NSEQ - 1, 1)
                values(NSEQ - 2)
                values(NSEQ - 1)

            @block.tensor
            def _(pe):
                def turn(b, i):
                    s, c = i % CHUNK, i // CHUNK
                    pe.wait_ge(k_in_ok[s], b * (16 * CHUNKS) + 16 * (c + 1))
                    pe.wait_ge(kt_ok, b * NPG + (i + 1))
                    for p in range(PAIRS):
                        mm = nc.tensor.transpose(ktp[i % 2][:, p, :], k_in[s][:, p * P:(p + 1) * P], g.ident[:])
                    mm.then_inc(k_turned, 1)

                def keys(b, e, r):
                    for i in range(r * CHUNK, (r + 1) * CHUNK):
                        if i % CHUNK == 0:
                            turn(b, i)
                        if (i + 1) % CHUNK:
                            turn(b, i + 1)
                        if i % QUAD == 0:
                            pe.wait_ge(added, b * QUADS + (i // QUAD + 1))
                        pe.wait_ge(kt_ok, b * NPG + (i + 3))
                        for p in range(PAIRS):
                            nc.tensor.matmul(stp[i // QUAD % 2][p * ROWS:(p + 1) * ROWS, i % QUAD * P:(i % QUAD + 1) * P],
                                             q_now[e][:, p, :], kt[i % 2][:, p, :], start=True, stop=True)\
                                .then_inc(scored, 1)

                def new_keys(b, e):
                    for p in range(PAIRS):
                        nc.tensor.matmul(stn[p * ROWS:(p + 1) * ROWS, :], q_now[e][:, p, :], g.k_s[:, p, :],
                                         start=True, stop=True).then_inc(new_scored, 1)

                def turn_probs(b, e, u):
                    pe.wait_ge(exped, b * (CHUNKS + 1) + (u * QUAD // CHUNK + 1))
                    pe.wait_ge(pt_ok, b * Q_V + (u + 1))
                    for k in range(QUAD if u < QUADS else 1):
                        at = (u * QUAD + k) * P
                        mm = nc.tensor.transpose(ptp[u % 2][:, k, :], st[e][:, at:at + P], g.ident[:])
                    mm.then_inc(pturned, 1)

                def products(b, u):
                    pe.wait_ge(pt_ok, b * Q_V + (u + 3))
                    for k in range(QUAD if u < QUADS else 1):
                        i = u * QUAD + k
                        if u < QUADS:
                            pe.wait_ge(v_in_ok[i % CHUNK], b * (16 * CHUNKS) + 16 * (i // CHUNK + 1))
                        v = v_in[i % CHUNK] if u < QUADS else g.v_s
                        for p in range(PAIRS):
                            nc.tensor.matmul(ov[p * ROWS:(p + 1) * ROWS, :], pt[u % 2][:, k, p * ROWS:(p + 1) * ROWS],
                                             v[:, p * P:(p + 1) * P], start=(i == 0), stop=(u == QUADS),
                                             skip_group_check=True).then_inc(valued, 1)

                def first():
                    pe.wait_ge(q_ok, 1)
                    for r in range(CHUNKS):
                        keys(0, 0, r)
                    new_keys(0, 0)

                def body(b, e, half, more):
                    if more:
                        pe.wait_ge(q_ok, b + 2)
                    for r in range(CHUNKS):
                        if more:
                            keys(b + 1, 1 - e, r)
                        if r == 0:
                            pe.wait_ge(on_ok, b + 1)
                        for u in (2 * r, 2 * r + 1):
                            turn_probs(b, e, u)
                        for u in (2 * r, 2 * r + 1):
                            products(b, u)
                    if more:
                        pe.wait_ge(out_ok, b + 1)
                        new_keys(b + 1, 1 - e)
                    turn_probs(b, e, QUADS)
                    products(b, QUADS)
                    pe.wait_ge(on_ok, b + 2)
                    nc.tensor.transpose(ot, on[:], g.ident[:]).then_inc(ot_ok, 1)
                sweep(pe, first, body)

            @block.scalar
            def _(act):
                act.preload_act_table(ACT.Exp)

                def keys(b, m):
                    for i in range(m * QUAD, (m + 1) * QUAD):
                        act.wait_ge(k_turned, b * NPG + (i + 1 + CHUNK))
                        act.wait_ge(scored, b * (4 * NPG) + (4 * i + 4))
                        nc.scalar.copy(kt[i % 2], ktp[i % 2]).then_inc(kt_ok, 1)

                def probs(b, e, piece):
                    c0 = piece * CHUNK * P
                    c1 = min(c0 + CHUNK * P, NEW)
                    nc.scalar.activation(st[e][:, c0:c1], st[e][:, c0:c1], ACT.Exp, bias=nmax[:],
                                         accum_out=parts[:, piece:piece + 1]).then_inc(exped, 1)

                def body(b, e, half, more):
                    for m in range(QUADS):
                        if more:
                            keys(b + 1, m)
                        if m == 0:
                            act.wait_ge(max_ok, b + 1)
                            act.wait_ge(on_ok, b + 1)
                        if m <= CHUNKS:
                            probs(b, e, m)

                def first():
                    for m in range(QUADS):
                        keys(0, m)
                sweep(act, first, body)

            @block.vector
            def _(dve):
                STEPS = 1

                def keys(b, e, half, m):
                    cols = st[e][:, m * QUAD * P:(m + 1) * QUAD * P]
                    if m == 0:
                        dve.wait_ge(biased[e], half * (16 * H_F) + 16 * H_F)
                    dve.wait_ge(scored, b * (4 * NPG) + ((m + 1) * 16 + 8))
                    nc.vector.tensor_tensor(cols, cols, stp[m % 2][:], ALU.add).then_inc(added, 1)
                    dve.wait_ge(added, b * QUADS + (m + 3))
                    nc.vector.tensor_reduce(tops[:, m:m + 1], cols, AX.X, ALU.max).then_inc(topped, 1)

                def maximum(b, e):
                    bn = bias_n[:, b] if isinstance(b, int) else bias_n[:, ds(b, 1)].rearrange("p o k -> p (o k)")
                    dve.wait_ge(new_scored, b * PAIRS + PAIRS)
                    nc.vector.tensor_tensor(st[e][:, PAST:NEW], stn, bn, ALU.add).then_inc(new_st, 1)
                    dve.wait_ge(new_st, b + 1)
                    nc.vector.tensor_reduce(tops[:, QUADS:QUADS + 1], st[e][:, PAST:NEW], AX.X, ALU.max)\
                        .then_inc(topped, 1)
                    dve.wait_ge(topped, b * (QUADS + 1) + (QUADS + 1))
                    nc.vector.tensor_reduce(nmax[:], tops[:], AX.X, ALU.max, negate=True).then_inc(max_ok, 1)
                    dve.wait_ge(max_ok, b + 1)

                def probs(b, u):
                    at = 36 if u == 0 else 40 + 16 * (u - 1)
                    n = QUAD if u < QUADS else 1
                    dve.wait_ge(pturned, b * Q_V + (u + 1 + 2 * Q_V))
                    dve.wait_ge(valued, b * USED + at)
                    nc.vector.tensor_copy(pt[u % 2][:, 0:n], ptp[u % 2][:, 0:n]).then_inc(pt_ok, 1)

                def first():
                    for m in range(QUADS):
                        keys(0, 0, 0, m)
                    maximum(0, 0)

                def body(b, e, half, more):
                    for r in range(CHUNKS):
                        for x in range(2):
                            if more:
                                keys(b + 1, 1 - e, half + e, 2 * r + x)
                        for x in range(2):
                            probs(b, 2 * r + x)
                    probs(b, QUADS)
                    dve.wait_ge(exped, b * (CHUNKS + 1) + (CHUNKS + 1))
                    if more:
                        maximum(b + 1, 1 - e)
                    dst = g.br[:, 8:12, ds(b * LSEQ + TP, LSEQ)]
                    chain = Chain(steps, b * 3)
                    chain.mark(nc.vector.tensor_reduce(rsum[:], parts[:], AX.X, ALU.add))
                    chain.wait(dve)
                    chain.mark(nc.vector.reciprocal(rsum[:], rsum[:]))
                    chain.wait(dve)
                    dve.wait_ge(valued, b * USED + (USED + 40))
                    nc.vector.tensor_scalar(on[:], ov[:], rsum[:], None, ALU.mult).then_inc(on_ok, 1)
                    dve.wait_ge(ot_ok, b + 1)
                    for s in range(2):
                        src = ot[HALVES[s], :].rearrange("p (a s q) -> p a s q", s=4, q=LSEQ)[:, :, s, :]
                        ins = nc.vector.tensor_copy(o_t[HALVES[s]], src)
                    chain.mark(ins)
                    chain.wait(dve)
                    nc.vector.tensor_copy(dst, o_t[:]).then_inc(out_ok, 1)
                    dve.wait_ge(out_ok, b + 2)
                sweep(dve, first, body)


def phase_mix(g, mix):
    nc, io, w = g.nc, g.io, g.w
    KB = 4
    outs = ("w_ret_o", "w_fox_o", "w_mem_o")
    tiles = (0, 8, 4)
    with ExitStack() as ctx:
        w.open(ctx, "mix")
        raw = [g.sb(ctx, f"mo_raw{i}", [P, KB, P]) for i in range(3)]
        gate = [g.sb(ctx, f"mo_gate{i}", [P, TW]) for i in range(2)]
        part = g.sb(ctx, "mo_part", [P, TW])
        acc = [g.ps(ctx, f"mo_acc{s}", [P, NB, 512]) for s in range(2)]
        raw_ok = [g.sem(f"mo_raw_ok{i}") for i in range(3)]
        branch, gated, mixed, steps = g.sem("mo_branch"), g.sem("mo_gated"), g.sem("mo_mixed"), g.sem("mo_steps")
        b0, b1 = w.n
        with nc.Block() as block:
            @block.sync
            def _(sp):
                sp.sem_inc(gated, 1)
                sp.sem_inc(mixed, 1)
                sp.sem_inc(branch, 3)
                with sp.Fori(0, KD // 2) as jj:
                    for u in range(6):
                        x, i = divmod(u, 3)
                        s = u % 2
                        w_src = io["w_in"][:, ds(jj * (2 * P) + (C_GATE + i * D + x * P), P)]
                        o_src = io[outs[i]][:, ds(jj * (2 * P) + x * P, P)].rearrange("(k p) c -> p k c", p=P)
                        w.load(sp, s, jj * 3 + (u // 2 + (b0, b1)[s]), w_src, KD)
                        sp.wait_ge(branch, jj * 6 + (u + 1))
                        sp.sem_inc(g.w.passed, 1)
                        sp.dma_start(raw[i][:], o_src).then_inc(raw_ok[i], 16)

            @block.gpsimd
            def _(pool):
                with pool.Fori(0, KD // 2) as jj:
                    for u in range(6):
                        s = u % 2
                        w.split(pool, s, jj * 3 + (u // 2 + (b0, b1)[s]), KD)

            @block.tensor
            def _(pe):
                with pe.Fori(0, KD // 2) as jj:
                    for u in range(6):
                        x, i = divmod(u, 3)
                        s = u % 2
                        pe.wait_ge(gated, jj * 6 + (u + 1))
                        w.products(pe, s, jj * 3 + (u // 2 + (b0, b1)[s]), KD, acc[0], g.xh, g.xl)
                        pe.wait_ge(raw_ok[i], jj * 32 + (x * 16 + 16))
                        pe.wait_ge(mixed, jj * 6 + (u + 1))
                        for k in range(KB):
                            for b in range(NB):
                                mm = nc.tensor.matmul(acc[1][:, b, 0:TB], raw[i][:, k, :],
                                                      g.br[:, tiles[i] + k, b * TB:(b + 1) * TB],
                                                      start=(k == 0), stop=(k == KB - 1))
                        mm.then_inc(branch, 1)

            @block.scalar
            def _(act):
                act.preload_act_table(ACT.Sigmoid)
                with act.Fori(0, KD // 2) as jj:
                    for u in range(6):
                        x, i = divmod(u, 3)
                        s = u % 2
                        bias = g.b_gate[:, i, ds(jj * 2 + x, 1)]
                        act.wait_ge(w.done[s], jj * 3 + (u // 2 + 2 + (b0, b1)[s]))
                        if u >= 2:
                            act.wait_ge(mixed, jj * 6 + u)
                        else:
                            act.wait_ge(mixed, jj * 6 + 1)
                        nc.scalar.activation(blocks_of(gate[s][:]), acc[0][:, :, 0:TB], ACT.Sigmoid, bias=bias)\
                            .then_inc(gated, 1)

            @block.vector
            def _(dve):
                with dve.Fori(0, KD // 2) as jj:
                    for u in range(6):
                        x, i = divmod(u, 3)
                        s = u % 2
                        row = mix[:, jj * 2 + x, :]
                        out = row if i == 0 else part[:]
                        dve.wait_ge(gated, jj * 6 + (u + 2))
                        dve.wait_ge(branch, jj * 6 + (u + 4))
                        nc.vector.tensor_tensor(blocks_of(out), blocks_of(gate[s][:]), acc[1][:, :, 0:TB], ALU.mult)\
                            .then_inc(mixed, 1)
                        dve.wait_ge(mixed, jj * 6 + (u + 2))
                        if i:
                            nc.vector.tensor_tensor(row, row, part[:], ALU.add).then_inc(steps, 1)
                            dve.wait_ge(steps, jj * 4 + (x * 2 + i))
        w.n = [b0 + 3 * KD // 2, b1 + 3 * KD // 2]


def phase_out(g, mix):
    nc, io = g.nc, g.io
    with ExitStack() as ctx:
        raw = [g.sb(ctx, f"o_raw{s}", [P, KD, P]) for s in range(2)]
        acc = [g.ps(ctx, f"o_acc{s}", [P, NB, 512]) for s in range(2)]
        loaded = [g.sem(f"o_loaded{s}") for s in range(2)]
        done = [g.sem(f"o_done{s}") for s in range(2)]
        free = [g.sem(f"o_free{s}") for s in range(2)]
        summed = g.sem("o_summed")
        with nc.Block() as block:
            @block.sync
            def _(sp):
                for s in range(2):
                    sp.sem_inc(done[s], 1)
                    sp.sem_inc(free[s], 1)
                with sp.Fori(0, KD // 2) as j:
                    for s in range(2):
                        src = io["w_out"][:, ds((j * 2 + s) * P, P)].rearrange("(k p) c -> p k c", p=P)
                        sp.wait_ge(done[s], j + 1)
                        sp.dma_start(raw[s][:], src).then_inc(loaded[s], 16)

            @block.gpsimd
            def _(pool):
                nc.gpsimd.tensor_tensor(g.res[:], g.xh[:].bitcast(F32), g.xl[:].bitcast(F32), ALU.add)\
                    .then_inc(summed, 1)

            @block.tensor
            def _(pe):
                with pe.Fori(0, KD // 2) as j:
                    for s in range(2):
                        pe.wait_ge(loaded[s], j * 16 + 16)
                        pe.wait_ge(free[s], j + 1)
                        for k in range(KD):
                            for b in range(NB):
                                mm = nc.tensor.matmul(acc[s][:, b, 0:TB], raw[s][:, k, :],
                                                      mix[:, k, b * TB:(b + 1) * TB], start=(k == 0), stop=(k == KD - 1))
                        mm.then_inc(done[s], 1)

            @block.vector
            def _(dve):
                dve.wait_ge(summed, 1)
                with dve.Fori(0, KD // 2) as j:
                    for s in range(2):
                        row = g.res[:, j * 2 + s, :]
                        dve.wait_ge(done[s], j + 2)
                        nc.vector.scalar_tensor_tensor(blocks_of(row), blocks_of(row), ALPHA, acc[s][:, :, 0:TB],
                                                       ALU.mult, ALU.add).then_inc(free[s], 1)


def phase_store(g):
    nc, io = g.nc, g.io
    with ExitStack() as ctx:
        stage = g.sb(ctx, "y_stage", [P, KD, P])
        y = g.sb(ctx, "y_out", [P, KD, P])
        yt = g.ps(ctx, "y_t", [P, KD, P])
        staged, turned, read, stored = g.sem("y_staged"), g.sem("y_turned"), g.sem("y_read"), g.sem("y_stored")
        with nc.Block() as block:
            @block.gpsimd
            def _(pool):
                with pool.Fori(0, NCH) as c:
                    src = g.res[:, :, ds(c * P, P)]
                    pool.wait_ge(turned, c + 1)
                    pool.sem_inc(g.w.passed, 1)
                    nc.gpsimd.tensor_copy(stage[:], src).then_inc(staged, 1)

            @block.tensor
            def _(pe):
                with pe.Fori(0, NCH) as c:
                    pe.wait_ge(staged, c + 1)
                    pe.wait_ge(read, c + 1)
                    for k in range(KD):
                        mm = nc.tensor.transpose(yt[:, k, :], stage[:, k, :], g.ident[:])
                    mm.then_inc(turned, 1)
                pe.wait_ge(read, NCH + 1)
                for k in range(KD):
                    mm = nc.tensor.transpose(yt[0:TS, k, :], g.res[:, k, TP:T], g.ident[:])
                mm.then_inc(turned, 1)

            @block.vector
            def _(dve):
                with dve.Fori(0, NCH) as c:
                    dve.wait_ge(turned, c + 2)
                    dve.wait_ge(stored, c * 16 + 16)
                    nc.vector.tensor_copy(y[:], yt[:]).then_inc(read, 1)
                dve.wait_ge(turned, NCH + 2)
                dve.wait_ge(stored, NCH * 16 + 16)
                nc.vector.tensor_copy(y[0:TS], yt[0:TS]).then_inc(read, 1)

            @block.sync
            def _(sp):
                sp.sem_inc(turned, 1)
                sp.sem_inc(read, 1)
                sp.sem_inc(stored, 16)
                with sp.Fori(0, NCH) as c:
                    dst = io["y_prompt"][0, ds(c * P, P), :]
                    sp.wait_ge(read, c + 2)
                    sp.dma_start(dst, y[:].rearrange("p a b -> p (a b)")).then_inc(stored, 16)
                sp.wait_ge(read, NCH + 2)
                sp.dma_start(io["y_sample"].rearrange("b t d -> (b t) d"), y[0:TS].rearrange("p a b -> p (a b)"))\
                    .then_inc(stored, 16)
                sp.wait_ge(stored, 16 * (NCH + 2))


def build_step(nc, io, until=None):
    with ExitStack() as ctx:
        g = Build(nc, ctx, io)
        g.w = Weights(nc, ctx)
        g.xh, g.xl = (g.sb(ctx, n, [P, KD, TW], F32R) for n in ("x_hi", "x_lo"))
        g.ident, g.ones, g.causal = (g.sb(ctx, n, [P, P]) for n in ("ident_sb", "ones_sb", "causal_sb"))
        g.ln_g, g.ln_b = g.sb(ctx, "ln_g_sb", [P, 3, KD]), g.sb(ctx, "ln_b_sb", [P, 3, KD])
        g.b_gate, g.gn_g = g.sb(ctx, "b_gate_sb", [P, 3, KD]), g.sb(ctx, "gn_g_sb", [P, H_R])
        g.b_forget, g.pages = g.sb(ctx, "b_forget_sb", [H_F, 1]), g.sb(ctx, "pages_sb", [1, NSEQ * NPG], I32)
        g.mem_kt, g.mem_v = g.sb(ctx, "mem_kt", [P, H_M, N_MEM]), g.sb(ctx, "mem_v", [P, N_MEM // P, H_M * DM])
        with ExitStack() as first:
            g.res = g.sb(first, "res0", [P, KD, TW])
            phase_load(g)
            g.end_phase()
            phase_memory(g)
            g.end_phase()
            phase_ffn(g, 0)
            g.end_phase()
            phase_norm(g, 0, last=False)
            g.end_phase()
        if until == "norm0":
            return g
        with ExitStack() as middle:
            g.br = g.sb(middle, "br", [P, 12, TW])
            phase_retention_in(g)
            g.end_phase()
            phase_retention(g)
            g.end_phase()
            phase_head_norm(g)
            g.end_phase()
            with ExitStack() as fox:
                g.k_s, g.v_s = g.sb(fox, "k_s", [P, PAIRS, TS]), g.sb(fox, "v_s", [P, H_F * DF])
                g.lfn = g.sb(fox, "lfn", [P, NCH + 1, H_F])
                with ExitStack() as sums:
                    g.fkv = g.sb(sums, "fkv", [P, 8, TW])
                    g.negc = g.sb(sums, "negc", [H_F, TW])
                    phase_attention_in(g)
                    g.end_phase()
                    phase_kv_natural(g)
                    g.end_phase()
                    phase_fox_prompt(g)
                    g.end_phase()
                phase_cross(g)
                g.end_phase()
                with ExitStack() as sample:
                    qz = g.sb(sample, "d_qz", [P, NSEQ, PAIRS, ROWS])
                    bias_n = g.sb(sample, "d_bias_n", [P, NSEQ, TS])
                    bias_past = nc.dram_tensor("bias_past", [2 * NSEQ, NPG // 2, H_F, PAGE], F32, kind="Internal").ap()
                    phase_sample_bias(g, qz, bias_n, bias_past)
                    g.end_phase()
                    phase_fox_sample(g, qz, bias_n, bias_past)
                    g.end_phase()
            with ExitStack() as mixed:
                mix = g.sb(mixed, "mix", [P, KD, TW])
                phase_mix(g, mix)
                g.end_phase()
                g.res = g.br[:, 0:KD, :]
                phase_out(g, mix)
                g.end_phase()
            phase_norm(g, 1, last=False)
            g.end_phase()
            phase_ffn(g, 1)
            g.end_phase()
            phase_norm(g, 2, last=True)
            g.end_phase()
            phase_store(g)
            g.end_phase()
    return g


_INS = ["x_prompt", "x_sample", "mem_prompt", "cache_fox_k", "cache_fox_v", "cache_fox_logf", "state_ret",
        "cache_mem_k", "cache_mem_v", "page_table", "ln_g", "ln_b", "w_ffn_gate", "w_ffn_up", "w_ffn_down",
        "w_in", "b_forget", "b_gate", "ret_gn_g", "w_ret_o", "w_fox_o", "w_mem_k", "w_mem_v", "w_mem_o", "w_out"]
_OUTS = [("y_prompt", (1, TP, D)), ("y_sample", (NSEQ, LSEQ, D)),
         ("fox_k_prompt", (1, TP, H_F, DF)), ("fox_v_prompt", (1, TP, H_F, DF)), ("fox_logf_prompt", (1, TP, H_F)),
         ("ret_state_prompt", (1, H_R, DK, DM)), ("mem_k_prompt", (1, N_MEM, H_M, DM)),
         ("mem_v_prompt", (1, N_MEM, H_M, DM)), ("fox_k_sample", (NSEQ, LSEQ, H_F, DF)),
         ("fox_v_sample", (NSEQ, LSEQ, H_F, DF)), ("fox_logf_sample", (NSEQ, LSEQ, H_F)),
         ("ret_state_sample", (NSEQ, H_R, DK, DM))]


def kernel(**inputs):
    import numpy as np
    from concourse import bacc
    from concourse.bass_utils import run_bass_kernel_spmd

    nc = bacc.Bacc("TRN2", target_bir_lowering=False, num_devices=1)
    arrays = {n: np.ascontiguousarray(inputs[n]) for n in _INS}
    arrays.update(shape_tables())
    io = {n: nc.dram_tensor(n, a.shape, mybir.dt.from_np(a.dtype), kind="ExternalInput").ap()
          for n, a in arrays.items()}
    for n, shape in _OUTS:
        io[n] = nc.dram_tensor(n, shape, F32, kind="ExternalOutput").ap()
    build_step(nc, io)
    r = run_bass_kernel_spmd(nc, [arrays], core_ids=[0])
    return tuple(r.results[0][n] for n, _ in _OUTS)
```

```python
from contextlib import ExitStack

import concourse.bass as bass
from concourse import mybir

F32 = mybir.dt.float32
F32R = mybir.dt.float32r
I32 = mybir.dt.int32
ALU = mybir.AluOpType
ACT = mybir.ActivationFunctionType
AX = mybir.AxisListType
ds = bass.ds

P = 128
D = 1024
KD = D // P
TP = 1024
NSEQ, LSEQ = 8, 8
TS = NSEQ * LSEQ
T = TP + TS
NB, TB = 3, 364
TW = NB * TB
NCH = TP // P
D_FF = 2816
FT = D_FF // P
FC = 4
H_R, DK, H_F, DF, H_M, DM = 4, 64, 8, 64, 4, 128
N_MEM, PAGE, NPG = 256, 128, 32
PAST = PAGE * NPG
C_FQ, C_FL, C_MQ, C_GATE = 1536, 3072, 3080, 3592
ALPHA = 2.0 ** 0.25
EPS = 1e-5
NEG = -1e30
PAIRS = H_F // 2
RING = 16


def gammas():
    import numpy as np
    h = np.arange(H_R, dtype=np.float32)
    return np.log1p(-np.exp2(np.float32(-5.0) - h)).astype(np.float32)


def decays(c):
    import numpy as np
    return [float(np.exp(np.float32(c) * g, dtype=np.float32)) for g in gammas()]


def shape_tables():
    import numpy as np
    f = np.float32
    lg = gammas()
    ident = np.eye(P, dtype=f)
    rot = np.zeros((P, P), f)
    for m in range(P):
        if m % DK < DK // 2:
            rot[m + DK // 2, m] = -1.0
        else:
            rot[m - DK // 2, m] = 1.0
    half = DK // 2
    inv = (10000.0 ** (-np.arange(half) / half)).astype(f)
    pos = np.concatenate([np.arange(TP, dtype=f), np.tile(PAST + np.arange(LSEQ, dtype=f), NSEQ)])
    ang = (pos[None, :] * inv[:, None]).astype(f)
    cos = np.tile(np.cos(ang), (4, 1)).astype(f)
    sin = np.tile(np.sin(ang), (4, 1)).astype(f)

    def dec(steps):
        return np.exp(steps[..., None].astype(f) * lg).astype(f)

    i = np.arange(P)
    j = np.arange(TS)
    scale = f(DK ** -0.5)
    qd = dec(i + 1).T.reshape(2, 2, 1, P).transpose(1, 2, 0, 3)
    q_dec = np.broadcast_to(qd, (2, DK, 2, P)).reshape(P, 2, P)
    qs = dec(j % LSEQ + 1).T.reshape(2, 2, 1, TS).transpose(1, 2, 0, 3)
    q_dec_s = np.broadcast_to(qs, (2, DK, 2, TS)).reshape(P, 2, TS)
    k_dec = np.repeat(dec(P - 1 - i) * scale, DK, axis=1)
    k_dec_s = np.repeat(dec(LSEQ - 1 - j % LSEQ) * scale, DK, axis=1)
    d = i[None, :] - i[:, None]
    dmask = (np.where(d[..., None] >= 0, dec(np.maximum(d, 0)), 0) * scale).transpose(0, 2, 1)
    e = j[None, :] - j[:, None]
    same = (j[None, :] // LSEQ == j[:, None] // LSEQ) & (e >= 0)
    dmask_s = (np.where(same[..., None], dec(np.maximum(e, 0)), 0) * scale).transpose(0, 2, 1)
    causal = np.where(i[:, None] >= i[None, :], 0.0, NEG)
    seq = (j[:, None] // LSEQ == np.arange(NSEQ)[None, :])
    cols = np.broadcast_to(seq.T[None], (P, NSEQ, TS))
    new = np.where(seq[:, :, None] & (j[:, None, None] % LSEQ <= np.arange(LSEQ)), 0.0, NEG)
    own = np.arange(P)[:, None] // DF == np.arange(2)[None]
    tables = {
        "ident": ident, "rot": rot, "cos": cos, "sin": sin,
        "q_dec": q_dec, "q_dec_s": q_dec_s, "k_dec": k_dec, "k_dec_s": k_dec_s,
        "dmask": dmask, "dmask_s": dmask_s, "causal": causal, "seq_rows": seq, "seq_cols": cols,
        "new_mask": np.tile(new.transpose(2, 1, 0), (P // LSEQ, 1, 1)), "own_rows": own,
        "after": (i[:, None] > i[None, :]),
        "upto": (same & (e >= 0)),
    }
    return {n: np.ascontiguousarray(a, dtype=f) for n, a in tables.items()}


class Chain:

    def __init__(self, sem, base=0):
        self.sem, self.base, self.n = sem, base, 0

    def mark(self, instruction):
        instruction.then_inc(self.sem, 1)
        self.n += 1

    def wait(self, engine):
        engine.wait_ge(self.sem, self.base + self.n)


class Weights:

    def __init__(self, nc, ctx):
        self.nc = nc
        self.loaded = [ctx.enter_context(nc.semaphore(f"w_loaded{s}")) for s in range(2)]
        self.high = [ctx.enter_context(nc.semaphore(f"w_high{s}")) for s in range(2)]
        self.low = [ctx.enter_context(nc.semaphore(f"w_low{s}")) for s in range(2)]
        self.done = [ctx.enter_context(nc.semaphore(f"w_done{s}")) for s in range(2)]
        self.passed = ctx.enter_context(nc.semaphore("w_passed"))
        self.n = [0, 0]

    def open(self, ctx, tag):
        nc = self.nc
        self.raw = [ctx.enter_context(nc.sbuf_tensor(f"w_raw{s}_{tag}", [P, KD, P], F32)) for s in range(2)]
        self.hi = [ctx.enter_context(nc.sbuf_tensor(f"w_hi{s}_{tag}", [P, KD, P], F32R)) for s in range(2)]
        self.lo = [ctx.enter_context(nc.sbuf_tensor(f"w_lo{s}_{tag}", [P, KD, P], F32R)) for s in range(2)]

    def load(self, sp, s, n, src, kt):
        sp.wait_ge(self.low[s], n + 1)
        sp.dma_start(self.raw[s][:, 0:kt, :], src.rearrange("(k p) c -> p k c", p=P))\
          .then_inc(self.loaded[s], 16)

    def split(self, pool, s, n, kt):
        raw, hi, lo = (x[s][:, 0:kt, :] for x in (self.raw, self.hi, self.lo))
        pool.wait_ge(self.loaded[s], n * 16 + 16)
        pool.wait_ge(self.done[s], n + 1)
        pool.sem_inc(self.passed, 1)
        self.nc.gpsimd.tensor_copy(hi, raw).then_inc(self.high[s], 1)
        pool.wait_ge(self.high[s], n + 1)
        self.nc.gpsimd.tensor_tensor(lo, raw, hi.bitcast(F32), ALU.subtract).then_inc(self.low[s], 1)

    def split_high(self, act, s, n, kt):
        act.wait_ge(self.loaded[s], n * 16 + 16)
        act.wait_ge(self.done[s], n + 1)
        self.nc.scalar.copy(self.hi[s][:, 0:kt, :], self.raw[s][:, 0:kt, :]).then_inc(self.high[s], 1)

    def split_low(self, dve, s, n, kt):
        dve.wait_ge(self.high[s], n + 1)
        self.nc.vector.tensor_tensor(self.lo[s][:, 0:kt, :], self.raw[s][:, 0:kt, :],
                                     self.hi[s][:, 0:kt, :].bitcast(F32), ALU.subtract).then_inc(self.low[s], 1)

    def products(self, pe, s, n, kt, out, x_hi, x_lo, width=TB, blocks=NB, ready=None):
        pe.wait_ge(self.low[s], n + 2)
        for k in range(kt):
            if ready is not None:
                pe.wait_ge(ready[0], ready[1] + k)
            for w, x, first, last in ((self.hi, x_hi, True, False), (self.hi, x_lo, False, False),
                                      (self.lo, x_hi, False, True)):
                for b in range(blocks):
                    mm = self.nc.tensor.matmul(out[:, b, 0:width], w[s][:, k, :],
                                               x[:, k, b * width:(b + 1) * width],
                                               start=(k == 0 and first), stop=(k == kt - 1 and last))
        mm.then_inc(self.done[s], 1)


class Build:

    def __init__(self, nc, ctx, io):
        self.nc, self.ctx, self.io = nc, ctx, io
        self.sems = []

    def sem(self, name):
        self.sems.append(self.nc.alloc_semaphore(name))
        return self.sems[-1]

    def end_phase(self):
        for sem in self.sems:
            self.nc.gpsimd.sem_clear(sem)
        self.nc.all_engine_barrier()
        for sem in self.sems:
            self.nc.release_semaphore(sem)
        self.sems = []

    def sb(self, ctx, name, shape, dt=F32):
        return ctx.enter_context(self.nc.sbuf_tensor(name, shape, dt))

    def ps(self, ctx, name, shape):
        size = 1
        for n in shape[1:]:
            size *= n
        whole = ctx.enter_context(self.nc.psum_tensor(name, [shape[0], -(-size // 512) * 512], F32))
        flat = whole[:, 0:size]
        return flat if len(shape) == 2 else flat.rearrange("p (a b) -> p a b", b=shape[2]) if len(shape) == 3 \
            else flat.rearrange("p (a b c) -> p a b c", b=shape[2], c=shape[3])


def blocks_of(tile):
    return tile.rearrange("p (b t) -> p b t", t=TB)


def sweep(engine, first, body):
    first()
    with engine.Fori(0, NSEQ // 2 - 1) as j:
        for e in range(2):
            body(j * 2 + e, e, j, True)
    body(NSEQ - 2, 0, NSEQ // 2 - 1, True)
    body(NSEQ - 1, 1, NSEQ // 2 - 1, False)


def phase_load(g):
    nc, io = g.nc, g.io
    with ExitStack() as ctx:
        xin = [g.sb(ctx, f"x_in{s}", [P, D]) for s in range(2)]
        xt = [g.ps(ctx, f"x_t{s}", [P, KD, P]) for s in range(2)]
        consts, ident_ok = g.sem("consts_loaded"), g.sem("ident_loaded")
        loaded = [g.sem(f"x_loaded{s}") for s in range(2)]
        turned = [g.sem(f"x_turned{s}") for s in range(2)]
        hi = [g.sem(f"x_hi{s}") for s in range(2)]
        lo = [g.sem(f"x_lo{s}") for s in range(2)]
        acc = [g.sem(f"x_acc{s}") for s in range(2)]
        n_const = 7
        xs = io["x_sample"].rearrange("b t d -> (b t) d")
        with nc.Block() as block:
            @block.sync
            def _(sp):
                for s in range(2):
                    for sem in (g.w.low[s], g.w.done[s], turned[s], lo[s], acc[s]):
                        sp.sem_inc(sem, 1)
                sp.dma_start(g.ident[:], io["ident"]).then_inc(ident_ok, 16)
                with sp.Fori(0, NCH // 2) as i:
                    for s in range(2):
                        src = io["x_prompt"][0, ds((i * 2 + s) * P, P), :]
                        sp.wait_ge(turned[s], i + 1)
                        sp.dma_start(xin[s][:], src).then_inc(loaded[s], 16)
                sp.wait_ge(turned[0], NCH // 2 + 1)
                sp.dma_start(xin[0][0:TS, :], xs).then_inc(loaded[0], 16)
                sp.dma_start(g.ln_g[:], io["ln_g"].rearrange("l (k p) -> p l k", p=P),
                             allow_slow_non_contiguous=True).then_inc(consts, 16)
                sp.dma_start(g.ln_b[:], io["ln_b"].rearrange("l (k p) -> p l k", p=P),
                             allow_slow_non_contiguous=True).then_inc(consts, 16)
                sp.dma_start(g.b_gate[:], io["b_gate"].rearrange("i (k p) -> p i k", p=P),
                             allow_slow_non_contiguous=True).then_inc(consts, 16)
                sp.dma_start(g.gn_g[:], io["ret_gn_g"].rearrange("(h p) -> p h", p=P),
                             allow_slow_non_contiguous=True).then_inc(consts, 16)
                sp.dma_start(g.b_forget[:], io["b_forget"].rearrange("(h o) -> h o", o=1)).then_inc(consts, 16)
                sp.dma_start(g.pages[:], io["page_table"].rearrange("b n -> (b n)").unsqueeze(0)).then_inc(consts, 16)
                sp.dma_start(g.causal[:], io["causal"]).then_inc(consts, 16)
                sp.wait_ge(consts, 16 * n_const)

            def turn(pe, s, n, rows):
                pe.wait_ge(loaded[s], n * 16 + 16)
                pe.wait_ge(lo[s], n + 1)
                pe.wait_ge(acc[s], n + 1)
                for k in range(KD):
                    mm = nc.tensor.transpose(xt[s][:, k, 0:rows], xin[s][0:rows, k * P:(k + 1) * P],
                                             g.ident[0:rows, 0:rows])
                mm.then_inc(turned[s], 1)

            @block.tensor
            def _(pe):
                pe.wait_ge(ident_ok, 16)
                with pe.Fori(0, NCH // 2) as i:
                    for s in range(2):
                        turn(pe, s, i, P)
                turn(pe, 0, NCH // 2, TS)

            @block.scalar
            def _(act):
                def copies(s, n, hi_dst, acc_dst, rows):
                    act.wait_ge(turned[s], n + 2)
                    nc.scalar.copy(hi_dst, xt[s][:, :, 0:rows]).then_inc(hi[s], 1)
                    nc.scalar.mul(acc_dst, xt[s][:, :, 0:rows], ALPHA).then_inc(acc[s], 1)
                with act.Fori(0, NCH // 2) as i:
                    for s in range(2):
                        at = ds((i * 2 + s) * P, P)
                        copies(s, i, g.xh[:, :, at], g.res[:, :, at], P)
                copies(0, NCH // 2, g.xh[:, :, TP:T], g.res[:, :, TP:T], TS)

            @block.vector
            def _(dve):
                nc.vector.memset(g.xh[:, :, T:TW].bitcast(F32), 0.0)
                nc.vector.memset(g.xl[:, :, T:TW].bitcast(F32), 0.0)
                nc.vector.memset(g.res[:, :, T:TW], 0.0)
                nc.vector.memset(g.ones[:], 1.0)

                def lows(s, n, lo_dst, hi_src, rows):
                    dve.wait_ge(hi[s], n + 1)
                    dve.wait_ge(acc[s], n + 2)
                    nc.vector.tensor_tensor(lo_dst, xt[s][:, :, 0:rows], hi_src.bitcast(F32), ALU.subtract)\
                        .then_inc(lo[s], 1)
                with dve.Fori(0, NCH // 2) as i:
                    for s in range(2):
                        at = ds((i * 2 + s) * P, P)
                        lows(s, i, g.xl[:, :, at], g.xh[:, :, at], P)
                lows(0, NCH // 2, g.xl[:, :, TP:T], g.xh[:, :, TP:T], TS)


def phase_memory(g):
    nc, io, w = g.nc, g.io, g.w
    MT = N_MEM // P
    with ExitStack() as ctx:
        w.open(ctx, "mem")
        m_in = g.sb(ctx, "m_in", [P, MT, D])
        mh = g.sb(ctx, "mh", [P, KD, N_MEM], F32R)
        ml = g.sb(ctx, "ml", [P, KD, N_MEM], F32R)
        kv = [g.sb(ctx, f"m_kv{s}", [P, N_MEM]) for s in range(2)]
        kn = g.sb(ctx, "m_kn", [P, MT, H_M * DM])
        acc = [g.ps(ctx, f"m_acc{s}", [P, 1, 512]) for s in range(2)]
        mt = g.ps(ctx, "m_t", [P, KD, P])
        tn = g.ps(ctx, "m_tn", [P, 2, MT, P])
        loaded, turned, hi, lo = g.sem("m_loaded"), g.sem("m_turned"), g.sem("m_hi"), g.sem("m_lo")
        kv_out = [g.sem(f"m_kv_out{s}") for s in range(2)]
        nat, nat_out, stored = g.sem("m_nat"), g.sem("m_nat_out"), g.sem("m_stored")
        kt_out = g.sem("m_kt_out")
        base = list(w.n)
        with nc.Block() as block:
            @block.sync
            def _(sp):
                for s in range(2):
                    sp.sem_inc(kv_out[s], 1)
                sp.sem_inc(nat_out, 1)
                sp.dma_start(m_in[:], io["mem_prompt"][0].rearrange("(m p) d -> p m d", p=P)).then_inc(loaded, 16)
                with sp.Fori(0, H_M) as h:
                    for s, name in enumerate(("w_mem_k", "w_mem_v")):
                        w.load(sp, s, h + base[s], io[name][:, ds(h * DM, DM)], KD)
                sp.wait_ge(nat_out, H_M + 1)
                for name, src in (("mem_k_prompt", kn), ("mem_v_prompt", g.mem_v)):
                    sp.dma_start(io[name][0].rearrange("(m p) h d -> p m (h d)", p=P), src[:]).then_inc(stored, 16)
                sp.wait_ge(stored, 32)

            @block.tensor
            def _(pe):
                pe.wait_ge(loaded, 16)
                for m in range(MT):
                    if m > 0:
                        pe.wait_ge(lo, m)
                    for k in range(KD):
                        mm = nc.tensor.transpose(mt[:, k, :], m_in[:, m, k * P:(k + 1) * P], g.ident[:])
                    mm.then_inc(turned, 1)
                pe.wait_ge(lo, MT)
                with pe.Fori(0, H_M) as h:
                    for s in range(2):
                        pe.wait_ge(kv_out[s], h + 1)
                        w.products(pe, s, h + base[s], KD, acc[s], mh, ml, width=N_MEM, blocks=1)
                    pe.wait_ge(nat_out, h + 1)
                    for s in range(2):
                        pe.wait_ge(kv_out[s], h + 2)
                        for m in range(MT):
                            mm = nc.tensor.transpose(tn[:, s, m, :], kv[s][:, m * P:(m + 1) * P], g.ident[:])
                    mm.then_inc(nat, 1)

            @block.scalar
            def _(act):
                for m in range(MT):
                    act.wait_ge(turned, m + 1)
                    nc.scalar.copy(mh[:, :, m * P:(m + 1) * P], mt[:]).then_inc(hi, 1)

                def head(h, more):
                    dst = g.mem_kt[:, ds(h, 1), :].rearrange("p o m -> p (o m)")
                    act.wait_ge(w.done[0], h + (base[0] + 2))
                    nc.scalar.copy(kv[0][:], acc[0][:, 0, 0:N_MEM]).then_inc(kv_out[0], 1)
                    if more:
                        for s in range(2):
                            w.split_high(act, s, h + (base[s] + 1), KD)
                    act.wait_ge(kv_out[0], h + 2)
                    nc.scalar.copy(dst, kv[0][:]).then_inc(kt_out, 1)
                    act.wait_ge(kt_out, h + 1)
                    act.wait_ge(nat, h + 1)
                for s in range(2):
                    w.split_high(act, s, base[s], KD)
                with act.Fori(0, H_M - 1) as h:
                    head(h, True)
                head(H_M - 1, False)

            @block.vector
            def _(dve):
                for m in range(MT):
                    dve.wait_ge(hi, m + 1)
                    nc.vector.tensor_tensor(ml[:, :, m * P:(m + 1) * P], mt[:],
                                            mh[:, :, m * P:(m + 1) * P].bitcast(F32), ALU.subtract).then_inc(lo, 1)

                def head(h, more):
                    if more:
                        w.split_low(dve, 0, h + (base[0] + 1), KD)
                    dve.wait_ge(w.done[1], h + (base[1] + 2))
                    nc.vector.tensor_copy(kv[1][:], acc[1][:, 0, 0:N_MEM]).then_inc(kv_out[1], 1)
                    if more:
                        w.split_low(dve, 1, h + (base[1] + 1), KD)
                    k_dst, v_dst = kn[:, :, ds(h * DM, DM)], g.mem_v[:, :, ds(h * DM, DM)]
                    dve.wait_ge(nat, h + 1)
                    nc.vector.tensor_copy(k_dst, tn[:, 0])
                    nc.vector.tensor_copy(v_dst, tn[:, 1]).then_inc(nat_out, 1)
                for s in range(2):
                    w.split_low(dve, s, base[s], KD)
                with dve.Fori(0, H_M - 1) as h:
                    head(h, True)
                head(H_M - 1, False)
        w.n = [x + H_M for x in base]


def phase_ffn(g, layer):
    nc, io, w = g.nc, g.io, g.w
    wg, wu, wd = (io[n][layer] for n in ("w_ffn_gate", "w_ffn_up", "w_ffn_down"))
    full = FT // FC
    rest = FT - full * FC
    per = FC + KD // 2
    with ExitStack() as ctx:
        w.open(ctx, f"ffn{layer}")
        hh = g.sb(ctx, f"h_hi{layer}", [P, FC, TW], F32R)
        hl = g.sb(ctx, f"h_lo{layer}", [P, FC, TW], F32R)
        silu = g.sb(ctx, f"silu{layer}", [P, TW])
        hid = g.sb(ctx, f"hid{layer}", [P, TW])
        acc = [g.ps(ctx, f"f_acc{s}_{layer}", [P, NB, 512]) for s in range(2)]
        free = [g.sem(f"f_free{s}_{layer}") for s in range(2)]
        hh_ok, hl_ok = g.sem(f"f_hh{layer}"), g.sem(f"f_hl{layer}")
        b0, b1 = w.n
        with nc.Block() as block:
            @block.sync
            def _(sp):
                for s in range(2):
                    sp.sem_inc(free[s], 1)

                def ups(c, n, ft):
                    with sp.Fori(0, ft) as f:
                        at = ds((c * FC + f) * P, P)
                        w.load(sp, 0, n + f + b0, wg[:, at], KD)
                        w.load(sp, 1, n + f + b1, wu[:, at], KD)

                def downs(c, n, ft):
                    with sp.Fori(0, KD // 2) as j:
                        for s in range(2):
                            src = wd[ds(c * (FC * P), ft * P), ds((j * 2 + s) * P, P)]
                            w.load(sp, s, n + j + (b0, b1)[s], src, ft)

                with sp.Fori(0, full) as c:
                    ups(c, c * per, FC)
                    downs(c, c * per + FC, FC)
                ups(full, full * per, rest)
                downs(full, full * per + rest, rest)

            @block.tensor
            def _(pe):
                def ups(n, ft):
                    with pe.Fori(0, ft) as f:
                        for s in range(2):
                            pe.wait_ge(free[s], n + f + 1)
                            w.products(pe, s, n + f + (b0, b1)[s], KD, acc[s], g.xh, g.xl)

                def downs(c, n, ft):
                    with pe.Fori(0, KD // 2) as j:
                        for s in range(2):
                            pe.wait_ge(free[s], n + j + 1)
                            w.products(pe, s, n + j + (b0, b1)[s], ft, acc[s], hh, hl,
                                       ready=(hl_ok, c * FC + 1))

                with pe.Fori(0, full) as c:
                    ups(c * per, FC)
                    downs(c, c * per + FC, FC)
                ups(full * per, rest)
                downs(full, full * per + rest, rest)

            @block.gpsimd
            def _(pool):
                def tiles(n, count, kt):
                    with pool.Fori(0, count) as j:
                        for s in range(2):
                            w.split(pool, s, n + j + (b0, b1)[s], kt)

                with pool.Fori(0, full) as c:
                    tiles(c * per, FC, KD)
                    tiles(c * per + FC, KD // 2, FC)
                tiles(full * per, rest, KD)
                tiles(full * per + rest, KD // 2, rest)

            @block.scalar
            def _(act):
                act.preload_act_table(ACT.Silu)

                def ups(c, n, ft):
                    with act.Fori(0, ft) as f:
                        dst = hh[:, f, :]
                        act.wait_ge(w.done[0], n + f + (b0 + 2))
                        nc.scalar.activation(blocks_of(silu[:]), acc[0][:, :, 0:TB], ACT.Silu)\
                            .then_inc(free[0], 1)
                        act.wait_ge(free[1], n + f + 2)
                        nc.scalar.copy(dst, hid[:]).then_inc(hh_ok, 1)

                with act.Fori(0, full) as c:
                    ups(c, c * per, FC)
                ups(full, full * per, rest)

            @block.vector
            def _(dve):
                def ups(c, n, ft):
                    with dve.Fori(0, ft) as f:
                        hi_src, lo_dst = hh[:, f, :], hl[:, f, :]
                        dve.wait_ge(free[0], n + f + 2)
                        dve.wait_ge(w.done[1], n + f + (b1 + 2))
                        nc.vector.tensor_tensor(blocks_of(hid[:]), blocks_of(silu[:]), acc[1][:, :, 0:TB],
                                                ALU.mult).then_inc(free[1], 1)
                        dve.wait_ge(free[1], n + f + 2)
                        dve.wait_ge(hh_ok, c * FC + f + 1)
                        nc.vector.tensor_tensor(lo_dst, hid[:], hi_src.bitcast(F32), ALU.subtract)\
                            .then_inc(hl_ok, 1)
                        dve.wait_ge(hl_ok, c * FC + f + 1)

                def downs(n, ft):
                    with dve.Fori(0, KD // 2) as j:
                        for s in range(2):
                            row = g.res[:, j * 2 + s, :]
                            dve.wait_ge(w.done[s], n + j + ((b0, b1)[s] + 2))
                            nc.vector.scalar_tensor_tensor(blocks_of(row), acc[s][:, :, 0:TB], 0.5, blocks_of(row),
                                                           ALU.mult, ALU.add).then_inc(free[s], 1)

                with dve.Fori(0, full) as c:
                    ups(c, c * per, FC)
                    downs(c * per + FC, FC)
                ups(full, full * per, rest)
                downs(full * per + rest, rest)
        used = full * per + rest + KD // 2
        w.n = [b0 + used, b1 + used]


def phase_norm(g, which, keep):
    nc = g.nc
    parts = keep != "result"
    with ExitStack() as ctx:
        mean_w = g.sb(ctx, f"mean_w{which}", [P, P])
        sq = [g.sb(ctx, f"sq{s}_{which}", [P, KD, TB]) for s in range(2)]
        rstd = [g.sb(ctx, f"rstd{b}_{which}", [P, TB]) for b in range(NB)]
        std = [g.sb(ctx, f"std{b}_{which}", [P, TB]) for b in range(NB)]
        eps, alpha_b = g.sb(ctx, f"eps{which}", [P, 1]), g.sb(ctx, f"alpha_b{which}", [P, KD])
        mean = [g.ps(ctx, f"mean{b}_{which}", [P, 512]) for b in range(NB)]
        var = [g.ps(ctx, f"var{b}_{which}", [P, 512]) for b in range(NB)]
        ready, mean_ok, var_ok = g.sem(f"n_ready{which}"), g.sem(f"n_mean{which}"), g.sem(f"n_var{which}")
        centred, squared, std_ok = g.sem(f"n_centred{which}"), g.sem(f"n_squared{which}"), g.sem(f"n_std{which}")
        rstd_ok, scaled = g.sem(f"n_rstd{which}"), g.sem(f"n_scaled{which}")
        high, low, alpha_ok = g.sem(f"n_high{which}"), g.sem(f"n_low{which}"), g.sem(f"n_alpha{which}")
        gain, shift = g.ln_g[:, which, :], g.ln_b[:, which, :]

        def cols(b):
            return slice(b * TB, (b + 1) * TB)

        def low_parts(dve, b):
            dve.wait_ge(high, b + 1)
            for k in range(KD):
                ins = nc.vector.scalar_tensor_tensor(g.xl[:, k, cols(b)], g.res[:, k, cols(b)], shift[:, k:k + 1],
                                                  g.xh[:, k, cols(b)].bitcast(F32), ALU.add, ALU.subtract)
            ins.then_inc(low, 1)

        with nc.Block() as block:
            @block.gpsimd
            def _(pool):
                nc.gpsimd.memset(mean_w[:], 1.0 / D).then_inc(ready, 1)
                nc.gpsimd.memset(eps[:], EPS).then_inc(ready, 1)

            @block.tensor
            def _(pe):
                pe.wait_ge(ready, 2)
                for b in range(NB):
                    for k in range(KD):
                        mm = nc.tensor.matmul(mean[b][:, 0:TB], mean_w[:], g.res[:, k, cols(b)],
                                              start=(k == 0), stop=(k == KD - 1))
                    mm.then_inc(mean_ok, 1)
                for b in range(NB):
                    pe.wait_ge(squared, b + 1)
                    for k in range(KD):
                        mm = nc.tensor.matmul(var[b][:, 0:TB], mean_w[:], sq[b % 2][:, k, :],
                                              start=(k == 0), stop=(k == KD - 1))
                    mm.then_inc(var_ok, 1)

            @block.vector
            def _(dve):
                for b in range(NB):
                    dve.wait_ge(mean_ok, b + 1)
                    nc.vector.tensor_tensor(g.res[:, :, cols(b)], g.res[:, :, cols(b)],
                                            mean[b][:, 0:TB].unsqueeze(1).broadcast_to([P, KD, TB]), ALU.subtract)\
                        .then_inc(centred, 1)
                for b in range(NB):
                    dve.wait_ge(std_ok, b + 1)
                    nc.vector.reciprocal(rstd[b][:], std[b][:]).then_inc(rstd_ok, 1)
                    dve.wait_ge(rstd_ok, b + 1)
                    dve.wait_ge(squared, b + 1)
                    for k in range(KD):
                        row = g.res[:, k, cols(b)]
                        ins = nc.vector.scalar_tensor_tensor(row, row, gain[:, k:k + 1], rstd[b][:], ALU.mult, ALU.mult)
                    ins.then_inc(scaled, 1)
                    if parts and b > 0:
                        low_parts(dve, b - 1)
                if parts:
                    low_parts(dve, NB - 1)

            @block.scalar
            def _(act):
                act.wait_ge(ready, 2)
                if keep == "both":
                    nc.scalar.mul(alpha_b[:], shift, ALPHA).then_inc(alpha_ok, 1)
                for b in range(NB):
                    act.wait_ge(centred, b + 1)
                    if b >= 2:
                        act.wait_ge(var_ok, b - 1)
                    nc.scalar.activation(sq[b % 2][:], g.res[:, :, cols(b)], ACT.Square).then_inc(squared, 1)
                for b in range(NB):
                    act.wait_ge(var_ok, b + 1)
                    nc.scalar.activation(std[b][:], var[b][:, 0:TB], ACT.Sqrt, bias=eps[:]).then_inc(std_ok, 1)

                def scaled_back(b):
                    act.wait_ge(low, b + 1)
                    for k in range(KD):
                        nc.scalar.activation(g.res[:, k, cols(b)], g.res[:, k, cols(b)], ACT.Identity,
                                             bias=alpha_b[:, k:k + 1], scale=ALPHA)
                if keep == "both":
                    act.wait_ge(alpha_ok, 1)
                for b in range(NB):
                    act.wait_ge(scaled, b + 1)
                    for k in range(KD):
                        dst = g.xh if parts else g.res
                        ins = nc.scalar.activation(dst[:, k, cols(b)], g.res[:, k, cols(b)], ACT.Identity,
                                                   bias=shift[:, k:k + 1])
                    ins.then_inc(high, 1)
                    if keep == "both" and b > 0:
                        scaled_back(b - 1)
                if keep == "both":
                    scaled_back(NB - 1)


def phase_retention_in(g):
    nc, io, w = g.nc, g.io, g.w
    pairs, plain = 6, 4
    with ExitStack() as ctx:
        w.open(ctx, "ret")
        acc = [g.ps(ctx, f"r_acc{s}", [P, NB, 512]) for s in range(2)]
        free = [g.sem(f"r_free{s}") for s in range(2)]
        b0, b1 = w.n
        with nc.Block() as block:
            @block.sync
            def _(sp):
                for s in range(2):
                    sp.sem_inc(free[s], 1)
                with sp.Fori(0, pairs) as n:
                    for s in range(2):
                        w.load(sp, s, n + (b0, b1)[s], io["w_in"][:, ds((n * 2 + s) * P, P)], KD)

            @block.gpsimd
            def _(pool):
                with pool.Fori(0, pairs) as n:
                    for s in range(2):
                        w.split(pool, s, n + (b0, b1)[s], KD)

            @block.tensor
            def _(pe):
                with pe.Fori(0, pairs) as n:
                    for s in range(2):
                        pe.wait_ge(free[s], n + 1)
                        w.products(pe, s, n + (b0, b1)[s], KD, acc[s], g.xh, g.xl)

            @block.scalar
            def _(act):
                act.preload_act_table(ACT.Silu)
                with act.Fori(0, plain) as n:
                    dst = blocks_of(g.br[:, n * 2 + 4, :])
                    act.wait_ge(w.done[0], n + (b0 + 2))
                    nc.scalar.copy(dst, acc[0][:, :, 0:TB]).then_inc(free[0], 1)
                with act.Fori(plain, pairs) as n:
                    for s in range(2):
                        dst = blocks_of(g.br[:, n * 2 + (s - 2 * plain), :])
                        act.wait_ge(w.done[s], n + ((b0, b1)[s] + 2))
                        nc.scalar.activation(dst, acc[s][:, :, 0:TB], ACT.Silu).then_inc(free[s], 1)

            @block.vector
            def _(dve):
                with dve.Fori(0, plain) as n:
                    dst = blocks_of(g.br[:, n * 2 + 5, :])
                    dve.wait_ge(w.done[1], n + (b1 + 2))
                    nc.vector.tensor_copy(dst, acc[1][:, :, 0:TB]).then_inc(free[1], 1)
        w.n = [b0 + pairs, b1 + pairs]


HALVES = [slice(0, DK), slice(DK, P)]


def phase_retention(g):
    nc, io = g.nc, g.io
    dec_c, dec_s = decays(P), decays(LSEQ)
    with ExitStack() as ctx:
        def sb(name, shape):
            return g.sb(ctx, "rt_" + name, shape)
        cos, sin, rot = sb("cos", [P, T]), sb("sin", [P, T]), sb("rot", [P, P])
        q_dec, k_dec, dmask = sb("q_dec", [P, 2, P]), sb("k_dec", [P, H_R * DK]), sb("dmask", [P, H_R, P])
        q_dec_s, k_dec_s = sb("q_dec_s", [P, 2, TS]), sb("k_dec_s", [TS, H_R * DK])
        dmask_s, seq_rows, seq_cols = sb("dmask_s", [TS, H_R, TS]), sb("seq_rows", [TS, NSEQ]), sb("seq_cols", [P, NSEQ, TS])
        v_in = [sb(f"v_in{s}", [P, H_R, P]) for s in range(2)]
        by_cos, qk = sb("by_cos", [P, 4, P]), sb("qk", [P, 4, P])
        qz = sb("qz", [P, 2, 2, P])
        qd = [sb(f"qd{s}", [P, 2, 2, P]) for s in range(2)]
        vn = [sb(f"vn{s}", [P, H_R, P]) for s in range(2)]
        kd, at = sb("kd", [P, H_R * DK]), sb("at", [P, H_R, P])
        state = sb("state", [P, 2, DM])
        s0, s1 = ([sb(f"s{i}_{s}", [P, 2, DM]) for s in range(2)] for i in range(2))
        kdm = [sb(f"kdm{s}", [TS, H_R * DK]) for s in range(2)]
        qdm = [sb(f"qdm{s}", [P, 2, 2, TS]) for s in range(2)]
        swap = g.ps(ctx, "rt_swap", [P, 4, P])
        vt = g.ps(ctx, "rt_vt", [P, H_R, P])
        kt = g.ps(ctx, "rt_kt", [P, 2, P])
        scores = g.ps(ctx, "rt_scores", [P, H_R, P])
        o = g.ps(ctx, "rt_o", [P, H_R, P])
        o_s = g.ps(ctx, "rt_o_s", [P, H_R, P])
        upd = g.ps(ctx, "rt_upd", [P, H_R, P])
        upd_s = [upd, o]
        names = {"cos": cos, "sin": sin, "rot": rot, "q_dec": q_dec, "k_dec": k_dec, "dmask": dmask,
                 "q_dec_s": q_dec_s, "k_dec_s": k_dec_s, "dmask_s": dmask_s, "seq_rows": seq_rows, "seq_cols": seq_cols}
        consts, zeroed = g.sem("rt_consts"), g.sem("rt_zeroed")
        staged, scored, pe_out = g.sem("rt_staged"), g.sem("rt_scored"), g.sem("rt_pe_out")
        turned = g.sem("rt_turned")
        roped, v_nat, masked, o_read = g.sem("rt_roped"), g.sem("rt_v_nat"), g.sem("rt_masked"), g.sem("rt_o_read")
        state_ok, steps = g.sem("rt_state"), g.sem("rt_steps")
        loaded = [g.sem(f"rt_s_loaded{s}") for s in range(2)]
        s_stored = [g.sem(f"rt_s_stored{s}") for s in range(2)]
        s_masked, s_pe, s_new, stored = g.sem("rt_s_masked"), g.sem("rt_s_pe"), g.sem("rt_s_new"), g.sem("rt_stored")
        STEPS = 2

        def columns(c):
            return (slice(TP, T), TS) if isinstance(c, int) and c == NCH else (ds(c * P, P), P)

        def chunks(engine, first, body):
            first()
            with engine.Fori(0, NCH // 2 - 1) as j:
                for e in range(2):
                    body(j * 2 + e, e)
            body(NCH - 2, 0)
            body(NCH - 1, 1)

        with nc.Block() as block:
            @block.sync
            def _(sp):
                for sem in (roped, v_nat, o_read, masked):
                    sp.sem_inc(sem, 1)
                for sem in (turned, s_pe, s_new):
                    sp.sem_inc(sem, 2)
                for s in range(2):
                    sp.sem_inc(s_stored[s], 32)
                for name, dst in names.items():
                    sp.dma_start(dst[:], io[name]).then_inc(consts, 16)

                def halves(name, b):
                    ap = io[name][b].rearrange("(pr two) d e -> two d pr e", two=2)
                    return [ap[i] for i in range(2)]

                def load(b, e, src):
                    for i in range(2):
                        sp.dma_start(s0[e][HALVES[i]], src[i]).then_inc(loaded[e], 16)

                def store(e, dst):
                    for i in range(2):
                        sp.dma_start(dst[i], s1[e][HALVES[i]]).then_inc(s_stored[e], 16)
                for e in range(2):
                    load(e, e, halves("state_ret", e))
                with sp.Fori(0, NSEQ // 2 - 1) as j:
                    for e in range(2):
                        b = j * 2 + e
                        dst, src = halves("ret_state_sample", b), halves("state_ret", b + 2)
                        sp.wait_ge(s_new, b + 3)
                        store(e, dst)
                        load(b + 2, e, src)
                for e in range(2):
                    sp.wait_ge(s_new, NSEQ + 1 + e)
                    store(e, halves("ret_state_sample", NSEQ - 2 + e))
                sp.wait_ge(state_ok, NCH + 1)
                dst = halves("ret_state_prompt", 0)
                for i in range(2):
                    sp.dma_start(dst[i], state[HALVES[i]]).then_inc(stored, 16)
                sp.wait_ge(stored, 32)
                for e in range(2):
                    sp.wait_ge(s_stored[e], 32 + 16 * NSEQ)

            @block.gpsimd
            def _(pool):
                nc.gpsimd.memset(qz[:], 0.0).then_inc(zeroed, 1)
                for s in range(2):
                    nc.gpsimd.memset(qd[s][:], 0.0).then_inc(zeroed, 1)
                with pool.Fori(0, NCH // 2) as j:
                    for e in range(2):
                        src = g.br[:, 8:12, ds(j * (2 * P) + e * P, P)]
                        pool.wait_ge(turned, j * 2 + (e + 1))
                        pool.sem_inc(g.w.passed, 1)
                        nc.gpsimd.tensor_copy(v_in[e][:], src).then_inc(staged, 1)

            @block.tensor
            def _(pe):
                def turn(c, e):
                    at_c, n = columns(c)
                    moving = g.br[:, 4:8, at_c]
                    pe.wait_ge(roped, c + 1)
                    pe.wait_ge(v_nat, c + 1)
                    if n == P:
                        pe.wait_ge(staged, c + 1)
                    nc.tensor.matmul(swap[:, :, 0:n], rot[:], moving, start=True, stop=True)
                    for h in range(H_R):
                        src = v_in[e][:, h, :] if n == P else g.br[:, 8 + h, at_c]
                        mm = nc.tensor.transpose(vt[0:n, h, :], src, g.ident[:])
                    mm.then_inc(turned, 1)

                def chunk_scores(c):
                    n = columns(c)[1]
                    pe.wait_ge(roped, c + 2)
                    pe.wait_ge(masked, c + 1)
                    for p in range(2):
                        nc.tensor.transpose(kt[0:n, p, :], qk[:, 2 + p, 0:n], g.ident[:])
                    for h in range(H_R):
                        mm = nc.tensor.matmul(scores[0:n, h, 0:n], qk[:, 2 + h // 2, 0:n], qz[:, h % 2, h // 2, 0:n],
                                              start=True, stop=True)
                    mm.then_inc(scored, 1)

                def body(c, e):
                    chunk_scores(c)
                    turn(c + 1, 1 - e)
                    pe.wait_ge(masked, c + 2)
                    pe.wait_ge(v_nat, c + 2)
                    pe.wait_ge(state_ok, c + 1)
                    pe.wait_ge(o_read, c + 1)
                    for h in range(H_R):
                        nc.tensor.matmul(o[:, h, :], vn[e][:, h, :], at[:, h, :], start=True, stop=False)
                        nc.tensor.matmul(o[:, h, :], state[:, h // 2, :], qd[e][:, h % 2, h // 2, :],
                                         start=False, stop=True)
                    for h in range(H_R):
                        mm = nc.tensor.matmul(upd[:, h, :], kd[:, (h // 2) * P:(h // 2 + 1) * P], vn[e][:, h, :],
                                              start=True, stop=True)
                    mm.then_inc(pe_out, 1)

                pe.wait_ge(consts, 16 * len(names))
                chunks(pe, lambda: turn(0, 0), body)
                chunk_scores(NCH)
                pe.wait_ge(masked, NCH + 2)
                pe.wait_ge(v_nat, NCH + 2)
                pe.wait_ge(o_read, NCH + 1)
                pe.wait_ge(state_ok, NCH + 1)
                for h in range(H_R):
                    nc.tensor.matmul(o_s[:, h, 0:TS], vn[0][0:TS, h, :], at[0:TS, h, 0:TS], start=(h == 0), stop=False,
                                     skip_group_check=True)
                with pe.Fori(0, NSEQ // 2) as j:
                    for e in range(2):
                        b = j * 2 + e
                        pe.wait_ge(loaded[e], j * 32 + 32)
                        pe.wait_ge(s_masked, b + 1)
                        for h in range(H_R):
                            nc.tensor.matmul(o_s[:, h, 0:TS], s0[e][:, h // 2, :], qdm[e][:, h % 2, h // 2, :],
                                             start=False, stop=False, skip_group_check=True)
                        pe.wait_ge(s_new, b + 1)
                        for h in range(H_R):
                            mm = nc.tensor.matmul(upd_s[e][:, h, :], kdm[e][:, (h // 2) * P:(h // 2 + 1) * P],
                                                  vn[0][0:TS, h, :], start=True, stop=True)
                        mm.then_inc(s_pe, 1)

            @block.scalar
            def _(act):
                def natural(c, e):
                    n = columns(c)[1]
                    act.wait_ge(turned, c + 3)
                    nc.scalar.copy(vn[e][0:n], vt[0:n]).then_inc(v_nat, 1)

                def body(c, e):
                    dst = g.br[:, 8:12, columns(c)[0]]
                    natural(c + 1, 1 - e)
                    act.wait_ge(pe_out, c + 1)
                    nc.scalar.copy(dst, o[:]).then_inc(o_read, 1)
                chunks(act, lambda: natural(0, 0), body)
                act.wait_ge(s_pe, NSEQ + 2)
                nc.scalar.copy(g.br[:, 8:12, TP:T], o_s[:, :, 0:TS]).then_inc(o_read, 1)

            def rope(dve, c, e):
                at_c, n = columns(c)
                t_cos, t_sin, src = cos[:, at_c], sin[:, at_c], g.br[:, 4:8, at_c]
                q_decay = q_dec if n == P else q_dec_s
                chain = Chain(steps, c * STEPS)
                dve.wait_ge(turned, c + 3)
                nc.vector.tensor_tensor(by_cos[:, :, 0:n], src, t_cos.unsqueeze(1).broadcast_to([P, 4, n]), ALU.mult)
                chain.mark(nc.vector.tensor_tensor(qk[:, :, 0:n], swap[:, :, 0:n],
                                                   t_sin.unsqueeze(1).broadcast_to([P, 4, n]), ALU.mult))
                chain.wait(dve)
                nc.vector.tensor_tensor(qk[:, 2:4, 0:n], qk[:, 2:4, 0:n], by_cos[:, 2:4, 0:n], ALU.add)
                for s, rows in enumerate(HALVES):
                    ins = nc.vector.tensor_tensor(qz[rows, s, :, 0:n], qk[rows, 0:2, 0:n], by_cos[rows, 0:2, 0:n], ALU.add)
                chain.mark(ins)
                chain.wait(dve)
                for s, rows in enumerate(HALVES):
                    ins = nc.vector.tensor_tensor(qd[e][rows, s, :, 0:n], qz[rows, s, :, 0:n], q_decay[rows], ALU.mult)
                ins.then_inc(roped, 1)
                assert chain.n == STEPS

            def masks(dve, c, mask, k_decay):
                n = columns(c)[1]
                dve.wait_ge(scored, c + 1)
                nc.vector.tensor_tensor(at[0:n, :, 0:n], scores[0:n, :, 0:n], mask[:], ALU.mult)
                nc.vector.tensor_tensor(kd[0:n, :], kt[0:n].rearrange("p a b -> p (a b)"), k_decay[:], ALU.mult)\
                    .then_inc(masked, 1)

            def new_state(dst, old, change, dec, done):
                for h in range(H_R):
                    rows = HALVES[h % 2]
                    ins = nc.vector.scalar_tensor_tensor(dst[rows, h // 2, :], old[rows, h // 2, :], dec[h],
                                                         change[rows, h, :], ALU.mult, ALU.add)
                ins.then_inc(done, 1)

            @block.vector
            def _(dve):
                def body(c, e):
                    masks(dve, c, dmask, k_dec)
                    rope(dve, c + 1, 1 - e)
                    dve.wait_ge(pe_out, c + 1)
                    dve.wait_ge(state_ok, c + 1)
                    new_state(state, state, upd, dec_c, state_ok)

                def alone(b, e):
                    cols = seq_cols[:, ds(b, 1), :].broadcast_to([P, 4, TS])
                    row = seq_rows[:, ds(b, 1)]
                    dve.wait_ge(s_pe, b + 1)
                    nc.vector.tensor_tensor(qdm[e][:].rearrange("p s a t -> p (s a) t"),
                                            qd[0][:].rearrange("p s a t -> p (s a) t")[:, :, 0:TS], cols, ALU.mult)
                    nc.vector.tensor_scalar(kdm[e][:], kd[0:TS, :], row, None, ALU.mult).then_inc(s_masked, 1)

                def sequence(b, e, half, more):
                    if more:
                        alone(b + 1, 1 - e)
                    dve.wait_ge(s_pe, b + 3)
                    dve.wait_ge(s_stored[e], half * 32 + 32)
                    new_state(s1[e], s0[e], upd_s[e], dec_s, s_new)

                dve.wait_ge(consts, 16 * len(names))
                nc.vector.memset(state[:], 0.0).then_inc(state_ok, 1)
                dve.wait_ge(zeroed, 3)
                chunks(dve, lambda: rope(dve, 0, 0), body)
                masks(dve, NCH, dmask_s, k_dec_s)
                dve.wait_ge(masked, NCH + 2)
                sweep(dve, lambda: alone(0, 0), sequence)


def phase_head_norm(g):
    nc = g.nc
    with ExitStack() as ctx:
        mean_w, eps = g.sb(ctx, "hn_mean_w", [P, P]), g.sb(ctx, "hn_eps", [P, 1])
        sq = [g.sb(ctx, f"hn_sq{s}", [P, TW]) for s in range(2)]
        std = [g.sb(ctx, f"hn_std{s}", [P, TW]) for s in range(2)]
        mean = g.ps(ctx, "hn_mean", [P, NB, 512])
        var = g.ps(ctx, "hn_var", [P, NB, 512])
        ready, mean_ok, centred, squared = g.sem("hn_ready"), g.sem("hn_mean_ok"), g.sem("hn_centred"), g.sem("hn_squared")
        var_ok, std_ok, steps = g.sem("hn_var_ok"), g.sem("hn_std_ok"), g.sem("hn_steps")
        with nc.Block() as block:
            @block.gpsimd
            def _(pool):
                nc.gpsimd.memset(mean_w[:], 1.0 / P).then_inc(ready, 1)
                nc.gpsimd.memset(eps[:], EPS).then_inc(ready, 1)

            @block.tensor
            def _(pe):
                pe.wait_ge(ready, 2)
                for h in range(H_R + 1):
                    if h < H_R:
                        if h > 0:
                            pe.wait_ge(centred, h)
                        for b in range(NB):
                            mm = nc.tensor.matmul(mean[:, b, 0:TB], mean_w[:], g.br[:, 8 + h, b * TB:(b + 1) * TB],
                                                  start=True, stop=True)
                        mm.then_inc(mean_ok, 1)
                    if h > 0:
                        pe.wait_ge(squared, h)
                        if h > 1:
                            pe.wait_ge(std_ok, h - 1)
                        for b in range(NB):
                            mm = nc.tensor.matmul(var[:, b, 0:TB], mean_w[:], sq[(h - 1) % 2][:, b * TB:(b + 1) * TB],
                                                  start=True, stop=True)
                        mm.then_inc(var_ok, 1)

            @block.scalar
            def _(act):
                act.wait_ge(ready, 2)
                for h in range(H_R):
                    act.wait_ge(centred, h + 1)
                    if h >= 2:
                        act.wait_ge(var_ok, h - 1)
                    nc.scalar.activation(sq[h % 2][:], g.br[:, 8 + h, :], ACT.Square).then_inc(squared, 1)
                    act.wait_ge(var_ok, h + 1)
                    if h >= 2:
                        act.wait_ge(steps, 3 * (h - 1))
                    nc.scalar.activation(blocks_of(std[h % 2][:]), var[:, :, 0:TB], ACT.Sqrt, bias=eps[:])\
                        .then_inc(std_ok, 1)

            @block.vector
            def _(dve):
                chain = Chain(steps)
                for h in range(H_R + 1):
                    if h < H_R:
                        row = blocks_of(g.br[:, 8 + h, :])
                        dve.wait_ge(mean_ok, h + 1)
                        nc.vector.tensor_tensor(row, row, mean[:, :, 0:TB], ALU.subtract).then_inc(centred, 1)
                    if h > 0:
                        s, x, y = std[(h - 1) % 2], g.br[:, 7 + h, :], g.br[:, h - 1, :]
                        dve.wait_ge(std_ok, h)
                        chain.mark(nc.vector.reciprocal(s[:], s[:]))
                        chain.wait(dve)
                        chain.mark(nc.vector.tensor_tensor(x, x, s[:], ALU.mult))
                        chain.wait(dve)
                        chain.mark(nc.vector.scalar_tensor_tensor(y, x, g.gn_g[:, h - 1:h], y, ALU.mult, ALU.mult))


def phase_attention_in(g):
    nc, io, w = g.nc, g.io, g.w
    fox, mq = 6, 2
    pairs = fox + mq
    with ExitStack() as ctx:
        w.open(ctx, "att")
        ga = g.sb(ctx, "ga", [H_F, TW])
        gb = g.negc
        lf = g.sb(ctx, "lf", [H_F, TW])
        acc = [g.ps(ctx, f"a_acc{s}", [P, NB, 512]) for s in range(2)]
        lfn_ps = g.ps(ctx, "lfn_ps", [P, NCH + 1, H_F])
        free = [g.sem(f"a_free{s}") for s in range(2)]
        steps, a_steps = g.sem("a_dve_steps"), g.sem("a_act_steps")
        turned, nat, stored, scanned = (g.sem(n) for n in ("lf_turned", "lf_nat", "lf_stored", "lf_scanned"))
        b0, b1 = w.n
        with nc.Block() as block:
            @block.sync
            def _(sp):
                for s in range(2):
                    sp.sem_inc(free[s], 1)
                w.load(sp, 0, b0, io["w_in"][:, C_FL:C_FL + P], KD)
                w.load(sp, 1, b1, io["w_in"][:, C_FQ:C_FQ + P], KD)
                with sp.Fori(1, 2 * fox // 2) as n:
                    w.load(sp, 0, n + b0, io["w_in"][:, ds(n * (2 * P) + (C_FQ - P), P)], KD)
                    w.load(sp, 1, n + b1, io["w_in"][:, ds(n * (2 * P) + C_FQ, P)], KD)
                w.load(sp, 0, fox + b0, io["w_in"][:, C_FQ + (2 * fox - 1) * P:C_FQ + 2 * fox * P], KD)
                w.load(sp, 1, fox + b1, io["w_in"][:, C_MQ:C_MQ + P], KD)
                with sp.Fori(1, mq) as n:
                    w.load(sp, 0, n + (fox + b0), io["w_in"][:, ds(n * (2 * P) + (C_MQ - P), P)], KD)
                    w.load(sp, 1, n + (fox + b1), io["w_in"][:, ds(n * (2 * P) + C_MQ, P)], KD)
                w.load(sp, 0, fox + mq + b0, io["w_in"][:, C_MQ + 3 * P:C_MQ + 4 * P], KD)
                sp.wait_ge(nat, 1)
                sp.dma_start(io["fox_logf_prompt"][0].rearrange("(c p) h -> p c h", p=P), g.lfn[:, 0:NCH, :],
                             allow_slow_non_contiguous=True).then_inc(stored, 16)
                sp.dma_start(io["fox_logf_sample"].rearrange("b t h -> (b t) h"), g.lfn[0:TS, NCH, :])\
                    .then_inc(stored, 16)
                sp.wait_ge(stored, 32)

            @block.gpsimd
            def _(pool):
                with pool.Fori(0, pairs) as n:
                    for s in range(2):
                        w.split(pool, s, n + (b0, b1)[s], KD)
                w.split(pool, 0, pairs + b0, KD)

            @block.tensor
            def _(pe):
                with pe.Fori(0, pairs) as n:
                    for s in range(2):
                        pe.wait_ge(free[s], n + 1)
                        w.products(pe, s, n + (b0, b1)[s], KD, acc[s], g.xh, g.xl)
                pe.wait_ge(free[0], pairs + 1)
                w.products(pe, 0, pairs + b0, KD, acc[0], g.xh, g.xl)
                pe.wait_ge(scanned, 1)
                for c in range(NCH + 1):
                    n = P if c < NCH else TS
                    mm = nc.tensor.transpose(lfn_ps[0:n, c, :], lf[:, c * P:c * P + n], g.ident[0:H_F, 0:H_F])
                mm.then_inc(turned, 1)

            @block.scalar
            def _(act):
                act.wait_ge(free[0], 2)
                chain = Chain(a_steps)
                chain.mark(nc.scalar.activation(gb[:], ga[:], ACT.Abs))
                chain.wait(act)
                chain.mark(nc.scalar.activation(gb[:], gb[:], ACT.Exp, scale=-1.0))
                chain.wait(act)
                chain.mark(nc.scalar.activation(gb[:], gb[:], ACT.Ln, bias=1.0))

                def read(n, dst, scale):
                    act.wait_ge(w.done[0], n + (b0 + 2))
                    nc.scalar.mul(dst, acc[0][:, :, 0:TB], scale).then_inc(free[0], 1)
                for n in range(1, 3):
                    read(n, blocks_of(g.br[:, 8 + 2 * n - 1, :]), DF ** -0.5)
                with act.Fori(3, 7) as n:
                    read(n, blocks_of(g.fkv[:, n * 2 - 5, :]), 1.0)
                for n in range(7, 9):
                    read(n, blocks_of(g.br[:, 4 + 2 * (n - fox) - 1, :]), 1.0)

            @block.vector
            def _(dve):
                chain = Chain(steps)
                dve.wait_ge(w.done[0], b0 + 2)
                nc.vector.tensor_scalar(blocks_of(ga[:]), acc[0][0:H_F, :, 0:TB], g.b_forget[:], None, ALU.add)\
                    .then_inc(free[0], 1)

                def read(n, dst, scale):
                    dve.wait_ge(w.done[1], n + (b1 + 2))
                    nc.vector.tensor_scalar(dst, acc[1][:, :, 0:TB], scale, None, ALU.mult).then_inc(free[1], 1)
                for n in range(2):
                    read(n, blocks_of(g.br[:, 8 + 2 * n, :]), DF ** -0.5)
                dve.wait_ge(a_steps, 3)
                chain.mark(nc.vector.scalar_tensor_tensor(lf[:], ga[:], 0.0, gb[:], ALU.min, ALU.subtract))
                chain.wait(dve)
                chain.mark(nc.vector.memset(ga[:], 1.0))
                chain.wait(dve)
                nc.vector.tensor_tensor_scan(gb[:, 0:TP], ga[:, 0:TP], lf[:, 0:TP], 0.0, ALU.mult, ALU.subtract)\
                    .then_inc(scanned, 1)
                with dve.Fori(2, 6) as n:
                    read(n, blocks_of(g.fkv[:, n * 2 - 4, :]), 1.0)
                for n in range(6, 8):
                    read(n, blocks_of(g.br[:, 4 + 2 * (n - fox), :]), 1.0)
                dve.wait_ge(turned, 1)
                nc.vector.tensor_copy(g.lfn[:, 0:NCH, :], lfn_ps[:, 0:NCH, :])
                nc.vector.tensor_copy(g.lfn[0:TS, NCH, :], lfn_ps[0:TS, NCH, :]).then_inc(nat, 1)
        w.n = [b0 + pairs + 1, b1 + pairs]


def phase_kv_natural(g):
    nc, io = g.nc, g.io
    with ExitStack() as ctx:
        kn = [g.sb(ctx, f"kv_kn{s}", [P, 4, P]) for s in range(2)]
        kt = [g.ps(ctx, f"kv_kt{s}", [P, 4, P]) for s in range(2)]
        vt = [g.ps(ctx, f"kv_vt{s}", [P, 4, P]) for s in range(2)]
        turned = g.sem("kv_turned")
        k_ok, v_ok = g.sem("kv_k_ok"), g.sem("kv_v_ok")
        k_out = [g.sem(f"kv_k_out{s}") for s in range(2)]
        v_out = g.sem("kv_v_out")
        with nc.Block() as block:
            @block.gpsimd
            def _(pool):
                nc.gpsimd.tensor_copy(g.k_s[:], g.fkv[:, 0:4, TP:T])

            @block.tensor
            def _(pe):
                for c in range(NCH + 1):
                    n = P if c < NCH else TS
                    at = slice(c * P, c * P + n)
                    pe.wait_ge(k_ok, c + 1)
                    pe.wait_ge(v_ok, c + 1)
                    for j in range(4):
                        nc.tensor.transpose(kt[c % 2][0:n, j, :], g.fkv[:, j, at], g.ident[:])
                    for j in range(4):
                        mm = nc.tensor.transpose(vt[c % 2][0:n, j, :], g.fkv[:, 4 + j, at], g.ident[:])
                    mm.then_inc(turned, 1)

            @block.scalar
            def _(act):
                def keys(c, half, s, n):
                    act.wait_ge(turned, c + 1)
                    act.wait_ge(k_out[s], half * 16 + 16)
                    nc.scalar.copy(kn[s][0:n], kt[s][0:n]).then_inc(k_ok, 1)
                with act.Fori(0, NCH // 2) as i:
                    for s in range(2):
                        keys(i * 2 + s, i, s, P)
                keys(NCH, NCH // 2, 0, TS)

            @block.vector
            def _(dve):
                with dve.Fori(0, NCH // 2) as i:
                    for s in range(2):
                        dst = g.fkv[:, 4:8, ds(i * (2 * P) + s * P, P)]
                        dve.wait_ge(turned, i * 2 + (s + 1))
                        nc.vector.tensor_copy(dst, vt[s][:]).then_inc(v_ok, 1)
                dve.wait_ge(turned, NCH + 1)
                nc.vector.tensor_copy(g.v_s[0:TS], vt[0][0:TS].rearrange("p a b -> p (a b)")).then_inc(v_ok, 1)

            @block.sync
            def _(sp):
                sp.sem_inc(k_ok, 2)
                sp.sem_inc(v_ok, 2)
                for s in range(2):
                    sp.sem_inc(k_out[s], 16)
                with sp.Fori(0, NCH // 2) as i:
                    for s in range(2):
                        at = ds(i * (2 * P) + s * P, P)
                        k_dst = io["fox_k_prompt"][0, at].rearrange("t h d -> t (h d)")
                        v_dst = io["fox_v_prompt"][0, at].rearrange("t (j x) d -> t j (x d)", j=4)
                        v_src = g.fkv[:, 4:8, at]
                        sp.wait_ge(k_ok, i * 2 + (s + 3))
                        sp.dma_start(k_dst, kn[s][:].rearrange("p a b -> p (a b)")).then_inc(k_out[s], 16)
                        sp.wait_ge(v_ok, i * 2 + (s + 3))
                        sp.dma_start(v_dst, v_src).then_inc(v_out, 16)
                sp.wait_ge(k_ok, NCH + 3)
                sp.dma_start(io["fox_k_sample"].rearrange("b t h d -> (b t) (h d)"),
                             kn[0][0:TS].rearrange("p a b -> p (a b)")).then_inc(k_out[0], 16)
                sp.wait_ge(v_ok, NCH + 3)
                sp.dma_start(io["fox_v_sample"].rearrange("b t h d -> (b t) (h d)"), g.v_s[0:TS]).then_inc(v_out, 16)
                for s in range(2):
                    sp.wait_ge(k_out[s], 16 * (NCH // 2 + 2 - s))
                sp.wait_ge(v_out, 16 * (NCH + 1))


def phase_cross_prompt(g):
    nc = g.nc
    MT = N_MEM // P
    scale = DM ** -0.5
    UNITS = 2 * NCH
    with ExitStack() as ctx:
        q = g.sb(ctx, "c_q", [P, H_M, P])
        prob = [g.sb(ctx, f"c_prob{x}", [P, 2, N_MEM]) for x in range(2)]
        pt = [g.sb(ctx, f"c_pt{x}", [P, 2 * MT, P]) for x in range(2)]
        nmax, ssum, rsum = (g.sb(ctx, "c_" + n, [P, 2, 2]) for n in ("nmax", "ssum", "rsum"))
        sc = [g.ps(ctx, f"c_sc{x}", [P, 2, N_MEM]) for x in range(2)]
        ptp = [g.ps(ctx, f"c_ptp{x}", [P, 2 * MT, P]) for x in range(2)]
        o = g.ps(ctx, "c_o", [P, H_M, P])
        staged, scored, steps = g.sem("c_staged"), g.sem("c_scored"), g.sem("c_steps")
        maxed, exped, normed = g.sem("c_maxed"), g.sem("c_exped"), g.sem("c_normed")
        turned, pt_ok, out_ok = g.sem("c_turned"), g.sem("c_pt_ok"), g.sem("c_out_ok")
        o_read = g.sem("c_o_read")
        STEPS = 2

        def pipeline(engine, first, unit):
            first()
            with engine.Fori(0, NCH - 1) as c:
                for x in range(2):
                    unit(c, x, True)
            unit(NCH - 1, 0, True)
            unit(NCH - 1, 1, False)

        def following(c, x):
            return (c + x, 1 - x)

        with nc.Block() as block:
            @block.sync
            def _(sp):
                for sem in (exped, normed, turned, pt_ok, out_ok):
                    sp.sem_inc(sem, 2)
                sp.sem_inc(o_read, 1)
                sp.sem_inc(scored, 2)

            @block.gpsimd
            def _(pool):
                with pool.Fori(0, NCH) as c:
                    for x in range(2):
                        src = g.br[:, 4 + 2 * x:6 + 2 * x, ds(c * P, P)]
                        pool.wait_ge(scored, c * 2 + (x + 1))
                        pool.sem_inc(g.w.passed, 1)
                        nc.gpsimd.tensor_copy(q[:, 2 * x:2 * x + 2, :], src).then_inc(staged, 1)

            @block.tensor
            def _(pe):
                def scores(c, x):
                    pe.wait_ge(staged, c * 2 + (x + 1))
                    pe.wait_ge(exped, c * 2 + (x + 1))
                    for h in range(2):
                        mm = nc.tensor.matmul(sc[x][:, h, :], q[:, 2 * x + h, :], g.mem_kt[:, 2 * x + h, :],
                                              start=True, stop=True)
                    mm.then_inc(scored, 1)

                def unit(c, x, more):
                    if more:
                        scores(*following(c, x))
                    pe.wait_ge(normed, c * 2 + (x + 3))
                    pe.wait_ge(pt_ok, c * 2 + (x + 1))
                    for h in range(2):
                        for m in range(MT):
                            mm = nc.tensor.transpose(ptp[x][:, h * MT + m, :], prob[x][:, h, m * P:(m + 1) * P],
                                                     g.ident[:])
                    mm.then_inc(turned, 1)
                    pe.wait_ge(pt_ok, c * 2 + (x + 3))
                    if x == 0:
                        pe.wait_ge(o_read, c + 1)
                    for h in range(2):
                        for m in range(MT):
                            v = g.mem_v[:, m, (2 * x + h) * DM:(2 * x + h + 1) * DM]
                            mm = nc.tensor.matmul(o[:, 2 * x + h, :], v, pt[x][:, h * MT + m, :],
                                                  start=(m == 0), stop=(m == MT - 1))
                    mm.then_inc(out_ok, 1)
                pipeline(pe, lambda: scores(0, 0), unit)

            @block.scalar
            def _(act):
                act.preload_act_table(ACT.Exp)

                def start(c, x):
                    act.wait_ge(maxed, c * 2 + (x + 1))
                    act.wait_ge(turned, c * 2 + (x + 1))
                    act.wait_ge(normed, c * 2 + (x + 1))
                    for h in range(2):
                        ins = nc.scalar.activation(prob[x][:, h, :], sc[x][:, h, :], ACT.Exp, bias=nmax[:, x, h:h + 1],
                                                   scale=scale, accum_out=ssum[:, x, h:h + 1])
                    ins.then_inc(exped, 1)

                def unit(c, x, more):
                    if more:
                        start(*following(c, x))
                    if x == 1:
                        dst = g.br[:, 4:8, ds(c * P, P)]
                        act.wait_ge(out_ok, c * 2 + 4)
                        nc.scalar.copy(dst, o[:]).then_inc(o_read, 1)
                pipeline(act, lambda: start(0, 0), unit)

            @block.vector
            def _(dve):
                def start(c, x):
                    dve.wait_ge(scored, c * 2 + (x + 3))
                    dve.wait_ge(exped, c * 2 + (x + 1))
                    nc.vector.tensor_reduce(nmax[:, x, :], sc[x][:], AX.X, ALU.max).then_inc(steps, 1)
                    dve.wait_ge(steps, c * (2 * STEPS) + (x * STEPS + 1))
                    nc.vector.tensor_scalar(nmax[:, x, :], nmax[:, x, :], -scale, None, ALU.mult).then_inc(maxed, 1)

                def unit(c, x, more):
                    n0 = c * (2 * STEPS)
                    dve.wait_ge(exped, c * 2 + (x + 3))
                    nc.vector.reciprocal(rsum[:, x, :], ssum[:, x, :]).then_inc(steps, 1)
                    dve.wait_ge(steps, n0 + (x * STEPS + STEPS))
                    nc.vector.tensor_tensor(prob[x][:], prob[x][:], rsum[:, x, :].unsqueeze(2).broadcast_to([P, 2, N_MEM]),
                                            ALU.mult).then_inc(normed, 1)
                    if more:
                        start(*following(c, x))
                    dve.wait_ge(turned, c * 2 + (x + 3))
                    dve.wait_ge(out_ok, c * 2 + (x + 1))
                    nc.vector.tensor_copy(pt[x][:], ptp[x][:]).then_inc(pt_ok, 1)
                pipeline(dve, lambda: start(0, 0), unit)


def phase_cross_sample(g):
    nc, io = g.nc, g.io
    MT = N_MEM // P
    ROW = P // H_M
    scale = DM ** -0.5
    with ExitStack() as ctx:
        q = [g.sb(ctx, f"e_q{s}", [P, H_M, ROW]) for s in range(2)]
        kin = [g.sb(ctx, f"e_kin{s}", [P, MT, H_M * DM]) for s in range(2)]
        vin = [g.sb(ctx, f"e_vin{s}", [P, MT, H_M * DM]) for s in range(2)]
        kts = g.sb(ctx, "e_kts", [P, MT, H_M, P])
        prob, pt = g.sb(ctx, "e_prob", [P, N_MEM]), g.sb(ctx, "e_pt", [P, MT, P])
        nmax, ssum, rsum = (g.sb(ctx, "e_" + n, [P, 1]) for n in ("nmax", "ssum", "rsum"))
        on = g.sb(ctx, "e_on", [P, DM])
        ktp = [g.ps(ctx, f"e_ktp{m}", [P, H_M, P]) for m in range(MT)]
        sc = g.ps(ctx, "e_sc", [P, N_MEM])
        ptp = g.ps(ctx, "e_ptp", [P, MT, P])
        ov, ot = g.ps(ctx, "e_ov", [P, DM]), g.ps(ctx, "e_ot", [P, P])
        k_in_ok = [g.sem(f"e_k_in_ok{s}") for s in range(2)]
        v_in_ok = [g.sem(f"e_v_in_ok{s}") for s in range(2)]
        zeroed, q_ok = g.sem("e_zeroed"), g.sem("e_q_ok")
        k_turned = g.sem("e_k_turned")
        k_ok = [g.sem(f"e_k_ok{m}") for m in range(MT)]
        scored = g.sem("e_scored")
        maxed, exped, turned, pt_ok = g.sem("e_maxed"), g.sem("e_exped"), g.sem("e_turned"), g.sem("e_pt_ok")
        valued = g.sem("e_valued")
        on_ok, ot_ok, out_ok, steps = g.sem("e_on_ok"), g.sem("e_ot_ok"), g.sem("e_out_ok"), g.sem("e_steps")
        N = H_M * MT
        with nc.Block() as block:
            @block.sync
            def _(sp):
                for m in range(MT):
                    sp.sem_inc(k_ok[m], 1)
                sp.sem_inc(k_turned, 2)
                sp.sem_inc(valued, 2 * N)
                sp.sem_inc(out_ok, 1)
                sp.sem_inc(scored, N)
                with sp.Fori(0, NSEQ // 2) as j:
                    for e in range(2):
                        ks = io["cache_mem_k"][j * 2 + e].rearrange("(m p) h d -> p m (h d)", p=P)
                        vs = io["cache_mem_v"][j * 2 + e].rearrange("(m p) h d -> p m (h d)", p=P)
                        sp.wait_ge(k_turned, j * 2 + (e + 1))
                        sp.dma_start(kin[e][:], ks).then_inc(k_in_ok[e], 16)
                        sp.wait_ge(valued, j * (2 * N) + (e + 1) * N)
                        sp.dma_start(vin[e][:], vs).then_inc(v_in_ok[e], 16)

            @block.gpsimd
            def _(pool):
                for e in range(2):
                    nc.gpsimd.memset(q[e][:], 0.0).then_inc(zeroed, 1)
                pool.wait_ge(zeroed, 2)
                with pool.Fori(0, NSEQ // 2) as j:
                    for e in range(2):
                        src = g.br[:, 4:8, ds(j * (2 * LSEQ) + (TP + e * LSEQ), LSEQ)]
                        pool.wait_ge(valued, j * (2 * N) + (e + 1) * N)
                        pool.sem_inc(g.w.passed, 1)
                        nc.gpsimd.tensor_copy(q[e][:, :, 0:LSEQ], src).then_inc(q_ok, 1)

            @block.tensor
            def _(pe):
                def turn(b, e, half):
                    pe.wait_ge(k_in_ok[e], half * 16 + 16)
                    for m in range(MT):
                        pe.wait_ge(k_ok[m], b + 1)
                    for m in range(MT):
                        for h in range(H_M):
                            mm = nc.tensor.transpose(ktp[m][:, h, :], kin[e][:, m, h * DM:(h + 1) * DM], g.ident[:])
                    mm.then_inc(k_turned, 1)

                def scores(b, e):
                    pe.wait_ge(q_ok, b + 1)
                    for m in range(MT):
                        pe.wait_ge(k_ok[m], b + 2)
                        for h in range(H_M):
                            nc.tensor.matmul(sc[h * ROW:(h + 1) * ROW, m * P:(m + 1) * P], q[e][:, h, :],
                                             kts[:, m, h, :], start=True, stop=True).then_inc(scored, 1)

                def first():
                    turn(0, 0, 0)
                    scores(0, 0)

                def body(b, e, half, more):
                    if more:
                        turn(b + 1, 1 - e, half + e)
                    pe.wait_ge(exped, b + 1)
                    pe.sem_inc(g.w.passed, 1)
                    for m in range(MT):
                        mm = nc.tensor.transpose(ptp[:, m, :], prob[:, m * P:(m + 1) * P], g.ident[:])
                    mm.then_inc(turned, 1)
                    if more:
                        scores(b + 1, 1 - e)
                    pe.wait_ge(v_in_ok[e], half * 16 + 16)
                    pe.wait_ge(pt_ok, b + 1)
                    for m in range(MT):
                        for h in range(H_M):
                            nc.tensor.matmul(ov[h * ROW:(h + 1) * ROW, :], pt[:, m, h * ROW:(h + 1) * ROW],
                                             vin[e][:, m, h * DM:(h + 1) * DM], start=(m == 0), stop=(m == MT - 1),
                                             skip_group_check=True).then_inc(valued, 1)
                    pe.wait_ge(on_ok, b + 1)
                    pe.wait_ge(out_ok, b + 1)
                    nc.tensor.transpose(ot[:], on[:], g.ident[:]).then_inc(ot_ok, 1)
                sweep(pe, first, body)

            @block.scalar
            def _(act):
                act.preload_act_table(ACT.Exp)

                def keys(b):
                    act.wait_ge(k_turned, b + 3)
                    act.wait_ge(scored, b * N + N)
                    nc.scalar.copy(kts[:, 0], ktp[0][:]).then_inc(k_ok[0], 1)

                def body(b, e, half, more):
                    act.wait_ge(maxed, b + 1)
                    nc.scalar.activation(prob[:], sc[:], ACT.Exp, bias=nmax[:], scale=scale, accum_out=ssum[:])\
                        .then_inc(exped, 1)
                    if more:
                        keys(b + 1)
                sweep(act, lambda: keys(0), body)

            @block.vector
            def _(dve):
                STEPS = 2

                def keys(b):
                    dve.wait_ge(k_turned, b + 3)
                    dve.wait_ge(scored, b * N + N)
                    nc.vector.tensor_copy(kts[:, 1], ktp[1][:]).then_inc(k_ok[1], 1)

                def maximum(b):
                    chain = Chain(steps, b * STEPS)
                    dve.wait_ge(scored, b * N + 2 * N)
                    chain.mark(nc.vector.tensor_reduce(nmax[:], sc[:], AX.X, ALU.max))
                    chain.wait(dve)
                    nc.vector.tensor_scalar(nmax[:], nmax[:], -scale, None, ALU.mult).then_inc(maxed, 1)

                def first():
                    keys(0)
                    maximum(0)

                def body(b, e, half, more):
                    if more:
                        keys(b + 1)
                    dve.wait_ge(turned, b + 1)
                    dve.wait_ge(valued, b * N + 2 * N)
                    nc.vector.tensor_copy(pt[:], ptp[:]).then_inc(pt_ok, 1)
                    dve.wait_ge(exped, b + 1)
                    nc.vector.reciprocal(rsum[:], ssum[:]).then_inc(steps, 1)
                    dve.wait_ge(steps, b * STEPS + STEPS)
                    if more:
                        maximum(b + 1)
                    dve.wait_ge(valued, b * N + 3 * N)
                    nc.vector.tensor_scalar(on[:], ov[:], rsum[:], None, ALU.mult).then_inc(on_ok, 1)
                    dst = g.br[:, 4:8, ds(b * LSEQ + TP, LSEQ)]
                    dve.wait_ge(ot_ok, b + 1)
                    nc.vector.tensor_copy(dst, ot[:].rearrange("p (h q) -> p h q", h=H_M)[:, :, 0:LSEQ])\
                        .then_inc(out_ok, 1)
                    dve.wait_ge(out_ok, b + 2)
                sweep(dve, first, body)


def phase_fox_prompt(g):
    nc = g.nc
    UNITS = 2 * NCH
    HALF = NCH // 2
    with ExitStack() as ctx:
        qz = g.sb(ctx, "p_qz", [P, 2, TP])
        v_now = g.mem_kt[:].rearrange("p a b -> p (a b)")
        pt = [g.mem_v[:].rearrange("p a (b k) -> p (a b) k", k=P), g.sb(ctx, "p_pt", [P, NCH, P])]
        prob = [g.sb(ctx, f"p_prob{s}", [P, TP]) for s in range(2)]
        nmax, ssum, rsum = (g.sb(ctx, "p_" + n, [P, 2]) for n in ("nmax", "ssum", "rsum"))
        diag = g.sb(ctx, "p_diag", [P, 2, P])
        inv = g.sb(ctx, "p_inv", [P, P])
        own = g.sb(ctx, "p_own", [P, 2])
        sel = g.sb(ctx, "p_sel", [H_F, 2, P], F32R)
        causal, ident = g.sb(ctx, "p_causal", [P, P], F32R), g.sb(ctx, "p_ident", [P, P], F32R)
        neg_hi = g.sb(ctx, "p_neg_hi", [H_F, TP], F32R)
        neg_lo = g.sb(ctx, "p_neg_lo", [H_F, TP], F32R)
        sc = [g.ps(ctx, f"p_sc{s}", [P, TP]) for s in range(2)]
        ptp = [g.ps(ctx, f"p_ptp{s}", [P, HALF, P]) for s in range(2)]
        o, spread = g.ps(ctx, "p_o", [P, P]), g.ps(ctx, "p_spread", [P, P])
        const, own_ok, split = g.sem("p_const"), g.sem("p_own_ok"), g.sem("p_split")
        q_staged, v_staged, sel_ok = g.sem("p_q_staged"), g.sem("p_v_staged"), g.sem("p_sel_ok")
        scored, maxed = g.sem("p_scored"), g.sem("p_maxed")
        exped, diag_ok, spread_ok = g.sem("p_exped"), g.sem("p_diag_ok"), g.sem("p_spread_ok")
        turned = [g.sem(f"p_turned{s}") for s in range(2)]
        pt_ok = [g.sem(f"p_pt_ok{s}") for s in range(2)]
        valued, recip = g.sem("p_valued"), g.sem("p_recip")
        o_read, inv_ok = g.sem("p_o_read"), g.sem("p_inv_ok")

        def block_of(j):
            return NCH - 1 - j // 2
        with nc.Block() as block:
            @block.sync
            def _(sp):
                sp.dma_start(own[:], g.io["own_rows"]).then_inc(const, 16)
                for sem in (exped, diag_ok, spread_ok, turned[0]):
                    sp.sem_inc(sem, 2)
                for sem in (pt_ok[0], pt_ok[1], o_read, inv_ok):
                    sp.sem_inc(sem, 1)
                sp.sem_inc(valued, UNITS)
                sp.wait_ge(const, 16)

            @block.gpsimd
            def _(pool):
                pool.wait_ge(const, 16)

                def pick(p):
                    src = g.ident[0:H_F, ds(p * 2, 2)].unsqueeze(2).broadcast_to([H_F, 2, P])
                    if not isinstance(p, int):
                        pool.wait_ge(v_staged, p * NCH + NCH)
                        pool.sem_inc(g.w.passed, 1)
                    nc.gpsimd.tensor_copy(sel[:], src).then_inc(sel_ok, 1)

                def stage(p):
                    for x in range(NCH):
                        i = NCH - 1 - x
                        at = slice(i * P, (i + 1) * P)
                        q_src, v_src = g.br[:, p + 8, at], g.fkv[:, p + 4, at]
                        pool.wait_ge(valued, p * UNITS + (2 * x + 2))
                        pool.sem_inc(g.w.passed, 1)
                        nc.gpsimd.tensor_tensor(qz[:, :, at], q_src.unsqueeze(1).broadcast_to([P, 2, P]),
                                                own[:].unsqueeze(2).broadcast_to([P, 2, P]), ALU.mult)\
                            .then_inc(q_staged, 1)
                        nc.gpsimd.tensor_copy(v_now[:, at], v_src).then_inc(v_staged, 1)
                pick(0)
                stage(0)
                with pool.Fori(1, PAIRS) as p:
                    stage(p)
                    pick(p)

            @block.tensor
            def _(pe):
                pe.wait_ge(split, 4)
                with pe.Fori(0, PAIRS) as p:
                    n0 = p * UNITS

                    def scores(j):
                        i, s = block_of(j), j % 2
                        keys = (i + 1) * P
                        pe.wait_ge(q_staged, p * NCH + (j // 2 + 1))
                        if j == 0:
                            pe.wait_ge(sel_ok, p + 1)
                        pe.wait_ge(exped, n0 + (j + 1))
                        for k0 in range(0, keys, 512):
                            k1 = min(k0 + 512, keys)
                            out = sc[s][:, k0:k1]
                            nc.tensor.matmul(out, qz[:, s, i * P:keys], g.fkv[:, p, k0:k1], start=True, stop=False)
                            nc.tensor.matmul(out, sel[:, s, :], neg_hi[:, k0:k1], start=False, stop=False)
                            nc.tensor.matmul(out, sel[:, s, :], neg_lo[:, k0:k1], start=False, stop=(k1 < keys))
                        nc.tensor.matmul(sc[s][:, i * P:keys], ident[:], causal[:], start=False, stop=True)\
                            .then_inc(scored, 1)

                    def turn(j):
                        i, s = block_of(j), j % 2
                        pe.wait_ge(exped, n0 + (j + 3))
                        for x in range(2 if i >= HALF else 1):
                            pe.wait_ge(pt_ok[x], (p * (2 * HALF) if x else n0) + (j + 1))
                            for k in range(x * HALF, min(i + 1, (x + 1) * HALF)):
                                mm = nc.tensor.transpose(ptp[x][:, k - x * HALF, :], prob[s][:, k * P:(k + 1) * P], g.ident[:])
                            mm.then_inc(turned[x], 1)

                    def products(j):
                        i, s = block_of(j), j % 2
                        if j == 0:
                            pe.wait_ge(v_staged, p * NCH + NCH)
                        if s == 0:
                            pe.wait_ge(o_read, p * NCH + (j // 2 + 1))
                        for x in range(2 if i >= HALF else 1):
                            pe.wait_ge(pt_ok[x], (p * (2 * HALF) if x else n0) + (j + 2))
                            for k in range(x * HALF, min(i + 1, (x + 1) * HALF)):
                                v = v_now[:, k * P + s * DF:k * P + (s + 1) * DF]
                                mm = nc.tensor.matmul(o[HALVES[s], :], v, pt[s][:, k, :], start=(k == 0), stop=(k == i))
                        mm.then_inc(valued, 1)
                        pe.wait_ge(diag_ok, n0 + (j + 3))
                        if s == 0:
                            pe.wait_ge(inv_ok, p * NCH + (j // 2 + 1))
                        nc.tensor.matmul(spread[HALVES[s], :], g.ones[:, 0:DF], diag[:, s, :], start=True, stop=True)\
                            .then_inc(spread_ok, 1)

                    scores(0)
                    for j in range(UNITS):
                        if j + 1 < UNITS:
                            scores(j + 1)
                        turn(j)
                        if j >= 1:
                            products(j - 1)
                    products(UNITS - 1)

            @block.scalar
            def _(act):
                act.preload_act_table(ACT.Exp)
                nc.scalar.copy(neg_hi[:], g.negc[:, 0:TP]).then_inc(split, 1)
                nc.scalar.copy(causal[:], g.causal[:]).then_inc(split, 1)
                nc.scalar.copy(ident[:], g.ident[:]).then_inc(split, 1)
                with act.Fori(0, PAIRS) as p:
                    n0 = p * UNITS
                    for j in range(UNITS + 2):
                        if 1 <= j <= UNITS and block_of(j - 1) >= HALF:
                            n = block_of(j - 1) + 1 - HALF
                            act.wait_ge(turned[1], p * (2 * HALF) + j)
                            act.wait_ge(valued, n0 + (j - 2 + UNITS))
                            nc.scalar.copy(pt[(j - 1) % 2][:, HALF:HALF + n, :], ptp[1][:, 0:n, :]).then_inc(pt_ok[1], 1)
                        if j < UNITS:
                            s, keys = j % 2, (block_of(j) + 1) * P
                            act.wait_ge(maxed, n0 + (j + 1))
                            act.wait_ge(turned[0], n0 + (j + 1))
                            act.wait_ge(diag_ok, n0 + (j + 1))
                            nc.scalar.activation(prob[s][:, 0:keys], sc[s][:, 0:keys], ACT.Exp, bias=nmax[:, s:s + 1],
                                                 accum_out=ssum[:, s:s + 1]).then_inc(exped, 1)
                        if j >= 3 and j % 2:
                            act.wait_ge(spread_ok, n0 + (j + 1))
                            act.wait_ge(o_read, p * NCH + j // 2)
                            nc.scalar.copy(inv[:], spread[:]).then_inc(inv_ok, 1)

            @block.vector
            def _(dve):
                dve.wait_ge(split, 1)
                nc.vector.tensor_tensor(neg_lo[:], g.negc[:, 0:TP], neg_hi[:].bitcast(F32), ALU.subtract).then_inc(split, 1)
                with dve.Fori(0, PAIRS) as p:
                    n0 = p * UNITS

                    def output(j):
                        i = block_of(j)
                        dst = g.br[:, p + 8, i * P:(i + 1) * P]
                        dve.wait_ge(valued, n0 + (j + 1 + UNITS))
                        dve.wait_ge(inv_ok, p * NCH + (j // 2 + 2))
                        nc.vector.tensor_tensor(dst, o[:], inv[:], ALU.mult).then_inc(o_read, 1)

                    for j in range(UNITS + 2):
                        if 1 <= j <= UNITS:
                            s = (j - 1) % 2
                            dve.wait_ge(exped, n0 + (j + 2))
                            nc.vector.reciprocal(rsum[:, s:s + 1], ssum[:, s:s + 1]).then_inc(recip, 1)
                            dve.wait_ge(recip, n0 + j)
                            dve.wait_ge(spread_ok, n0 + j)
                            nc.vector.tensor_scalar(diag[:, s, :], g.ident[:], rsum[:, s:s + 1], None,
                                                    ALU.mult).then_inc(diag_ok, 1)
                        if j < UNITS:
                            s, keys = j % 2, (block_of(j) + 1) * P
                            dve.wait_ge(scored, n0 + (j + 1))
                            nc.vector.tensor_reduce(nmax[:, s:s + 1], sc[s][:, 0:keys], AX.X, ALU.max, negate=True)\
                                .then_inc(maxed, 1)
                        if 1 <= j <= UNITS:
                            n = min(block_of(j - 1) + 1, HALF)
                            dve.wait_ge(turned[0], n0 + (j + 2))
                            dve.wait_ge(valued, n0 + (j - 2 + UNITS))
                            nc.vector.tensor_copy(pt[(j - 1) % 2][:, 0:n, :], ptp[0][:, 0:n, :]).then_inc(pt_ok[0], 1)
                        if j >= 3 and j % 2:
                            output(j - 2)


QUAD = 4
CHUNK = 8
ROWS = 32
NEW = PAST + TS


def phase_sample_bias(g, qz, bias_n, bias_past):
    nc, io = g.nc, g.io
    HG = NPG // 2
    with ExitStack() as ctx:
        idx = g.sb(ctx, "d_idx", [P, 2], I32)
        rows = [g.sb(ctx, f"d_rows{j}", [P, PAGE * H_F]) for j in range(2)]
        lft = g.sb(ctx, "d_lft", [P, NSEQ, NPG, H_F])
        tot = [g.sb(ctx, f"d_tot{s}", [P, NSEQ, NPG + 1, H_F]) for s in range(2)]
        after, upto = g.sb(ctx, "d_after", [P, P]), g.sb(ctx, "d_upto", [TS, TS])
        mask, lfx = g.sb(ctx, "d_mask", [P, NSEQ, TS]), g.sb(ctx, "d_lfx", [TS, PAIRS, 4, LSEQ])
        out = g.sb(ctx, "d_out", [P, 2 * NSEQ, P])
        t = [g.ps(ctx, f"d_t{j}", [P, H_F, P]) for j in range(2)]
        sums = g.ps(ctx, "d_sums", [P, NSEQ, P])
        cn = g.ps(ctx, "d_cn", [P, TS])
        const, paged, turned, copied = g.sem("d_const"), g.sem("d_paged"), g.sem("d_turned"), g.sem("d_copied")
        steps, summed, read, stored = g.sem("d_steps"), g.sem("d_summed"), g.sem("d_read"), g.sem("d_stored")
        expanded, cn_ok, qz_ok = g.sem("d_expanded"), g.sem("d_cn_ok"), g.sem("d_qz_ok")
        indexed = g.sem("d_indexed")
        with nc.Block() as block:
            @block.sync
            def _(sp):
                sp.dma_start(idx[:], io["page_table"].rearrange("b n -> (b n)").rearrange("(j p) -> p j", p=P),
                             allow_slow_non_contiguous=True).then_inc(indexed, 16)
                for name, dst in (("after", after), ("upto", upto), ("new_mask", mask)):
                    sp.dma_start(dst[:], io[name]).then_inc(const, 16)
                sp.wait_ge(const, 48)
                for x in range(2):
                    sp.wait_ge(read, x + 1)
                    c = slice(x * NSEQ, (x + 1) * NSEQ)
                    sp.dma_start(bias_past[c].rearrange("c g h t -> (g h) c t"), out[:, c, :]).then_inc(stored, 16)
                sp.wait_ge(stored, 32)

            @block.gpsimd
            def _(pool):
                pool.wait_ge(indexed, 16)
                gates = io["cache_fox_logf"].rearrange("n t h -> n (t h)")
                for j in range(2):
                    nc.gpsimd.indirect_dma_start(out=rows[j][:], out_offset=None, in_=gates,
                                                 in_offset=bass.IndirectOffsetOnAxis(ap=idx[:, j:j + 1], axis=0))\
                        .then_inc(paged, 16)
                nc.gpsimd.memset(qz[:], 0.0).then_inc(qz_ok, 1)
                pool.wait_ge(qz_ok, 1)
                pool.wait_ge(paged, 32)
                q = g.br[:, 8:12, TP:T].rearrange("p a (b q) -> p b a q", q=LSEQ)
                for b in range(NSEQ):
                    for s in range(2):
                        nc.gpsimd.tensor_copy(qz[HALVES[s], b, :, s * LSEQ:(s + 1) * LSEQ], q[HALVES[s], b])

            @block.tensor
            def _(pe):
                pe.wait_ge(paged, 32)
                for j in range(2):
                    by_head = rows[j][:].rearrange("p (t h) -> p h t", h=H_F)
                    for h in range(H_F):
                        mm = nc.tensor.transpose(t[j][:, h, :], by_head[:, h, :], g.ident[:])
                    mm.then_inc(turned, 1)
                pe.wait_ge(const, 48)
                pe.wait_ge(expanded, 2)
                nc.tensor.matmul(cn[:], lfx[:].rearrange("p a s q -> p (a s q)"), upto[:], start=True, stop=True)\
                    .then_inc(cn_ok, 1)
                pe.wait_ge(copied, 2)
                pe.wait_ge(steps, 6)
                for c in range(2 * NSEQ):
                    if c == NSEQ:
                        pe.wait_ge(read, 1)
                    b, x = divmod(c, 2)
                    own = lft[:, b, x * HG:(x + 1) * HG, :].rearrange("p g h -> p (g h)")
                    behind = tot[1][:, b, x * HG + 1:(x + 1) * HG + 1, :].rearrange("p g h -> p (g h)")
                    nc.tensor.matmul(sums[:, c % NSEQ, :], own, after[:], start=True, stop=False)
                    mm = nc.tensor.matmul(sums[:, c % NSEQ, :], behind, g.ones[:], start=False, stop=True)
                    if c % NSEQ == NSEQ - 1:
                        mm.then_inc(summed, 1)

            @block.scalar
            def _(act):
                for j in range(2):
                    act.wait_ge(turned, j + 1)
                    nc.scalar.copy(lft[:, j * 4:j * 4 + 4].rearrange("p b g h -> p h (b g)"), t[j][:])\
                        .then_inc(copied, 1)
                for x in range(2):
                    act.wait_ge(summed, x + 1)
                    nc.scalar.copy(out[:, x * NSEQ:(x + 1) * NSEQ, :], sums[:]).then_inc(read, 1)

            @block.vector
            def _(dve):
                chain = Chain(steps)
                nc.vector.memset(lfx[:], 0.0).then_inc(expanded, 1)
                nc.vector.memset(g.v_s[TS:P, :], 0.0)
                for s in range(2):
                    nc.vector.memset(tot[s][:, :, NPG, :], 0.0)
                dve.wait_ge(expanded, 1)
                nc.vector.tensor_copy(lfx[:, :, 0:2, :],
                                      g.lfn[0:TS, NCH, :].rearrange("p (a s) -> p a s", s=2).unsqueeze(3)
                                      .broadcast_to([TS, PAIRS, 2, LSEQ])).then_inc(expanded, 1)
                dve.wait_ge(copied, 2)
                chain.mark(nc.vector.tensor_copy(tot[0][:, :, 0:NPG, :].rearrange("p b g h -> p b (g h)"),
                                                 lft[:].rearrange("p b g h -> p b (g h)")))
                chain.wait(dve)
                now, step = 0, 1
                while step < NPG:
                    x, y = tot[now], tot[1 - now]
                    nc.vector.tensor_tensor(y[:, :, 0:NPG - step, :].rearrange("p b g h -> p b (g h)"),
                                            x[:, :, 0:NPG - step, :].rearrange("p b g h -> p b (g h)"),
                                            x[:, :, step:NPG, :].rearrange("p b g h -> p b (g h)"), ALU.add)
                    chain.mark(nc.vector.tensor_copy(y[:, :, NPG - step:NPG, :], x[:, :, NPG - step:NPG, :]))
                    chain.wait(dve)
                    now, step = 1 - now, step * 2
                assert now == 1 and chain.n == 6
                dve.wait_ge(const, 48)
                dve.wait_ge(cn_ok, 1)
                nc.vector.tensor_tensor(bias_n[:], mask[:], cn[:].unsqueeze(1).broadcast_to([P, NSEQ, TS]), ALU.subtract)


def phase_fox_sample(g, qz, bias_n, bias_past):
    nc, io = g.nc, g.io
    QUADS = NPG // QUAD
    CHUNKS = NPG // CHUNK
    Q_V = QUADS + 1
    USED = PAIRS * (NPG + 1)
    with ExitStack() as ctx:
        kt = [g.mem_kt[:, 2 * s:2 * s + 2, :].rearrange("p a (b k) -> p (a b) k", k=P) for s in range(2)]
        kt.append(g.mem_v[:, 0, :].rearrange("p (a k) -> p a k", k=P))
        pt = g.mem_v[:, 1, :].rearrange("p (a k) -> p a k", k=P)
        st = [g.sb(ctx, f"d_st{s}", [P, PAST + P]) for s in range(2)]
        k_in = [g.sb(ctx, f"d_k_in{s}", [P, H_F * DF]) for s in range(CHUNK)]
        v_in = [g.sb(ctx, f"d_v_in{s}", [P, H_F * DF]) for s in range(CHUNK)]
        q_now = [g.sb(ctx, f"d_q{s}", [P, PAIRS, ROWS]) for s in range(2)]
        tops, nmax = g.sb(ctx, "d_tops", [P, QUADS + 1]), g.sb(ctx, "d_nmax", [P, 1])
        parts, rsum = g.sb(ctx, "d_parts", [P, CHUNKS + 1]), g.sb(ctx, "d_rsum", [P, 1])
        on, o_t = g.sb(ctx, "d_on", [P, P]), g.sb(ctx, "d_o_t", [P, PAIRS, LSEQ])
        ktp = [g.ps(ctx, f"d_ktp{s}", [P, PAIRS, P]) for s in range(3)]
        stp = [g.ps(ctx, f"d_stp{s}", [P, QUAD * P]) for s in range(2)]
        ptp = g.ps(ctx, "d_ptp", [P, QUAD, P])
        ov = g.ps(ctx, "d_ov", [P, P])
        misc = g.ps(ctx, "d_misc", [P, 512])
        stn, ot = misc[:, 0:TS], misc[:, P:2 * P]
        k_in_ok = [g.sem(f"d_k_in_ok{s}") for s in range(CHUNK)]
        v_in_ok = [g.sem(f"d_v_in_ok{s}") for s in range(CHUNK)]
        k_turned = g.sem("d_k_turned")
        kt_ok = g.sem("d_kt_ok")
        scored = g.sem("d_scored")
        added = g.sem("d_added")
        topped = g.sem("d_topped")
        new_scored, new_st, max_ok = g.sem("d_new_scored"), g.sem("d_new_st"), g.sem("d_max_ok")
        exped = g.sem("d_exped")
        pturned = g.sem("d_pturned")
        pt_ok = g.sem("d_pt_ok")
        valued = g.sem("d_valued")
        q_ok = g.sem("d_q_ok")
        biased = [g.sem(f"d_biased{s}") for s in range(2)]
        on_ok, ot_ok, out_ok, steps = g.sem("d_on_ok"), g.sem("d_ot_ok"), g.sem("d_out_ok"), g.sem("d_steps2")
        zeroed = g.sem("d_zeroed")

        def back(i):
            return 3 if i % NPG >= 2 else 2

        with nc.Block() as block:
            @block.sync
            def _(sp):
                sp.sem_inc(k_turned, CHUNK)
                sp.sem_inc(kt_ok, 3)
                sp.sem_inc(scored, 12)
                sp.sem_inc(added, 2)
                sp.sem_inc(pturned, 2 * Q_V)
                sp.sem_inc(pt_ok, 1)
                sp.sem_inc(valued, 40)
                sp.sem_inc(on_ok, 1)
                sp.sem_inc(out_ok, 1)
                cache = io["cache_fox_k"]
                with sp.Fori(0, NSEQ * CHUNKS) as c:
                    _, pages = nc.values_load_multi_w_load_instructions(
                        g.pages[0:1, ds(c * CHUNK, CHUNK)], engines=(mybir.EngineType.SP,), min_val=0,
                        max_val=cache.shape[0] - 1)
                    for s in range(CHUNK):
                        src = cache[pages[s]].rearrange("t h d -> t (h d)")
                        sp.wait_ge(k_turned, c * CHUNK + (s + 1))
                        sp.dma_start(k_in[s][:], src).then_inc(k_in_ok[s], 16)

            @block.gpsimd
            def _(pool):
                cache = io["cache_fox_v"]
                def start(b, e):
                    dst = st[e][:, 0:PAST].rearrange("p (g t) -> p g t", t=PAGE)
                    src_q = qz[:, b] if isinstance(b, int) else qz[:, ds(b, 1)].rearrange("p o a q -> p (o a) q")
                    pool.wait_ge(pturned, b * Q_V + Q_V)
                    pool.sem_inc(g.w.passed, 1)
                    nc.gpsimd.tensor_copy(q_now[e][:], src_q).then_inc(q_ok, 1)
                    for h in range(H_F):
                        row = ROWS * (h // 2) + LSEQ * (h % 2)
                        src = bias_past[ds(b * 2, 2), :, h].rearrange("x g t -> (x g) t").unsqueeze(0)\
                            .broadcast_to([LSEQ, NPG, PAGE])
                        pool.dma_start(dst[row:row + LSEQ], src).then_inc(biased[e], 16)

                def values(b):
                    for r in range(CHUNKS):
                        _, pages = nc.values_load_multi_w_load_instructions(
                            g.pages[0:1, ds(b * NPG + r * CHUNK, CHUNK)], engines=(mybir.EngineType.Pool,), min_val=0,
                            max_val=cache.shape[0] - 1)
                        for s in range(CHUNK):
                            src = cache[pages[s]].rearrange("t h d -> t (h d)")
                            at = 4 * s + 12 if r == 0 else 44 + PAIRS * ((r - 1) * CHUNK + s + 1)
                            pool.wait_ge(valued, b * USED + at)
                            pool.dma_start(v_in[s][:], src).then_inc(v_in_ok[s], 16)

                for s in range(2):
                    nc.gpsimd.memset(st[s][:], 0.0).then_inc(zeroed, 1)
                pool.wait_ge(zeroed, 2)
                start(0, 0)
                with pool.Fori(0, NSEQ // 2 - 1) as j:
                    for e in range(2):
                        start(j * 2 + e + 1, 1 - e)
                        values(j * 2 + e)
                start(NSEQ - 1, 1)
                values(NSEQ - 2)
                values(NSEQ - 1)

            @block.tensor
            def _(pe):
                def turn(b, i):
                    s, c = i % CHUNK, i // CHUNK
                    pe.wait_ge(k_in_ok[s], b * (16 * CHUNKS) + 16 * (c + 1))
                    pe.wait_ge(kt_ok, b * NPG + (i + 4 - back(i)))
                    for p in range(PAIRS):
                        mm = nc.tensor.transpose(ktp[i % 3][:, p, :], k_in[s][:, p * P:(p + 1) * P], g.ident[:])
                    mm.then_inc(k_turned, 1)

                def keys(b, e, m):
                    if m == 0:
                        turn(b, 0)
                        turn(b, 1)
                    for i in range(m * QUAD, (m + 1) * QUAD):
                        if i + 2 < NPG:
                            turn(b, i + 2)
                        if i % QUAD == 0:
                            pe.wait_ge(added, b * QUADS + (m + 1))
                        pe.wait_ge(kt_ok, b * NPG + (i + 4))
                        for p in range(PAIRS):
                            nc.tensor.matmul(stp[m % 2][p * ROWS:(p + 1) * ROWS, i % QUAD * P:(i % QUAD + 1) * P],
                                             q_now[e][:, p, :], kt[i % 3][:, p, :], start=True, stop=True)\
                                .then_inc(scored, 1)

                def new_keys(b, e):
                    for p in range(PAIRS):
                        nc.tensor.matmul(stn[p * ROWS:(p + 1) * ROWS, :], q_now[e][:, p, :], g.k_s[:, p, :],
                                         start=True, stop=True).then_inc(new_scored, 1)

                def turn_probs(b, e, v):
                    first_page = (v - 1) * QUAD if v else NPG
                    pe.wait_ge(exped, b * (CHUNKS + 1) + (first_page // CHUNK + 2 if v else 1))
                    pe.wait_ge(pt_ok, b * Q_V + (v + 1))
                    for k in range(QUAD if v else 1):
                        at = (first_page + k) * P
                        mm = nc.tensor.transpose(ptp[:, k, :], st[e][:, at:at + P], g.ident[:])
                    mm.then_inc(pturned, 1)

                def products(b, v):
                    pe.wait_ge(pt_ok, b * Q_V + (v + 2))
                    for k in range(QUAD if v else 1):
                        i = (v - 1) * QUAD + k
                        if v:
                            pe.wait_ge(v_in_ok[i % CHUNK], b * (16 * CHUNKS) + 16 * (i // CHUNK + 1))
                        values = v_in[i % CHUNK] if v else g.v_s
                        for p in range(PAIRS):
                            nc.tensor.matmul(ov[p * ROWS:(p + 1) * ROWS, :], pt[:, k, p * ROWS:(p + 1) * ROWS],
                                             values[:, p * P:(p + 1) * P], start=(v == 0), stop=(i == NPG - 1),
                                             skip_group_check=True).then_inc(valued, 1)

                def first():
                    pe.wait_ge(q_ok, 1)
                    for m in range(QUADS):
                        keys(0, 0, m)
                    new_keys(0, 0)

                def body(b, e, half, more):
                    if more:
                        pe.wait_ge(q_ok, b + 2)
                    turn_probs(b, e, 0)
                    pe.wait_ge(on_ok, b + 1)
                    for m in range(QUADS):
                        if more:
                            keys(b + 1, 1 - e, m)
                        products(b, m)
                        turn_probs(b, e, m + 1)
                    if more:
                        pe.wait_ge(out_ok, b + 1)
                        new_keys(b + 1, 1 - e)
                    products(b, QUADS)
                    pe.wait_ge(on_ok, b + 2)
                    nc.tensor.transpose(ot, on[:], g.ident[:]).then_inc(ot_ok, 1)
                sweep(pe, first, body)

            @block.scalar
            def _(act):
                act.preload_act_table(ACT.Exp)

                def keys(b, m):
                    for i in range(m * QUAD, (m + 1) * QUAD):
                        act.wait_ge(k_turned, b * NPG + (i + 1 + CHUNK))
                        act.wait_ge(scored, b * (4 * NPG) + (4 * (i + 1 - back(i)) + 12))
                        nc.scalar.copy(kt[i % 3], ktp[i % 3]).then_inc(kt_ok, 1)

                def probs(b, e, piece):
                    c0 = (piece - 1) * CHUNK * P if piece else PAST
                    c1 = c0 + CHUNK * P if piece else NEW
                    nc.scalar.activation(st[e][:, c0:c1], st[e][:, c0:c1], ACT.Exp, bias=nmax[:],
                                         accum_out=parts[:, piece:piece + 1]).then_inc(exped, 1)

                def body(b, e, half, more):
                    act.wait_ge(max_ok, b + 1)
                    act.wait_ge(on_ok, b + 1)
                    probs(b, e, 0)
                    probs(b, e, 1)
                    for m in range(QUADS):
                        if more:
                            keys(b + 1, m)
                        if m + 2 <= CHUNKS:
                            probs(b, e, m + 2)

                def first():
                    for m in range(QUADS):
                        keys(0, m)
                sweep(act, first, body)

            @block.vector
            def _(dve):
                STEPS = 1

                def keys(b, e, half, m):
                    cols = st[e][:, m * QUAD * P:(m + 1) * QUAD * P]
                    if m == 0:
                        dve.wait_ge(biased[e], half * (16 * H_F) + 16 * H_F)
                    dve.wait_ge(scored, b * (4 * NPG) + ((m + 1) * 16 + 12))
                    nc.vector.tensor_tensor(cols, cols, stp[m % 2][:], ALU.add).then_inc(added, 1)
                    dve.wait_ge(added, b * QUADS + (m + 3))
                    nc.vector.tensor_reduce(tops[:, m:m + 1], cols, AX.X, ALU.max).then_inc(topped, 1)

                def maximum(b, e):
                    bn = bias_n[:, b] if isinstance(b, int) else bias_n[:, ds(b, 1)].rearrange("p o k -> p (o k)")
                    dve.wait_ge(new_scored, b * PAIRS + PAIRS)
                    nc.vector.tensor_tensor(st[e][:, PAST:NEW], stn, bn, ALU.add).then_inc(new_st, 1)
                    dve.wait_ge(new_st, b + 1)
                    nc.vector.tensor_reduce(tops[:, QUADS:QUADS + 1], st[e][:, PAST:NEW], AX.X, ALU.max)\
                        .then_inc(topped, 1)
                    dve.wait_ge(topped, b * (QUADS + 1) + (QUADS + 1))
                    nc.vector.tensor_reduce(nmax[:], tops[:], AX.X, ALU.max, negate=True).then_inc(max_ok, 1)
                    dve.wait_ge(max_ok, b + 1)

                def probs(b, v):
                    n = QUAD if v else 1
                    dve.wait_ge(pturned, b * Q_V + (v + 1 + 2 * Q_V))
                    dve.wait_ge(valued, b * USED + (44 + PAIRS * QUAD * (v - 1) if v else 40))
                    nc.vector.tensor_copy(pt[:, 0:n], ptp[:, 0:n]).then_inc(pt_ok, 1)

                def first():
                    for m in range(QUADS):
                        keys(0, 0, 0, m)
                    maximum(0, 0)

                def body(b, e, half, more):
                    for m in range(QUADS):
                        probs(b, m)
                        if more:
                            keys(b + 1, 1 - e, half + e, m)
                    probs(b, QUADS)
                    dve.wait_ge(exped, b * (CHUNKS + 1) + (CHUNKS + 1))
                    if more:
                        maximum(b + 1, 1 - e)
                    dst = g.br[:, 8:12, ds(b * LSEQ + TP, LSEQ)]
                    chain = Chain(steps, b * 3)
                    chain.mark(nc.vector.tensor_reduce(rsum[:], parts[:], AX.X, ALU.add))
                    chain.wait(dve)
                    chain.mark(nc.vector.reciprocal(rsum[:], rsum[:]))
                    chain.wait(dve)
                    dve.wait_ge(valued, b * USED + (USED + 40))
                    nc.vector.tensor_scalar(on[:], ov[:], rsum[:], None, ALU.mult).then_inc(on_ok, 1)
                    dve.wait_ge(ot_ok, b + 1)
                    for s in range(2):
                        src = ot[HALVES[s], :].rearrange("p (a s q) -> p a s q", s=4, q=LSEQ)[:, :, s, :]
                        ins = nc.vector.tensor_copy(o_t[HALVES[s]], src)
                    chain.mark(ins)
                    chain.wait(dve)
                    nc.vector.tensor_copy(dst, o_t[:]).then_inc(out_ok, 1)
                    dve.wait_ge(out_ok, b + 2)
                sweep(dve, first, body)


def phase_mix(g, mix):
    nc, io, w = g.nc, g.io, g.w
    KB = 4
    outs = ("w_ret_o", "w_fox_o", "w_mem_o")
    tiles = (0, 8, 4)
    with ExitStack() as ctx:
        w.open(ctx, "mix")
        raw = [g.sb(ctx, f"mo_raw{i}", [P, KB, P]) for i in range(3)]
        gate = [g.sb(ctx, f"mo_gate{i}", [P, TW]) for i in range(2)]
        part = g.sb(ctx, "mo_part", [P, TW])
        acc = [g.ps(ctx, f"mo_acc{s}", [P, NB, 512]) for s in range(2)]
        raw_ok = [g.sem(f"mo_raw_ok{i}") for i in range(3)]
        branch, gated, mixed, steps = g.sem("mo_branch"), g.sem("mo_gated"), g.sem("mo_mixed"), g.sem("mo_steps")
        b0, b1 = w.n
        with nc.Block() as block:
            @block.sync
            def _(sp):
                sp.sem_inc(gated, 1)
                sp.sem_inc(mixed, 1)
                sp.sem_inc(branch, 3)
                with sp.Fori(0, KD // 2) as jj:
                    for u in range(6):
                        x, i = divmod(u, 3)
                        s = u % 2
                        w_src = io["w_in"][:, ds(jj * (2 * P) + (C_GATE + i * D + x * P), P)]
                        o_src = io[outs[i]][:, ds(jj * (2 * P) + x * P, P)].rearrange("(k p) c -> p k c", p=P)
                        w.load(sp, s, jj * 3 + (u // 2 + (b0, b1)[s]), w_src, KD)
                        sp.wait_ge(branch, jj * 6 + (u + 1))
                        sp.sem_inc(g.w.passed, 1)
                        sp.dma_start(raw[i][:], o_src).then_inc(raw_ok[i], 16)

            @block.gpsimd
            def _(pool):
                with pool.Fori(0, KD // 2) as jj:
                    for u in range(6):
                        s = u % 2
                        w.split(pool, s, jj * 3 + (u // 2 + (b0, b1)[s]), KD)

            @block.tensor
            def _(pe):
                with pe.Fori(0, KD // 2) as jj:
                    for u in range(6):
                        x, i = divmod(u, 3)
                        s = u % 2
                        pe.wait_ge(gated, jj * 6 + (u + 1))
                        w.products(pe, s, jj * 3 + (u // 2 + (b0, b1)[s]), KD, acc[0], g.xh, g.xl)
                        pe.wait_ge(raw_ok[i], jj * 32 + (x * 16 + 16))
                        pe.wait_ge(mixed, jj * 6 + (u + 1))
                        for k in range(KB):
                            for b in range(NB):
                                mm = nc.tensor.matmul(acc[1][:, b, 0:TB], raw[i][:, k, :],
                                                      g.br[:, tiles[i] + k, b * TB:(b + 1) * TB],
                                                      start=(k == 0), stop=(k == KB - 1))
                        mm.then_inc(branch, 1)

            @block.scalar
            def _(act):
                act.preload_act_table(ACT.Sigmoid)
                with act.Fori(0, KD // 2) as jj:
                    for u in range(6):
                        x, i = divmod(u, 3)
                        s = u % 2
                        bias = g.b_gate[:, i, ds(jj * 2 + x, 1)]
                        act.wait_ge(w.done[s], jj * 3 + (u // 2 + 2 + (b0, b1)[s]))
                        if u >= 2:
                            act.wait_ge(mixed, jj * 6 + u)
                        else:
                            act.wait_ge(mixed, jj * 6 + 1)
                        nc.scalar.activation(blocks_of(gate[s][:]), acc[0][:, :, 0:TB], ACT.Sigmoid, bias=bias)\
                            .then_inc(gated, 1)

            @block.vector
            def _(dve):
                with dve.Fori(0, KD // 2) as jj:
                    for u in range(6):
                        x, i = divmod(u, 3)
                        s = u % 2
                        row = mix[:, jj * 2 + x, :]
                        out = row if i == 0 else part[:]
                        dve.wait_ge(gated, jj * 6 + (u + 2))
                        dve.wait_ge(branch, jj * 6 + (u + 4))
                        nc.vector.tensor_tensor(blocks_of(out), blocks_of(gate[s][:]), acc[1][:, :, 0:TB], ALU.mult)\
                            .then_inc(mixed, 1)
                        dve.wait_ge(mixed, jj * 6 + (u + 2))
                        if i:
                            nc.vector.tensor_tensor(row, row, part[:], ALU.add).then_inc(steps, 1)
                            dve.wait_ge(steps, jj * 4 + (x * 2 + i))
        w.n = [b0 + 3 * KD // 2, b1 + 3 * KD // 2]


def phase_out(g, mix):
    nc, io, w = g.nc, g.io, g.w
    with ExitStack() as ctx:
        w.open(ctx, "out")
        acc = [g.ps(ctx, f"o_acc{s}", [P, NB, 512]) for s in range(2)]
        free = [g.sem(f"o_free{s}") for s in range(2)]
        summed, high, low = g.sem("o_summed"), g.sem("o_high"), g.sem("o_low")
        b0, b1 = w.n
        with nc.Block() as block:
            @block.sync
            def _(sp):
                for s in range(2):
                    sp.sem_inc(free[s], 1)
                with sp.Fori(0, KD // 2) as j:
                    for s in range(2):
                        w.load(sp, s, j + (b0, b1)[s], io["w_out"][:, ds((j * 2 + s) * P, P)], KD)

            @block.gpsimd
            def _(pool):
                with pool.Fori(0, KD // 2) as j:
                    for s in range(2):
                        w.split(pool, s, j + (b0, b1)[s], KD)

            @block.tensor
            def _(pe):
                with pe.Fori(0, KD // 2) as j:
                    for s in range(2):
                        pe.wait_ge(free[s], j + 1)
                        w.products(pe, s, j + (b0, b1)[s], KD, acc[s], g.xh, g.xl, ready=(low, 1))

            @block.scalar
            def _(act):
                for k in range(KD):
                    act.wait_ge(summed, k + 1)
                    nc.scalar.copy(g.xh[:, k, :], mix[:, k, :]).then_inc(high, 1)

            @block.vector
            def _(dve):
                for k in range(KD + 1):
                    if k < KD:
                        nc.vector.tensor_tensor(g.res[:, k, :], g.xh[:, k, :].bitcast(F32), g.xl[:, k, :].bitcast(F32),
                                                ALU.add).then_inc(summed, 1)
                    if k > 0:
                        dve.wait_ge(high, k)
                        nc.vector.tensor_tensor(g.xl[:, k - 1, :], mix[:, k - 1, :], g.xh[:, k - 1, :].bitcast(F32),
                                                ALU.subtract).then_inc(low, 1)
                with dve.Fori(0, KD // 2) as j:
                    for s in range(2):
                        row = g.res[:, j * 2 + s, :]
                        dve.wait_ge(w.done[s], j + ((b0, b1)[s] + 2))
                        nc.vector.scalar_tensor_tensor(blocks_of(row), blocks_of(row), ALPHA, acc[s][:, :, 0:TB],
                                                       ALU.mult, ALU.add).then_inc(free[s], 1)
        w.n = [b0 + KD // 2, b1 + KD // 2]


def phase_store(g):
    nc, io = g.nc, g.io
    H = KD // 2
    with ExitStack() as ctx:
        y = [g.sb(ctx, f"y_out{s}", [P, KD, P]) for s in range(2)]
        yt = [[g.ps(ctx, f"y_t{s}_{x}", [P, H, P]) for x in range(2)] for s in range(2)]
        turned = g.sem("y_turned")
        read = [g.sem(f"y_read{x}") for x in range(2)]
        stored = [g.sem(f"y_stored{s}") for s in range(2)]
        with nc.Block() as block:
            @block.tensor
            def _(pe):
                for c in range(NCH + 1):
                    n = P if c < NCH else TS
                    for x in range(2):
                        pe.wait_ge(read[x], c + 1)
                        for k in range(H):
                            mm = nc.tensor.transpose(yt[c % 2][x][0:n, k, :], g.res[:, x * H + k, c * P:c * P + n], g.ident[:])
                    mm.then_inc(turned, 1)

            def halves(engine, x, copy):
                def chunk(c, half, s, n):
                    engine.wait_ge(turned, c + 1)
                    engine.wait_ge(stored[s], half * 16 + 16)
                    copy(y[s][0:n, x * H:(x + 1) * H, :], yt[s][x][0:n]).then_inc(read[x], 1)
                with engine.Fori(0, NCH // 2) as i:
                    for s in range(2):
                        chunk(i * 2 + s, i, s, P)
                chunk(NCH, NCH // 2, 0, TS)

            @block.scalar
            def _(act):
                halves(act, 0, nc.scalar.copy)

            @block.vector
            def _(dve):
                halves(dve, 1, nc.vector.tensor_copy)

            @block.sync
            def _(sp):
                for s in range(2):
                    sp.sem_inc(read[s], 2)
                    sp.sem_inc(stored[s], 16)
                with sp.Fori(0, NCH // 2) as i:
                    for s in range(2):
                        dst = io["y_prompt"][0, ds(i * (2 * P) + s * P, P), :]
                        for x in range(2):
                            sp.wait_ge(read[x], i * 2 + (s + 3))
                        sp.dma_start(dst, y[s][:].rearrange("p a b -> p (a b)")).then_inc(stored[s], 16)
                for x in range(2):
                    sp.wait_ge(read[x], NCH + 3)
                sp.dma_start(io["y_sample"].rearrange("b t d -> (b t) d"), y[0][0:TS].rearrange("p a b -> p (a b)"))\
                    .then_inc(stored[0], 16)
                for s in range(2):
                    sp.wait_ge(stored[s], 16 * (NCH // 2 + 2 - s))


def build_step(nc, io, until=None):
    with ExitStack() as ctx:
        g = Build(nc, ctx, io)
        g.w = Weights(nc, ctx)
        g.xh, g.xl = (g.sb(ctx, n, [P, KD, TW], F32R) for n in ("x_hi", "x_lo"))
        g.ident, g.ones, g.causal = (g.sb(ctx, n, [P, P]) for n in ("ident_sb", "ones_sb", "causal_sb"))
        g.ln_g, g.ln_b = g.sb(ctx, "ln_g_sb", [P, 3, KD]), g.sb(ctx, "ln_b_sb", [P, 3, KD])
        g.b_gate, g.gn_g = g.sb(ctx, "b_gate_sb", [P, 3, KD]), g.sb(ctx, "gn_g_sb", [P, H_R])
        g.b_forget, g.pages = g.sb(ctx, "b_forget_sb", [H_F, 1]), g.sb(ctx, "pages_sb", [1, NSEQ * NPG], I32)
        g.mem_kt, g.mem_v = g.sb(ctx, "mem_kt", [P, H_M, N_MEM]), g.sb(ctx, "mem_v", [P, N_MEM // P, H_M * DM])
        with ExitStack() as first:
            g.res = g.sb(first, "res0", [P, KD, TW])
            phase_load(g)
            g.end_phase()
            phase_memory(g)
            g.end_phase()
            phase_ffn(g, 0)
            g.end_phase()
            phase_norm(g, 0, keep="parts")
            g.end_phase()
        if until == "norm0":
            return g
        with ExitStack() as middle:
            g.br = g.sb(middle, "br", [P, 12, TW])
            phase_retention_in(g)
            g.end_phase()
            phase_retention(g)
            g.end_phase()
            phase_head_norm(g)
            g.end_phase()
            with ExitStack() as fox:
                g.k_s, g.v_s = g.sb(fox, "k_s", [P, PAIRS, TS]), g.sb(fox, "v_s", [P, H_F * DF])
                g.lfn = g.sb(fox, "lfn", [P, NCH + 1, H_F])
                with ExitStack() as sums:
                    g.fkv = g.sb(sums, "fkv", [P, 8, TW])
                    g.negc = g.sb(sums, "negc", [H_F, TW])
                    phase_attention_in(g)
                    g.end_phase()
                    phase_kv_natural(g)
                    g.end_phase()
                    phase_cross_prompt(g)
                    g.end_phase()
                    phase_cross_sample(g)
                    g.end_phase()
                    phase_fox_prompt(g)
                    g.end_phase()
                with ExitStack() as sample:
                    qz = g.sb(sample, "d_qz", [P, NSEQ, PAIRS, ROWS])
                    bias_n = g.sb(sample, "d_bias_n", [P, NSEQ, TS])
                    bias_past = nc.dram_tensor("bias_past", [2 * NSEQ, NPG // 2, H_F, PAGE], F32, kind="Internal").ap()
                    phase_sample_bias(g, qz, bias_n, bias_past)
                    g.end_phase()
                    phase_fox_sample(g, qz, bias_n, bias_past)
                    g.end_phase()
            with ExitStack() as mixed:
                mix = g.sb(mixed, "mix", [P, KD, TW])
                phase_mix(g, mix)
                g.end_phase()
                g.res = g.br[:, 0:KD, :]
                phase_out(g, mix)
                g.end_phase()
            phase_norm(g, 1, keep="both")
            g.end_phase()
            phase_ffn(g, 1)
            g.end_phase()
            phase_norm(g, 2, keep="result")
            g.end_phase()
            phase_store(g)
            g.end_phase()
    return g


_INS = ["x_prompt", "x_sample", "mem_prompt", "cache_fox_k", "cache_fox_v", "cache_fox_logf", "state_ret",
        "cache_mem_k", "cache_mem_v", "page_table", "ln_g", "ln_b", "w_ffn_gate", "w_ffn_up", "w_ffn_down",
        "w_in", "b_forget", "b_gate", "ret_gn_g", "w_ret_o", "w_fox_o", "w_mem_k", "w_mem_v", "w_mem_o", "w_out"]
_OUTS = [("y_prompt", (1, TP, D)), ("y_sample", (NSEQ, LSEQ, D)),
         ("fox_k_prompt", (1, TP, H_F, DF)), ("fox_v_prompt", (1, TP, H_F, DF)), ("fox_logf_prompt", (1, TP, H_F)),
         ("ret_state_prompt", (1, H_R, DK, DM)), ("mem_k_prompt", (1, N_MEM, H_M, DM)),
         ("mem_v_prompt", (1, N_MEM, H_M, DM)), ("fox_k_sample", (NSEQ, LSEQ, H_F, DF)),
         ("fox_v_sample", (NSEQ, LSEQ, H_F, DF)), ("fox_logf_sample", (NSEQ, LSEQ, H_F)),
         ("ret_state_sample", (NSEQ, H_R, DK, DM))]


def kernel(**inputs):
    import numpy as np
    from concourse import bacc
    from concourse.bass_utils import run_bass_kernel_spmd

    nc = bacc.Bacc("TRN2", target_bir_lowering=False, num_devices=1)
    arrays = {n: np.ascontiguousarray(inputs[n]) for n in _INS}
    arrays.update(shape_tables())
    io = {n: nc.dram_tensor(n, a.shape, mybir.dt.from_np(a.dtype), kind="ExternalInput").ap()
          for n, a in arrays.items()}
    for n, shape in _OUTS:
        io[n] = nc.dram_tensor(n, shape, F32, kind="ExternalOutput").ap()
    build_step(nc, io)
    r = run_bass_kernel_spmd(nc, [arrays], core_ids=[0])
    return tuple(r.results[0][n] for n, _ in _OUTS)
```
